# Optimizing a Trainium2 kernel written in Bass

```python
import math
import jax, jax.numpy as jnp
from jax import lax
import numpy as np

D_MODEL = 2048
BATCH = 1
SEQ = 512
DEPTH = 1
DEC_BATCH = 8
DEC_SEQ = 8
PAST_LEN = 512
PAGE_SIZE = 128

HEAD_DIM = 64
ATTN_WIDTH = D_MODEL // 2
N_HEADS = ATTN_WIDTH // HEAD_DIM
KV_HEADS = 4
Q_PER_KV = N_HEADS // KV_HEADS
CMP_STRIDE = 16
CMP_BLOCK = 2 * CMP_STRIDE
CMP_HIDDEN = 2 * HEAD_DIM
SEL_BLOCK = 64
N_SELECT = 8
WINDOW = 512
QUERY_BLOCK = 128
N_KV_SLOTS = 6
N_CACHE_SLOTS = 4
SSM_INNER = D_MODEL - ATTN_WIDTH
SSM_HEADDIM = 64
SSM_HEADS = SSM_INNER // SSM_HEADDIM
SSM_GROUPS = 4
SSM_HPG = SSM_HEADS // SSM_GROUPS
SSM_STATE = 128
SSM_CONV = 4
SSD_CHUNK = 128
CONV_DIM = SSM_INNER + 2 * SSM_GROUPS * SSM_STATE
MIX_WIDTH = ATTN_WIDTH + SSM_INNER
IN_WIDTH = ATTN_WIDTH + N_KV_SLOTS * KV_HEADS * HEAD_DIM + 3 * N_HEADS + SSM_INNER + CONV_DIM + SSM_HEADS
D_FF = ((8 * D_MODEL // 3 + 127) // 128) * 128
FFN_CONV = 3
REL_BUCKETS = 32
REL_MAX_DIST = 128
EPS = 1e-6
NEG = -1e30
TINY = 1e-30
FORCE_BONUS = 1e4
SCALE = HEAD_DIM ** -0.5

kernel_name = 'hybrid_nsa_ssd_convffn_step'

def rmsnorm(x, g):
    xf = x.astype(jnp.float32)
    y = xf * lax.rsqrt(jnp.mean(xf * xf, -1, keepdims=True) + EPS)
    return (y * g.astype(jnp.float32)).astype(x.dtype)

def masked_softmax(s, mask):
    m = jnp.max(jnp.where(mask, s, NEG), -1, keepdims=True)
    e = jnp.where(mask, jnp.exp(jnp.where(mask, s, m) - m), 0.0)
    return e / jnp.maximum(jnp.sum(e, -1, keepdims=True), TINY)

def rel_bucket(dist):
    n = jnp.maximum(dist, 0)
    max_exact = REL_BUCKETS // 2
    nf = jnp.maximum(n, 1).astype(jnp.float32)
    large = max_exact + (jnp.log(nf / max_exact) / math.log(REL_MAX_DIST / max_exact)
                         * (REL_BUCKETS - max_exact)).astype(jnp.int32)
    large = jnp.minimum(large, REL_BUCKETS - 1)
    return jnp.where(n < max_exact, n, large)

def causal_dwconv(x_full, w, b):
    width = w.shape[0]
    t = x_full.shape[1] - width + 1
    acc = b
    for k in range(width):
        acc = acc + x_full[:, k:k + t] * w[k]
    return acc

def project(x, g_pre, w_in):
    b, t = x.shape[:2]
    p = rmsnorm(x, g_pre) @ w_in
    o1 = ATTN_WIDTH
    o2 = o1 + N_KV_SLOTS * KV_HEADS * HEAD_DIM
    o3 = o2 + 3 * N_HEADS
    o4 = o3 + SSM_INNER
    o5 = o4 + CONV_DIM
    q, kv, gate, z, xbc, dt = jnp.split(p, [o1, o2, o3, o4, o5], axis=-1)
    q = q.reshape(b, t, KV_HEADS, Q_PER_KV, HEAD_DIM)
    kv = kv.reshape(b, t, N_KV_SLOTS, KV_HEADS, HEAD_DIM)
    gate = jax.nn.sigmoid(gate.astype(jnp.float32)).reshape(b, t, 3, KV_HEADS, Q_PER_KV)
    return q, kv, gate, z, xbc, dt

def compress(rows, pe, w1, b1, w2, b2, n_blk):
    b, _, g, d = rows.shape
    ch = rows[:, :(n_blk + 1) * CMP_STRIDE].reshape(b, n_blk + 1, CMP_STRIDE, g, d)
    pe2 = pe.reshape(2, CMP_STRIDE, 1, d)
    w12 = w1.reshape(2, CMP_STRIDE, d, CMP_HIDDEN)
    hid = (jnp.einsum('bnsgd,sdh->bngh', ch[:, :-1] + pe2[0], w12[0])
           + jnp.einsum('bnsgd,sdh->bngh', ch[:, 1:] + pe2[1], w12[1]) + b1)
    return jnp.einsum('bngh,hd->bngd', jax.nn.gelu(hid), w2) + b2

def overlap_map(n_cmp, n_sel):
    c0 = jnp.arange(n_cmp) * CMP_STRIDE
    s0 = jnp.arange(n_sel) * SEL_BLOCK
    ov = jnp.minimum(c0[:, None] + CMP_BLOCK, s0[None, :] + SEL_BLOCK) - jnp.maximum(c0[:, None], s0[None, :])
    return jnp.clip(ov, 0).astype(jnp.float32) / CMP_BLOCK

def gather_blocks(rows, idx):
    b, t, g, d = rows.shape
    kb = rows.reshape(b, t // SEL_BLOCK, SEL_BLOCK, g, d).transpose(0, 3, 1, 2, 4)
    bi = jnp.arange(b)[:, None, None, None]
    gi = jnp.arange(g)[None, None, :, None]
    return kb[bi, gi, idx]

def pad_rows(rows, n):
    return jnp.pad(rows, ((0, 0), (0, n - rows.shape[1]), (0, 0), (0, 0)))

def nsa_block(q, gate, q_pos, kc, vc, c_end, imp_map, k_sel, v_sel, kw, vw, kw_pos, rel_table):
    b, tq, g, r, d = q.shape
    table = rel_table.astype(jnp.float32).reshape(REL_BUCKETS, g, r)
    dist_c = q_pos[:, None] - c_end[None, :]
    bias_c = table[rel_bucket(dist_c)].transpose(0, 2, 3, 1)[None]
    s_c = jnp.einsum('btgrd,bngd->btgrn', q, kc).astype(jnp.float32) * SCALE + bias_c
    p_c = masked_softmax(s_c, (dist_c >= 0)[None, :, None, None, :])
    o_c = jnp.einsum('btgrn,bngd->btgrd', p_c.astype(vc.dtype), vc).astype(jnp.float32)
    ns = imp_map.shape[1]
    imp = jnp.einsum('btgrn,ns->btgs', p_c, imp_map)
    blk = jnp.arange(ns)
    q_blk = q_pos // SEL_BLOCK
    valid = (blk[None, :] <= q_blk[:, None])[None, :, None, :]
    forced = ((blk[None, :] == 0) | (blk[None, :] == q_blk[:, None]) | (blk[None, :] == q_blk[:, None] - 1))
    score = jnp.where(valid, imp + jnp.where(forced, FORCE_BONUS, 0.0)[None, :, None, :], -jnp.inf)
    k_top = min(N_SELECT, ns)
    _, idx = lax.top_k(score, k_top)
    idx_valid = idx <= q_blk[None, :, None, None]
    ks = gather_blocks(k_sel, idx)
    vs = gather_blocks(v_sel, idx)
    kpos = idx[..., None] * SEL_BLOCK + jnp.arange(SEL_BLOCK)
    dist_s = q_pos[None, :, None, None, None] - kpos
    mask_s = (idx_valid[..., None] & (dist_s >= 0)).reshape(b, tq, g, 1, k_top * SEL_BLOCK)
    bias_s = jnp.moveaxis(table[rel_bucket(dist_s), jnp.arange(g)[None, None, :, None, None]], -1, 3)
    s_s = jnp.einsum('btgrd,btgksd->btgrks', q, ks).astype(jnp.float32) * SCALE + bias_s
    p_s = masked_softmax(s_s.reshape(b, tq, g, r, k_top * SEL_BLOCK), mask_s)
    o_s = jnp.einsum('btgrm,btgmd->btgrd', p_s.astype(vs.dtype),
                     vs.reshape(b, tq, g, k_top * SEL_BLOCK, d)).astype(jnp.float32)
    dist_w = q_pos[:, None] - kw_pos[None, :]
    mask_w = (dist_w >= 0) & (dist_w <= WINDOW) & (kw_pos[None, :] >= 0)
    bias_w = table[rel_bucket(dist_w)].transpose(0, 2, 3, 1)[None]
    s_w = jnp.einsum('btgrd,bkgd->btgrk', q, kw).astype(jnp.float32) * SCALE + bias_w
    p_w = masked_softmax(s_w, mask_w[None, :, None, None, :])
    o_w = jnp.einsum('btgrk,bkgd->btgrd', p_w.astype(vw.dtype), vw).astype(jnp.float32)
    o = (gate[:, :, 0, :, :, None] * o_c + gate[:, :, 1, :, :, None] * o_s
         + gate[:, :, 2, :, :, None] * o_w)
    return o.astype(q.dtype).reshape(b, tq, g * r * d)

def nsa_prompt(q, kv, gate, cmp_pe, cmp_w1, cmp_b1, cmp_w2, cmp_b2, rel_table):
    b, t = q.shape[:2]
    n_cmp = (t - CMP_BLOCK) // CMP_STRIDE + 1
    kc = compress(kv[:, :, 0], cmp_pe[0], cmp_w1[0], cmp_b1[0], cmp_w2[0], cmp_b2[0], n_cmp)
    vc = compress(kv[:, :, 1], cmp_pe[1], cmp_w1[1], cmp_b1[1], cmp_w2[1], cmp_b2[1], n_cmp)
    c_end = jnp.arange(n_cmp) * CMP_STRIDE + CMP_BLOCK - 1
    n_sel = -(-t // SEL_BLOCK)
    imp_map = overlap_map(n_cmp, n_sel)
    k_sel = pad_rows(kv[:, :, 2], n_sel * SEL_BLOCK)
    v_sel = pad_rows(kv[:, :, 3], n_sel * SEL_BLOCK)
    pad_w = ((0, 0), (WINDOW, 0), (0, 0), (0, 0))
    kw_pad = jnp.pad(kv[:, :, 4], pad_w)
    vw_pad = jnp.pad(kv[:, :, 5], pad_w)

    def one_block(i):
        s = i * QUERY_BLOCK
        qb = lax.dynamic_slice_in_dim(q, s, QUERY_BLOCK, 1)
        gb = lax.dynamic_slice_in_dim(gate, s, QUERY_BLOCK, 1)
        q_pos = s + jnp.arange(QUERY_BLOCK)
        kwb = lax.dynamic_slice_in_dim(kw_pad, s, WINDOW + QUERY_BLOCK, 1)
        vwb = lax.dynamic_slice_in_dim(vw_pad, s, WINDOW + QUERY_BLOCK, 1)
        kw_pos = s - WINDOW + jnp.arange(WINDOW + QUERY_BLOCK)
        return nsa_block(qb, gb, q_pos, kc, vc, c_end, imp_map, k_sel, v_sel, kwb, vwb, kw_pos, rel_table)

    out = lax.map(one_block, jnp.arange(t // QUERY_BLOCK))
    return jnp.moveaxis(out, 0, 1).reshape(b, t, ATTN_WIDTH)

def nsa_sample(q, kv, gate, cache_kv_l, win_l, page_table, cmp_pe, cmp_w1, cmp_b1, cmp_w2, cmp_b2, rel_table):
    b, tn = q.shape[:2]
    n_pages = page_table.shape[1]
    past_len = n_pages * PAGE_SIZE
    past = cache_kv_l[page_table].reshape(b, past_len, N_CACHE_SLOTS, KV_HEADS, HEAD_DIM)
    full = jnp.concatenate([past, kv[:, :, :N_CACHE_SLOTS].astype(past.dtype)], 1)
    t_all = past_len + tn
    n_cmp = (t_all - CMP_BLOCK) // CMP_STRIDE + 1
    kc = compress(full[:, :, 0], cmp_pe[0], cmp_w1[0], cmp_b1[0], cmp_w2[0], cmp_b2[0], n_cmp)
    vc = compress(full[:, :, 1], cmp_pe[1], cmp_w1[1], cmp_b1[1], cmp_w2[1], cmp_b2[1], n_cmp)
    c_end = jnp.arange(n_cmp) * CMP_STRIDE + CMP_BLOCK - 1
    n_sel = -(-t_all // SEL_BLOCK)
    imp_map = overlap_map(n_cmp, n_sel)
    k_sel = pad_rows(full[:, :, 2], n_sel * SEL_BLOCK)
    v_sel = pad_rows(full[:, :, 3], n_sel * SEL_BLOCK)
    win_len = win_l.shape[1]
    win_all = jnp.concatenate([win_l, kv[:, :, N_CACHE_SLOTS:].astype(win_l.dtype)], 1)
    kw_pos = past_len - win_len + jnp.arange(win_len + tn)
    q_pos = past_len + jnp.arange(tn)
    o = nsa_block(q, gate, q_pos, kc, vc, c_end, imp_map, k_sel, v_sel,
                  win_all[:, :, 0], win_all[:, :, 1], kw_pos, rel_table)
    return o, win_all[:, -win_len:]

def ssd_scan(x, a, bm, cm, h0):
    b, t = x.shape[:2]
    q = min(SSD_CHUNK, t)
    n_ch = -(-t // q)
    pad = n_ch * q - t

    def chunks(v):
        v = jnp.pad(v, [(0, 0), (0, pad)] + [(0, 0)] * (v.ndim - 2))
        return jnp.moveaxis(v.reshape((b, n_ch, q) + v.shape[2:]), 1, 0)

    causal = jnp.tril(jnp.ones((q, q), bool))[None, :, :, None, None]

    def step(h, inp):
        xc, ac, bc, cc = inp
        acum = jnp.cumsum(ac, axis=1)
        seg = acum[:, :, None] - acum[:, None]
        decay = jnp.where(causal, jnp.exp(jnp.where(causal, seg, 0.0)), 0.0)
        cb = jnp.einsum('bign,bjgn->bijg', cc, bc)
        y = jnp.einsum('bijg,bijgr,bjgrp->bigrp', cb, decay, xc)
        y = y + jnp.einsum('bign,bgrpn->bigrp', cc, h) * jnp.exp(acum)[..., None]
        to_end = jnp.exp(acum[:, -1:] - acum)
        h = (h * jnp.exp(acum[:, -1])[..., None, None]
             + jnp.einsum('bjgn,bjgrp->bgrpn', bc, xc * to_end[..., None]))
        return h, y

    h_t, ys = lax.scan(step, h0, (chunks(x), chunks(a), chunks(bm), chunks(cm)))
    y = jnp.moveaxis(ys, 0, 1).reshape((b, n_ch * q) + x.shape[2:])[:, :t]
    return y, h_t

def ssd_mixer(z, xbc, dt_raw, conv_hist, h0, conv_w, conv_b, dt_bias, a_log, d_skip, norm_g):
    b, t = z.shape[:2]
    f32 = jnp.float32
    xbc_full = jnp.concatenate([conv_hist.astype(xbc.dtype), xbc], 1)
    xbc_c = jax.nn.silu(causal_dwconv(xbc_full, conv_w, conv_b))
    xs, bm, cm = jnp.split(xbc_c, [SSM_INNER, SSM_INNER + SSM_GROUPS * SSM_STATE], axis=-1)
    xs = xs.astype(f32).reshape(b, t, SSM_GROUPS, SSM_HPG, SSM_HEADDIM)
    bm = bm.astype(f32).reshape(b, t, SSM_GROUPS, SSM_STATE)
    cm = cm.astype(f32).reshape(b, t, SSM_GROUPS, SSM_STATE)
    dt = jax.nn.softplus(dt_raw.astype(f32) + dt_bias.astype(f32)).reshape(b, t, SSM_GROUPS, SSM_HPG)
    a = -jnp.exp(a_log.astype(f32)).reshape(SSM_GROUPS, SSM_HPG)
    h0g = h0.astype(f32).reshape(b, SSM_GROUPS, SSM_HPG, SSM_HEADDIM, SSM_STATE)
    y, h_t = ssd_scan(xs * dt[..., None], dt * a, bm, cm, h0g)
    y = y + xs * d_skip.astype(f32).reshape(SSM_GROUPS, SSM_HPG, 1)
    y = y.reshape(b, t, SSM_INNER) * jax.nn.silu(z.astype(f32))
    yg = y.reshape(b, t, SSM_GROUPS, SSM_INNER // SSM_GROUPS)
    yg = yg * lax.rsqrt(jnp.mean(yg * yg, -1, keepdims=True) + EPS)
    y = yg.reshape(b, t, SSM_INNER) * norm_g.astype(f32)
    new_h = h_t.reshape(b, SSM_HEADS, SSM_HEADDIM, SSM_STATE).astype(h0.dtype)
    return y.astype(z.dtype), xbc_full[:, -(SSM_CONV - 1):], new_h

def block_tail(x, attn, ssm, ffn_hist, w_out, g_mix_post, g_ffn_pre, w_gate, w_up, dw_w, dw_b, w_down, g_ffn_post):
    mix = jnp.concatenate([attn, ssm], -1) @ w_out
    x = x + rmsnorm(mix, g_mix_post)
    h = rmsnorm(x, g_ffn_pre)
    gp = h @ w_gate
    full = jnp.concatenate([ffn_hist.astype(gp.dtype), gp], 1)
    act = jax.nn.gelu(causal_dwconv(full, dw_w, dw_b), approximate=True) * (h @ w_up)
    x = x + rmsnorm(act @ w_down, g_ffn_post)
    return x, full[:, -(FFN_CONV - 1):]

def setup_inputs(seed: int = 0) -> dict:
    key = jax.random.key(seed)
    ks = iter(jax.random.split(key, 48))
    f32 = jnp.float32

    def nrm(shape, scale):
        return jax.random.normal(next(ks), shape, f32) * scale

    def gain(shape):
        return 1.0 + nrm(shape, 0.05)

    n_pages = PAST_LEN // PAGE_SIZE
    n_pool = (DEC_BATCH * n_pages * 5) // 4
    win_len = min(WINDOW, PAST_LEN)
    page_table = jax.random.permutation(next(ks), n_pool)[:DEC_BATCH * n_pages]
    page_table = page_table.reshape(DEC_BATCH, n_pages).astype(jnp.int32)
    dt0 = jnp.exp(jax.random.uniform(next(ks), (DEPTH, SSM_HEADS), f32, math.log(1e-3), math.log(1e-1)))
    dt_bias = dt0 + jnp.log(-jnp.expm1(-dt0))
    a_log = jnp.log(jax.random.uniform(next(ks), (DEPTH, SSM_HEADS), f32, 1.0, 16.0))
    return {
        'x_prompt': nrm((BATCH, SEQ, D_MODEL), 1.0),
        'x_sample': nrm((DEC_BATCH, DEC_SEQ, D_MODEL), 1.0),
        'cache_kv': nrm((DEPTH, n_pool, PAGE_SIZE, N_CACHE_SLOTS, KV_HEADS, HEAD_DIM), 1.0),
        'cache_win_kv': nrm((DEPTH, DEC_BATCH, win_len, 2, KV_HEADS, HEAD_DIM), 1.0),
        'state_ssm_conv': nrm((DEPTH, DEC_BATCH, SSM_CONV - 1, CONV_DIM), 1.0),
        'state_ssm': nrm((DEPTH, DEC_BATCH, SSM_HEADS, SSM_HEADDIM, SSM_STATE), 0.5),
        'state_ffn_conv': nrm((DEPTH, DEC_BATCH, FFN_CONV - 1, D_FF), 1.0),
        'page_table': page_table,
        'rel_table': nrm((REL_BUCKETS, N_HEADS), 0.5),
        'ln_mix_pre': gain((DEPTH, D_MODEL)),
        'w_in': nrm((DEPTH, D_MODEL, IN_WIDTH), D_MODEL ** -0.5),
        'cmp_pe': nrm((DEPTH, 2, CMP_BLOCK, HEAD_DIM), 0.1),
        'cmp_w1': nrm((DEPTH, 2, CMP_BLOCK, HEAD_DIM, CMP_HIDDEN), (CMP_BLOCK * HEAD_DIM) ** -0.5),
        'cmp_b1': nrm((DEPTH, 2, CMP_HIDDEN), 0.01),
        'cmp_w2': nrm((DEPTH, 2, CMP_HIDDEN, HEAD_DIM), CMP_HIDDEN ** -0.5),
        'cmp_b2': nrm((DEPTH, 2, HEAD_DIM), 0.01),
        'ssm_conv_w': nrm((DEPTH, SSM_CONV, CONV_DIM), SSM_CONV ** -0.5),
        'ssm_conv_b': nrm((DEPTH, CONV_DIM), 0.01),
        'ssm_dt_bias': dt_bias,
        'ssm_a_log': a_log,
        'ssm_d': gain((DEPTH, SSM_HEADS)),
        'ssm_norm_g': gain((DEPTH, SSM_INNER)),
        'w_out': nrm((DEPTH, MIX_WIDTH, D_MODEL), MIX_WIDTH ** -0.5),
        'ln_mix_post': gain((DEPTH, D_MODEL)),
        'ln_ffn_pre': gain((DEPTH, D_MODEL)),
        'ffn_w_gate': nrm((DEPTH, D_MODEL, D_FF), D_MODEL ** -0.5),
        'ffn_w_up': nrm((DEPTH, D_MODEL, D_FF), D_MODEL ** -0.5),
        'ffn_dw_w': nrm((DEPTH, FFN_CONV, D_FF), FFN_CONV ** -0.5),
        'ffn_dw_b': nrm((DEPTH, D_FF), 0.01),
        'ffn_w_down': nrm((DEPTH, D_FF, D_MODEL), D_FF ** -0.5),
        'ln_ffn_post': gain((DEPTH, D_MODEL)),
    }

def reference(x_prompt, x_sample, cache_kv, cache_win_kv, state_ssm_conv, state_ssm, state_ffn_conv,
              page_table, rel_table, ln_mix_pre, w_in, cmp_pe, cmp_w1, cmp_b1, cmp_w2, cmp_b2,
              ssm_conv_w, ssm_conv_b, ssm_dt_bias, ssm_a_log, ssm_d, ssm_norm_g, w_out, ln_mix_post,
              ln_ffn_pre, ffn_w_gate, ffn_w_up, ffn_dw_w, ffn_dw_b, ffn_w_down, ln_ffn_post):
    xp, xd = x_prompt, x_sample
    bp, tp = xp.shape[:2]
    kv_p, kv_d, win_p, win_d = [], [], [], []
    sc_p, sc_d, ss_p, ss_d, fc_p, fc_d = [], [], [], [], [], []
    for l in range(DEPTH):
        q, kv, gate, z, xbc, dt = project(xp, ln_mix_pre[l], w_in[l])
        attn = nsa_prompt(q, kv, gate, cmp_pe[l], cmp_w1[l], cmp_b1[l], cmp_w2[l], cmp_b2[l], rel_table)
        ssm, conv_new, h_new = ssd_mixer(
            z, xbc, dt, jnp.zeros((bp, SSM_CONV - 1, CONV_DIM), xp.dtype),
            jnp.zeros((bp, SSM_HEADS, SSM_HEADDIM, SSM_STATE), xp.dtype),
            ssm_conv_w[l], ssm_conv_b[l], ssm_dt_bias[l], ssm_a_log[l], ssm_d[l], ssm_norm_g[l])
        xp, ffn_new = block_tail(xp, attn, ssm, jnp.zeros((bp, FFN_CONV - 1, D_FF), xp.dtype),
                                 w_out[l], ln_mix_post[l], ln_ffn_pre[l], ffn_w_gate[l], ffn_w_up[l],
                                 ffn_dw_w[l], ffn_dw_b[l], ffn_w_down[l], ln_ffn_post[l])
        kv_p.append(kv[:, :, :N_CACHE_SLOTS])
        win_p.append(kv[:, tp - min(WINDOW, tp):, N_CACHE_SLOTS:])
        sc_p.append(conv_new)
        ss_p.append(h_new)
        fc_p.append(ffn_new)
        q, kv, gate, z, xbc, dt = project(xd, ln_mix_pre[l], w_in[l])
        attn, win_new = nsa_sample(q, kv, gate, cache_kv[l], cache_win_kv[l], page_table,
                                   cmp_pe[l], cmp_w1[l], cmp_b1[l], cmp_w2[l], cmp_b2[l], rel_table)
        ssm, conv_new, h_new = ssd_mixer(
            z, xbc, dt, state_ssm_conv[l], state_ssm[l],
            ssm_conv_w[l], ssm_conv_b[l], ssm_dt_bias[l], ssm_a_log[l], ssm_d[l], ssm_norm_g[l])
        xd, ffn_new = block_tail(xd, attn, ssm, state_ffn_conv[l],
                                 w_out[l], ln_mix_post[l], ln_ffn_pre[l], ffn_w_gate[l], ffn_w_up[l],
                                 ffn_dw_w[l], ffn_dw_b[l], ffn_w_down[l], ln_ffn_post[l])
        kv_d.append(kv[:, :, :N_CACHE_SLOTS])
        win_d.append(win_new)
        sc_d.append(conv_new)
        ss_d.append(h_new)
        fc_d.append(ffn_new)
    new_kv_p = jnp.stack(kv_p)
    new_kv_d = jnp.stack(kv_d)
    new_win_p = jnp.stack(win_p)
    new_win_d = jnp.stack(win_d)
    new_conv_p = jnp.stack(sc_p)
    new_conv_d = jnp.stack(sc_d)
    new_ssm_p = jnp.stack(ss_p)
    new_ssm_d = jnp.stack(ss_d)
    new_ffn_p = jnp.stack(fc_p)
    new_ffn_d = jnp.stack(fc_d)
    return (xp, xd, new_kv_p, new_kv_d, new_win_p, new_win_d, new_conv_p, new_conv_d,
            new_ssm_p, new_ssm_d, new_ffn_p, new_ffn_d)


_drawn_inputs = setup_inputs


def setup_inputs(seed=0):
    import zlib

    import numpy as np

    out = dict(_drawn_inputs(seed))
    spreads = {}
    factors = {'cmp_b1': 23.043, 'cmp_b2': 8.0, 'ssm_conv_b': 3.51, 'ffn_dw_b': 8.0}
    for name, (base, spread) in spreads.items():
        noise = np.random.default_rng([zlib.crc32(name.encode()), seed]).standard_normal(out[name].shape)
        drawn = base * np.exp(spread * noise) if base else spread * noise
        out[name] = __import__('jax').numpy.asarray(drawn.astype(out[name].dtype))
    for name, factor in factors.items():
        out[name] = (out[name] * factor).astype(out[name].dtype)
    return out
```

```python
import concourse.bass as bass
from concourse import mybir
from concourse.alu_op_type import AluOpType as ALU
import numpy as np
from contextlib import ExitStack

F32 = mybir.dt.float32
F32R = mybir.dt.float32r
I32 = mybir.dt.int32
ACT = mybir.ActivationFunctionType
AX = mybir.AxisListType

D = 2048
NP, NB, NT = 512, 8, 8
NS = NB * NT
TOK = NP + NS
HALF = TOK // 2
KT = D // 128
HD, NH, NG, HPG = 64, 16, 4, 4
PAST, PAGE = 512, 128
QW = NH * HD
KVW = 6 * NG * HD
O_KV = QW
O_GATE = O_KV + KVW
O_Z = O_GATE + 3 * NH
O_XBC = O_Z + 1024
XBC = 2048
O_DT = O_XBC + XBC
INW = O_DT + NH
FF = 5504
FT = FF // 128
NCMP = 31
NSEL = 9
STATE = 128
EPS = 1e-6
NEG = -1e30
CLAMP = -1e29
TINY = 1e-30
BL = 656
BX = 520
XT = XBC // 128
NHIST, FHIST = 3, 2
TILES = [(128 * i, min(128, TOK - 128 * i)) for i in range(-(-TOK // 128))]
NTT = len(TILES)

U_Q, U_XBC, U_KV, U_Z, U_GD = 0, 32, 96, 144, 176
U_OUT = U_GD + 2
U_FFN = U_OUT + 4 * KT
U_DOWN = U_FFN + 8 * FT
U_END = U_DOWN + 4 * FT

C_ID, C_TRI, C_CB, C_TRIS, C_CBS, C_SEQ, C_SAME, C_OV, C_WM, C_IOTA = 0, 128, 256, 384, 448, 512, 520, 648, 657, 665
C_ONE, C_BLK = 672, 800
C_END = 864


def constants():
    c = np.zeros((128, C_END), np.float32)
    k, i = np.arange(128)[:, None], np.arange(128)[None, :]
    c[:, C_ID:C_ID + 128] = k == i
    c[:, C_TRI:C_TRI + 128] = k <= i
    c[:, C_CB:C_CB + 128] = np.where(k <= i, 0.0, NEG)
    ks, js = np.arange(64)[:, None], np.arange(64)[None, :]
    same = ks // NT == js // NT
    c[:64, C_TRIS:C_TRIS + 64] = same & (ks <= js)
    c[:64, C_CBS:C_CBS + 64] = np.where(same & (ks <= js), 0.0, NEG)
    c[:64, C_SEQ:C_SEQ + 8] = ks // NT == np.arange(8)[None, :]
    c[:, C_SAME:C_SAME + 128] = (k // 32 == i // 32) & (k % 8 == i % 8)
    c0, s0 = np.arange(NCMP)[:, None] * 16, np.arange(NSEL)[None, :] * 64
    c[:NCMP, C_OV:C_OV + NSEL] = np.clip(np.minimum(c0 + 32, s0 + 64) - np.maximum(c0, s0), 0, None) / 32
    c[:, C_WM:C_WM + 8] = np.where(np.arange(8)[None, :] < k % 8, NEG, 0.0)
    c[:, C_IOTA:C_IOTA + 6] = np.arange(1, 7)[None, :]
    c[:, C_ONE:C_ONE + 128] = 1.0
    c[:64, C_BLK:C_BLK + 64] = same
    return c


def onehot():
    dist = BX - np.arange(BL)
    n = np.maximum(dist, 0)
    nf = np.maximum(n, 1).astype(np.float32)
    large = 16 + (np.log(nf / np.float32(16)) / np.float32(np.log(8.0)) * np.float32(16)).astype(np.int32)
    b = np.where(n < 16, n, np.minimum(large, 31))
    o = np.zeros((33, BL), np.float32)
    ok = dist >= 0
    o[b[ok], np.arange(BL)[ok]] = 1.0
    o[32, ~ok] = NEG
    return o


def build(nc, A, O):
    ctx = ExitStack()
    with ctx:
        def at(name, shape, off, dt=F32):
            return nc.alloc_sbuf_tensor_at(name, shape, dt, offset=BASE + off)

        def sem(name):
            return ctx.enter_context(nc.semaphore(name))

        def dram(ap, off, dims):
            return bass.AP(ap.tensor, off, dims)

        BASE = -(-nc.sbuf_base // 32) * 32
        ps = ctx.enter_context(nc.psum_tensor("ps", [128, 8, 512], F32))
        RA = 0
        RW = 73728
        RC = RW + 16384
        RB = RC + 8192
        hT_hi = at("hT_hi", [128, KT, TOK], RA, F32R)
        hT_lo = at("hT_lo", [128, KT, TOK], RA + 36864, F32R)
        w_raw = at("w_raw", [128, 4, 512], RW)
        w_hi = at("w_hi", [128, 2, 512], RW + 8192, F32R)
        w_lo = at("w_lo", [128, 2, 512], RW + 12288, F32R)
        con = at("con", [128, C_END], RC)
        cwT = at("cwT", [128, XT, 29], RC + 3456)
        cst = at("cst", [128, XT, 27], RC + 3456 + 1856)
        small = at("small", [128, 256], RC + 3456 + 1856 + 1728)
        qT = at("qT", [128, 8, TOK], RB)
        xbcT = at("xbcT", [128, XT, TOK], RB + 18432)
        kvt = at("kvt", [128, NTT, KVW], RB + 55296)
        zs = at("zs", [128, NTT, 1024], RB + 86016)
        RX = RB + 106496
        xr = at("xr", [128, 604], RX)
        xc = at("xc", [128, 604], RX + 2432)
        xin = at("xin", [128, NTT, D], RB + 55296)
        gb = at("gb", [128, D], RB + 55296 + 40960)
        cwst = at("cwst", [29, XBC], RB + 18432)
        junk = at("junk", [128, D], RB)
        gdt = at("gdt", [128, NTT, 64], RX)
        ss = small[:, 0:5]
        rs = small[:, 5:10]
        ident = con[:, C_ID:C_ID + 128]

        ld_const, ld_x, ld_g, ld_cw = sem("ld_const"), sem("ld_x"), sem("ld_g"), sem("ld_cw")
        raw_loaded = [sem(f"raw_loaded{i}") for i in range(4)]
        hi_done, lo_done, pe_unit = sem("hi_done"), sem("lo_done"), sem("pe_unit")
        phase = sem("phase_done")
        a_ch, v_ch = sem("act_chain"), sem("dve_chain")
        ss_ready, xn_ready = sem("ss_ready"), sem("xn_ready")
        xT_ready, hT_hi_done, hT_lo_done = sem("xT_ready"), sem("hT_hi_done"), sem("hT_lo_done")
        cw_ready = sem("cwT_transposed")
        feat_evac, tok_evac, xr_ready, conv_done = sem("feat_evac"), sem("tok_evac"), sem("xr_ready"), sem("conv_done")
        kv_stored, out_stored = sem("kv_stored"), sem("out_stored")

        w_in, w_out = A["w_in"], A["w_out"]

        class Chain:
            def __init__(self, eng, s):
                self.eng, self.s, self.n = eng, s, 0

            def __call__(self, ins):
                self.n += 1
                ins.then_inc(self.s, 1)
                self.eng.wait_ge(self.s, self.n)

        def join(eng, k):
            eng.drain().then_inc(phase, 1)
            eng.wait_ge(phase, 4 * (k + 1))

        block = ctx.enter_context(nc.Block())

        xsk = at("xs_tok", [128, NTT, 1024], RA)
        Bk = at("B_tok", [128, NTT, 512], RA + 20480)
        h0r = at("h0", [128, 2, NB, STATE], RA + 30720)
        h0T = at("h0T", [128, NB, 128], RA + 38912)
        hst = at("h_state", [128, 1024], RA + 38912)
        seg = at("seg", [128, 2, 4, 128], RA + 43008)
        bex = at("B_by_sequence", [64, NB, 128], RA + 47104)
        yoff = at("y_off", [64, 1024], RA + 51200)
        xdt = at("x_dt", [128, 2, 1024], RA + 55296)
        xte = at("x_to_end", [128, 2, 1024], RA + 63488)
        sp_ = at("ssd_small", [128, 512], RA + 71680)
        dtb, eA, dsk = sp_[:, 0:16], sp_[:, 16:32], sp_[:, 32:48]
        r5 = lambda o: sp_[:, o:o + 80].rearrange("p (t h) -> p t h", t=NTT)
        dt_, a_, eac, ete, eto = r5(48), r5(128), r5(208), r5(288), r5(368)
        ss2 = sp_[:, 448:468]
        pool_ch = sem("pool_chain")
        acs = at("a_cumulative", [128, NTT, NH], RX + 6656)
        dec = sp_[:, 468:484].rearrange("p (b s) -> p b s", b=2)
        yoT = at("y_off_T", [128, 64], RX + 6400)
        ngb = at("norm_gain", [128, 1024], RX + 1280)
        tmp2 = at("y_tmp", [128, 256], RX + 5376)
        v_, w5 = xdt[:, 0, 0:80].rearrange("p (t h) -> p t h", t=NTT), xdt[:, 0, 80:160].rearrange("p (t h) -> p t h", t=NTT)
        cso = at("conv_out", [27, XBC], RA + 30720)
        hso = at("state_out", [128, 8, 128], RA + 47104)
        ld_ssd = sem("ld_ssd")
        h0_loaded, h0_stored = [sem("h0_loaded0"), sem("h0_loaded1")], [sem("h0_stored0"), sem("h0_stored1")]
        tokT_ready, tokT_evac, a_ready, sums_ready, exps_ready = sem("tokT_ready"), sem("tokT_evac"), sem("a_ready"), sem("sums_ready"), sem("exps_ready")
        sum_ready = sem("sum_copies_ready")
        v_ready, l_ready = sem("softplus_arg"), sem("softplus_log")
        h0T_ready, h0T_evac, yo_ready, yoT_evac = sem("h0T_ready"), sem("h0T_evac"), sem("yo_ready"), sem("yoT_evac")
        yoff_ready, yoff_evac, dec_ready, newps_ready, new_ready = sem("yoff_ready"), sem("yoff_evac"), sem("dec_ready"), sem("newps_ready"), sem("new_ready")
        bexp_ready, xt_ready = sem("bexp_ready"), sem("xt_ready")
        s1_ready, seg_ready, dec_exp, M_done = sem("s1_ready"), sem("seg_ready"), sem("decay_ready"), sem("M_done")
        y_ready, unit_done = sem("y_ready"), sem("ssd_unit_done")
        ss2_ready, inv2, rs2 = sem("ss2_ready"), sem("inv2"), sem("rs2_ready")
        fin_T, fin_copied, ssd_stored = sem("fin_T"), sem("fin_copied"), sem("ssd_stored")

        XF = RB + 36864
        mixA = at("mix_attn", [128, 8, TOK], RB + 18432)
        vc = at("v_cmp", [NCMP, 9, 256], XF)
        kcT = at("k_cmp_T", [128, 9, 2, NCMP], XF + 9216)
        kvp = at("pairs_T", [128, 2, 4, 4, 256], RA)
        craw = at("cmp_rows", [128, 2, 2, 2, 4, 2, 64], RA + 32768)
        w1p = at("w1_pairs", [128, 2, 16, 128], RA + 49152)
        gact = at("cmp_hidden", [128, 496], RA + 65536)
        cs = at("cmp_small", [128, 480], RA + 67584)
        w2t, b1t, b2k, hb = cs[:, 0:128].rearrange("p (a d) -> p a d", a=2), cs[:, 128:130], cs[:, 130:131], cs[:, 132:134]
        b2v, pes, peT = cs[0:NCMP, 136:200], cs[0:32, 200:328], cs[:, 328:360]
        tab = cs[0:33, 360:376]
        oh = at("onehot_sb", [33, BL], RA + 69504)
        brow = at("bias_rows", [NH, BL], RX + 1280)
        rb = nc.dram_tensor("bias_scratch", (NH, 128, BL), F32).ap()
        gsc = nc.dram_tensor("gate_scratch", (128, 24), F32).ap()
        ld_c, rb_stored, gsc_stored, tab_set, win_copied = sem("ld_cmp_params"), sem("bias_stored"), sem("gates_stored"), sem("tab_set"), sem("win_copied")
        craw_loaded = [sem("craw_loaded0"), sem("craw_loaded1")]
        rb_mm, rb_ready, pe_T, peT_ready, pb_mm, hb_ready = sem("bias_mm"), sem("bias_rows_ready"), sem("pe_T"), sem("peT_ready"), sem("pe_bias_mm"), sem("hid_bias_ready")
        pairT_ready, pairT_evac = sem("pairT_ready"), sem("pairT_evac")
        hid_ready, gelu_done, kc_ready, kc_evac, vc_ready, vc_evac = sem("hid_ready"), sem("gelu_done"), sem("kc_ready"), sem("kc_evac"), sem("vc_ready"), sem("vc_evac")
        CH = [(0, 4), (4, 4), (8, 1)]

        araw = at("kv_rows", [128, 3, 4, 512], RA)
        KTs = at("K_T", [128, 2, 2, 512], RA + 24576)
        pTs = at("p_T", [128, 2, 5, 128], RA + 32768)
        scs = at("scores_s", [128, 2, 576], RA + 37888)
        sb_ = at("bias_s", [128, 2, 512], RA + 42496)
        nb = at("bias_new", [128, 120], RA + 46592)
        qs = at("q_s", [128, 2, NB, 32], RA + 47104)
        knT = at("k_new_T", [128, 2, 2, 64], RA + 49152)
        pc0 = at("pc_T", [NCMP, NB, 128], RA + 50176)
        pcg = at("pc_gated_T", [NCMP, NB, 128], RA + 54272)
        scc = at("scores_c", [128, NB, NCMP], RA + 58368)
        scg = at("probs_c_gated", [128, NB, NCMP], RA + 59392)
        osb = at("o_s", [128, 2, 64], RA + 60416)
        as_ = at("attn_small", [128, 512], RA + 61440)
        imp = as_[:, 0:72].rearrange("p (s b) -> p s b", s=NB)
        drop = as_[:, 72:120].rearrange("p (s b) -> p s b", s=NB)
        d1 = as_[:, 120:168].rearrange("p (s b) -> p s b", s=NB)
        m8, r8 = as_[:, 168:176], as_[:, 176:184]
        gsm = as_[:, 184:208].rearrange("p (s b) -> p s b", s=NB)
        st_ = as_[:, 208:232].rearrange("p (u x) -> p u x", u=2)
        ld_b, ld_gs = sem("ld_bias_s"), sem("ld_gates_s")
        a_loaded = [sem(f"kv_rows_loaded{i}") for i in range(3)]
        nb_set, qs_ready, kn_mm, kn_ready = sem("nb_set"), sem("qs_ready"), sem("kn_mm"), sem("kn_ready")
        sc_mm, pc_sub, pc_exp, pc_ready, pcT_mm, pcT_evac = sem("cmp_scores_mm"), sem("pc_sub"), sem("pc_exp"), sem("pc_ready"), sem("pcT_mm"), sem("pcT_evac")
        imp_mm, imp_ready, imp2_mm, drop_ready, pcg_ready = sem("imp_mm"), sem("imp_ready"), sem("imp2_mm"), sem("drop_ready"), sem("pcg_ready")
        KT_mm, KT_evac, s_mm, s_max, s_exp, s_p, pT_mm, pT_evac, pv_mm = [sem("sa_" + x) for x in ("KT_mm", "KT_evac", "scores", "max", "exp", "probs", "pT_mm", "pT_evac", "pv")]
        o_ready, oT_mm, oT_evac = sem("sa_o_ready"), sem("sa_oT_mm"), sem("sa_oT_evac")

        TT = at("bias_p", [128, NH, 512], RA)
        pT = at("pT_prompt", [128, 2, 2, 4, 512], RA + 32768)
        pcT = at("pcT_prompt", [NCMP, 2, 512], RA + 65536)
        ast = at("softmax_small", [128, 64], RA + 69632)
        KTp = at("K_T_prompt", [128, 2, 2, 512], XF)
        scp = at("scores_p", [128, 3, 512], XF + 11520)
        ld_TT, kp_mm, kp_evac = sem("ld_TT"), sem("kp_mm"), sem("kp_evac")
        P_mm, P_add, P_max, P_exp, P_p, P_T, P_Te, P_pv, P_o = [sem("pa_" + x) for x in ("scores", "scores_copied", "max", "exp", "probs", "pT_mm", "pT_evac", "pv", "o_evac")]
        NU = 12 * NH
        def pu(w):
            h, i, br = w // 12, w % 12 // 3, w % 3
            return h, i, br, (128 * (i + 1) if br < 2 else 7 + 8 * i)

        mo = at("mix_out", [128, NTT, D], RB)
        gb2 = at("gain2", [128, D], RB + 40960)
        x2d = nc.dram_tensor("x2_scratch", (TOK, D), F32).ap()
        acT = at("ffn_act_T", [128, FT, TOK], RB)
        fwT = at("ffn_params_T", [128, FT, 20], RB + 99072)
        fst = at("ffn_conv_rows", [128, FT, 18], RB + 102528)
        xr2 = at("ffn_xr", [128, 594], RB + 105632)
        xc2 = at("ffn_xc", [128, 594], RB + 108032)
        gl = at("gelu_gate", [128, TOK], RB + 110432)
        fwst = at("ffn_params", [20, FF], RB + 55296)
        a_hi = at("act_hi", [128, 2, TOK], RA, F32R)
        a_lo = at("act_lo", [128, 2, TOK], RA + 4608, F32R)
        yb = at("ffn_out", [128, NTT, D], RA + 9216)
        gb3 = at("gain3", [128, D], RA + 50176)
        x2r = at("x2", [128, NTT, D], RB)
        fco = at("ffn_conv_out", [18, FF], RB + 49152)
        ms_hi, ms_lo = sem("mix_hi"), sem("mix_lo")
        x2_ready, x2_stored, fw_T = sem("x2_ready"), sem("x2_stored"), sem("fw_T")
        g_ready, g_sum, g_act, up_done, f_ch = sem("gate_out"), sem("gate_sum"), sem("gate_act"), sem("up_done"), sem("ffn_chain")
        ahi_done, alo_done, y_evac, fin_y, y_stored = sem("act_hi_done"), sem("act_lo_done"), sem("y_evac"), sem("y_ready_out"), sem("y_stored")
        fco_T, fco_done = sem("fco_T"), sem("fco_done")

        def loop_units(c):
            return range(3), 10

        def bc(ap, dims):
            return ap.unsqueeze(len(ap.shape)).broadcast_to(dims)

        @block.sync
        def _(sp):
            sp.dma_start(con[:], A["con"]).then_inc(ld_const, 16)
            for t, (t0, n) in enumerate(TILES):
                src = A["x_prompt"][0, t0:t0 + n, :] if t < 4 else A["x_sample"].rearrange("b t d -> (b t) d")
                sp.dma_start(xin[0:n, t, :], src).then_inc(ld_x, 16)
            sp.dma_start(gb[:], dram(A["ln_mix_pre"], 0, [[0, 128], [1, D]])).then_inc(ld_g, 16)
            sp.dma_start(cwst[0:24, :], A["state_ssm_conv"].rearrange("l b k c -> (l b k) c")).then_inc(ld_cw, 16)
            sp.dma_start(cwst[24:28, :], A["ssm_conv_w"].rearrange("l k c -> (l k) c")).then_inc(ld_cw, 16)
            sp.dma_start(cwst[28:29, :], A["ssm_conv_b"]).then_inc(ld_cw, 16)

            def unit(u, src, shape):
                if u >= 4:
                    sp.wait_ge(lo_done, u - 3)
                dst = w_raw[:, u % 4, :]
                if shape:
                    dst = dst.rearrange("p (k c) -> p k c", k=shape)
                sp.dma_start(dst, src).then_inc(raw_loaded[u % 4], 16)

            def feat_cols(w, wd, col, k0):
                return dram(w, k0 * 128 * wd + col, [[wd, 128], [128 * wd, 4], [1, 128]])

            for f in range(8):
                gp, r = f // 4, f % 4
                for j in range(4):
                    col = (8 * gp + r) * HD
                    u = U_Q + 4 * f + j
                    if u >= 4:
                        sp.wait_ge(lo_done, u - 3)
                    for h in range(2):
                        dst = w_raw[:, u % 4, :].rearrange("p (k c) -> p k c", k=4)[:, :, 64 * h:64 * h + 64]
                        src = dram(w_in, j * 512 * INW + col + 256 * h, [[INW, 128], [128 * INW, 4], [1, 64]])
                        sp.dma_start(dst, src).then_inc(raw_loaded[u % 4], 16)
            for f in range(XT):
                for j in range(4):
                    unit(U_XBC + 4 * f + j, feat_cols(w_in, INW, O_XBC + 128 * f, 4 * j), 4)
            for c in range(5):
                col = O_KV + 512 * c if c < 3 else O_Z + 512 * (c - 3)
                for k in range(KT):
                    unit(U_KV + KT * c + k, dram(w_in, k * 128 * INW + col, [[INW, 128], [1, 512]]), 0)
            for j in range(2):
                u = U_GD + j
                sp.wait_ge(lo_done, u - 3)
                d = w_raw[:, u % 4, :].rearrange("p (k c) -> p k c", k=8)
                sp.dma_start(d[:, :, 0:48], dram(w_in, j * 1024 * INW + O_GATE, [[INW, 128], [128 * INW, 8], [1, 48]])).then_inc(raw_loaded[u % 4], 16)
                sp.dma_start(d[:, :, 48:64], dram(w_in, j * 1024 * INW + O_DT, [[INW, 128], [128 * INW, 8], [1, 16]])).then_inc(raw_loaded[u % 4], 16)

            sp.wait_ge(phase, 8)
            sp.dma_start(dtb, dram(A["ssm_dt_bias"], 0, [[0, 128], [1, NH]])).then_inc(ld_ssd, 16)
            sp.dma_start(eA, dram(A["ssm_a_log"], 0, [[0, 128], [1, NH]])).then_inc(ld_ssd, 16)
            sp.dma_start(dsk, dram(A["ssm_d"], 0, [[0, 128], [1, NH]])).then_inc(ld_ssd, 16)
            sp.dma_start(ngb[:], dram(A["ssm_norm_g"], 0, [[0, 128], [1, 1024]])).then_inc(ld_ssd, 16)
            HS = NH * HD * STATE
            for p in range(10):
                if p >= 2:
                    q = p - 2
                    sp.wait_ge(new_ready, q + 1)
                    sp.dma_start(dram(O["ssm_sample"], q * 16384, [[STATE, 128], [HS, NB], [1, STATE]]), h0r[:, q % 2]).then_inc(h0_stored[q % 2], 16)
                if p < 8:
                    if p >= 2:
                        sp.wait_ge(h0_stored[p % 2], 16 * (p // 2))
                    sp.dma_start(h0r[:, p % 2], dram(A["state_ssm"], p * 16384, [[STATE, 128], [HS, NB], [1, STATE]])).then_inc(h0_loaded[p % 2], 16)
            sp.wait_ge(fin_copied, 2)
            sp.dma_start(O["ssm_conv_prompt"].rearrange("l b k c -> (l b k) c"), cso[0:3, :]).then_inc(ssd_stored, 16)
            sp.dma_start(O["ssm_conv_sample"].rearrange("l b k c -> (l b k) c"), cso[3:27, :]).then_inc(ssd_stored, 16)
            sp.dma_start(dram(O["ssm_prompt"], 0, [[STATE, 128], [16384, 8], [1, STATE]]), hso[:]).then_inc(ssd_stored, 16)
            sp.wait_ge(phase, 12)
            sp.wait_ge(ssd_stored, 48)
            sp.dma_start(oh[:], A["onehot"]).then_inc(ld_c, 16)
            sp.dma_start(tab[0:32, :], A["rel_table"]).then_inc(ld_c, 16)
            sp.dma_start(pes, A["cmp_pe"].rearrange("l a (s q) d -> (l a s) (q d)", q=2)).then_inc(ld_c, 16)
            for a in range(2):
                sp.dma_start(w1p[:, a], dram(A["cmp_w1"], a * 262144, [[128, 128], [16384, 16], [1, 128]])).then_inc(ld_c, 16)
            sp.dma_start(w2t, dram(A["cmp_w2"], 0, [[64, 128], [8192, 2], [1, 64]])).then_inc(ld_c, 16)
            sp.dma_start(b1t, dram(A["cmp_b1"], 0, [[1, 128], [128, 2]]), allow_slow_non_contiguous=True).then_inc(ld_c, 16)
            for a in range(2):
                sp.dma_start(cs[64 * a:64 * a + 64, 130:131], dram(A["cmp_b2"], 0, [[1, 64], [1, 1]])).then_inc(ld_c, 16)
            sp.dma_start(b2v, dram(A["cmp_b2"], 64, [[0, NCMP], [1, 64]])).then_inc(ld_c, 16)
            for s in range(NB):
                for b in range(3):
                    sp.dma_start(dram(gsc, 3 * s + b, [[24, NT], [192, NH]]), gdt[8 * s:8 * s + 8, 4, 16 * b:16 * b + 16],
                                 allow_slow_non_contiguous=True).then_inc(gsc_stored, 16)
            sp.wait_ge(kv_stored, 64)
            PGW = PAGE * 1024
            ckv = A["cache_kv"].rearrange("l n t s g d -> (l n) (t s g d)")
            def page_index(s, p):
                return sp.value_load(A["page_table"][s:s + 1, p:p + 1], min_val=0, max_val=39)
            for s in range(9):
                if s >= 2:
                    sp.wait_ge(pairT_evac, 4 * (s - 1))
                for p in range(4):
                    dst = craw[64 * (p % 2):64 * (p % 2) + 64, s % 2, p // 2]
                    if s < 8:
                        src = ckv[bass.ds(page_index(s, p), 1), :].rearrange("n (i q s g d) -> i (n s g) q d", q=2, s=4, g=NG, d=HD)[:, 0:8]
                    else:
                        src = O["kv_prompt"].rearrange("l b t s g d -> (l b t) s g d")[128 * p:128 * p + 128].rearrange("(i q) s g d -> i (s g) q d", q=2)[:, 0:8]
                    dst = dst.rearrange("i a g q d -> i (a g) q d")
                    for q in range(2):
                        sp.dma_start(dst[:, :, q, :], src[:, :, q, :]).then_inc(craw_loaded[s % 2], 16)
            sp.wait_ge(rb_ready, 1)
            sp.dma_start(rb, brow[:].unsqueeze(1).broadcast_to([NH, 128, BL])).then_inc(rb_stored, 16)
            for s in range(NB):
                sp.dma_start(O["win_sample"][0, s, 0:PAST - NT].rearrange("t s g d -> t (s g d)"),
                             A["cache_win_kv"][0, s, NT:PAST].rearrange("t s g d -> t (s g d)")).then_inc(win_copied, 16)
            sp.wait_ge(phase, 16)
            sp.wait_ge(rb_stored, 16)
            sp.wait_ge(gsc_stored, 16 * 3 * NB)
            sp.wait_ge(nb_set, 1)
            for h in range(NH):
                sp.dma_start(sb_[8 * h:8 * h + 8, 0, :], dram(rb, h * 128 * BL + 8, [[BL - 1, 8], [1, 512]])).then_inc(ld_b, 16)
                sp.dma_start(nb[8 * h:8 * h + 8, 56:64], dram(rb, h * 128 * BL + BX, [[BL - 1, 8], [1, 8]])).then_inc(ld_b, 16)
            sp.dma_start(as_[:, 184:208], gsc).then_inc(ld_gs, 16)
            for y in range(16):
                s, br = y // 2, y % 2
                if y >= 3:
                    sp.wait_ge(pv_mm, y - 2)
                if br == 0:
                    for p in range(4):
                        src = ckv[bass.ds(page_index(s, p), 1), :].rearrange("n (t c) -> (n t) c", t=PAGE)[:, 512:1024]
                        sp.dma_start(araw[:, y % 3, p, :], src).then_inc(a_loaded[y % 3], 16)
                else:
                    for p in range(4):
                        sp.dma_start(araw[:, y % 3, p, :], A["cache_win_kv"][0, s, 128 * p:128 * p + 128].rearrange("t s g d -> t (s g d)")).then_inc(a_loaded[y % 3], 16)
            sp.wait_ge(phase, 20)
            sp.dma_start(TT[:], dram(rb, 136, [[BL - 1, 128], [128 * BL, NH], [1, 512]])).then_inc(ld_TT, 16)
            for c in range(4):
                for k in range(KT):
                    unit(U_OUT + KT * c + k, dram(A["w_out"], k * 128 * D + 512 * c, [[D, 128], [1, 512]]), 0)
            sp.wait_ge(phase, 28)
            sp.wait_ge(out_stored, 208)
            for t, (t0, n) in enumerate(TILES):
                src = A["x_prompt"][0, t0:t0 + n, :] if t < 4 else A["x_sample"].rearrange("b t d -> (b t) d")
                sp.dma_start(xin[0:n, t, :], src).then_inc(ld_x, 16)
            sp.dma_start(gb[:], dram(A["ln_mix_post"], 0, [[0, 128], [1, D]])).then_inc(ld_g, 16)
            sp.dma_start(gb2[:], dram(A["ln_ffn_pre"], 0, [[0, 128], [1, D]])).then_inc(ld_g, 16)
            for t, (t0, n) in enumerate(TILES):
                sp.wait_ge(x2_ready, t + 1)
                sp.dma_start(x2d[t0:t0 + n, :], xin[0:n, t, :]).then_inc(x2_stored, 16)
            sp.wait_ge(phase, 32)
            sp.wait_ge(x2_stored, 16 * NTT)
            sp.dma_start(fwst[0:16, :], A["state_ffn_conv"].rearrange("l b k c -> (l b k) c")).then_inc(ld_cw, 16)
            sp.dma_start(fwst[16:19, :], A["ffn_dw_w"].rearrange("l k c -> (l k) c")).then_inc(ld_cw, 16)
            sp.dma_start(fwst[19:20, :], A["ffn_dw_b"]).then_inc(ld_cw, 16)
            W2 = [A[x][0].rearrange("(k p) c -> p k c", p=128) for x in ("ffn_w_gate", "ffn_w_up")]
            with sp.Fori(0, FT) as f:
                for j in range(8):
                    sp.wait_ge(lo_done, f * 8 + (U_FFN + j - 3))
                    sp.dma_start(w_raw[:, (U_FFN + j) % 4, :].rearrange("p (k c) -> p k c", k=4),
                                 W2[j // 4][:, 4 * (j % 4):4 * (j % 4) + 4, bass.ds(f * 128, 128)]).then_inc(raw_loaded[(U_FFN + j) % 4], 16)
            Wd = A["ffn_w_down"][0]
            for c in range(4):
                u0 = U_DOWN + FT * c
                peeled, turns = loop_units(c)
                for k in peeled:
                    unit(u0 + k, Wd[128 * k:128 * k + 128, 512 * c:512 * c + 512], 0)
                with sp.Fori(0, turns) as i:
                    for j in range(4):
                        sp.wait_ge(lo_done, i * 4 + (u0 + j))
                        sp.dma_start(w_raw[:, (u0 + 3 + j) % 4, :], Wd[bass.ds(i * 512 + 128 * (3 + j), 128), 512 * c:512 * c + 512]).then_inc(raw_loaded[(u0 + 3 + j) % 4], 16)
            sp.wait_ge(phase, 40)
            for t, (t0, n) in enumerate(TILES):
                sp.dma_start(x2r[0:n, t, :], x2d[t0:t0 + n, :]).then_inc(ld_x, 16)
            sp.dma_start(gb3[:], dram(A["ln_ffn_post"], 0, [[0, 128], [1, D]])).then_inc(ld_x, 16)
            sp.wait_ge(fco_done, 3)
            sp.dma_start(O["ffn_conv_prompt"].rearrange("l b k c -> (l b k) c"), fco[0:2, :]).then_inc(y_stored, 16)
            sp.dma_start(O["ffn_conv_sample"].rearrange("l b k c -> (l b k) c"), fco[2:18, :]).then_inc(y_stored, 16)
            for t, (t0, n) in enumerate(TILES):
                sp.wait_ge(fin_y, t + 1)
                dst = O["y_prompt"][0, t0:t0 + n, :] if t < 4 else O["y_sample"].rearrange("b t d -> (b t) d")
                sp.dma_start(dst, yb[0:n, t, :]).then_inc(y_stored, 16)
            sp.wait_ge(y_stored, 16 * (2 + NTT))
            sp.wait_ge(win_copied, 128)
            sp.wait_ge(ssd_stored, 48)
            sp.wait_ge(h0_stored[0], 64)
            sp.wait_ge(h0_stored[1], 64)
            sp.wait_ge(kv_stored, 64)
            sp.wait_ge(out_stored, 208)

        def raw_count(u):
            return 16 * sum(2 if v < U_XBC or U_GD <= v < U_OUT else 1 for v in range(u % 4, u + 1, 4))

        def act_feature(act, ch, f):
            act.wait_ge(pe_unit, 4 * (f + 1))
            b = 2 * (f % 2)
            if f < 8:
                act.activation(qT[:, f, :].rearrange("p (h c) -> p h c", h=2), ps[:, b:b + 2, 0:HALF],
                               ACT.Copy, scale=HD ** -0.5).then_inc(feat_evac, 1)
                return
            x = f - 8
            if x:
                act.wait_ge(conv_done, x)
            act.activation(xr[:, 3:3 + HALF], ps[:, b, 0:HALF], ACT.Copy)
            act.activation(xr[:, 3 + HALF:3 + NP], ps[:, b + 1, 0:NP - HALF], ACT.Copy)
            last = act.activation(xr[:, 515:603].rearrange("p (s c) -> p s c", s=8)[:, :, 3:11],
                                  ps[:, b + 1, NP - HALF:HALF].rearrange("p (s c) -> p s c", s=8), ACT.Copy)
            last.then_inc(xr_ready, 1)
            act.wait_ge(xr_ready, x + 1)
            act.sem_inc(feat_evac, 1)
            act.wait_ge(acc_ready, x + 1)
            act.activation(xbcT[:, x, 0:NP], xc[:, 0:NP], ACT.Silu)
            act.activation(xbcT[:, x, NP:TOK].rearrange("p (s c) -> p s c", s=8),
                           xc[:, 515:603].rearrange("p (s c) -> p s c", s=8)[:, :, 0:8], ACT.Silu).then_inc(conv_done, 1)

        inv_ready = sem("mean_square_inverse")
        rs_ready = sem("rs_ready")
        small_zero = sem("small_zeroed")
        acc_ready = sem("conv_sum_ready")

        def act_tokens(act, ch, c):
            act.wait_ge(pe_unit, U_KV + KT * (c + 1))
            for t, (t0, n) in enumerate(TILES):
                if c < 3:
                    i = act.activation(kvt[0:n, t, 512 * c:512 * c + 512], ps[0:n, t, :], ACT.Copy)
                else:
                    i = act.activation(zs[0:n, t, 512 * (c - 3):512 * (c - 3) + 512], ps[0:n, t, :], ACT.Silu)
                i.then_inc(tok_evac, 1)
            if c == 2:
                act.wait_ge(tok_evac, 5 * (c + 1))
                for t, (t0, n) in enumerate(TILES[:4]):
                    act.dma_start(O["kv_prompt"].rearrange("l b t s g d -> (l b t) (s g d)")[t0:t0 + n, :],
                                  kvt[0:n, t, 0:1024]).then_inc(kv_stored, 16)
                    act.dma_start(O["win_prompt"].rearrange("l b t s g d -> (l b t) (s g d)")[t0:t0 + n, :],
                                  kvt[0:n, t, 1024:1536]).then_inc(out_stored, 16)
                act.dma_start(O["kv_sample"].rearrange("l b t s g d -> (l b t) (s g d)"), kvt[0:NS, 4, 0:1024]).then_inc(out_stored, 16)
                for s in range(NB):
                    act.dma_start(O["win_sample"][0, s, PAST - NT:PAST].rearrange("t s g d -> t (s g d)"),
                                  kvt[8 * s:8 * s + 8, 4, 1024:1536]).then_inc(out_stored, 16)

        def out_tokens(act, c):
            act.wait_ge(pe_unit, U_OUT + KT * (c + 1))
            for t, (t0, n) in enumerate(TILES):
                act.activation(mo[0:n, t, 512 * c:512 * c + 512], ps[0:n, t, :], ACT.Copy).then_inc(tok_evac, 1)

        def down_hi(act, c, k, i):
            v = FT * c + k
            u = U_DOWN + v
            at_ = (lambda per, base: base) if i is None else (lambda per, base: i * per + base)
            act.wait_ge(raw_loaded[u % 4], at_(16, raw_count(u)))
            act.wait_ge(pe_unit, at_(4, u - 1))
            act.activation(w_hi[:, u % 2, :], w_raw[:, u % 4, :], ACT.Copy).then_inc(hi_done, 1)
            src = acT[:, k, :] if i is None else acT[:, bass.ds(i * 4 + k, 1), :].rearrange("p a c -> p (a c)")
            act.activation(a_hi[:, v % 2, :], src, ACT.Copy).then_inc(ahi_done, 1)

        def down_lo(dve, c, k, i):
            v = FT * c + k
            at_ = (lambda per, base: base) if i is None else (lambda per, base: i * per + base)
            dve.wait_ge(ahi_done, at_(4, v + 1))
            src = acT[:, k, :] if i is None else acT[:, bass.ds(i * 4 + k, 1), :].rearrange("p a c -> p (a c)")
            dve.tensor_tensor(a_lo[:, v % 2, :], src, a_hi[:, v % 2, :].bitcast(F32), ALU.subtract).then_inc(alo_done, 1)

        def prompt_out(dve, h):
            dve.wait_ge(P_pv, h + 1)
            q = 64 * (h % 2)
            dve.tensor_copy(mixA[q:q + 64, h // 2, 0:NP], ps[q:q + 64, 5 + h // 2 % 2, :]).then_inc(P_o, 1)

        @block.scalar
        def _(act):
            ch = Chain(act, a_ch)

            def hi(u):
                act.wait_ge(raw_loaded[u % 4], raw_count(u))
                if u >= 2:
                    act.wait_ge(pe_unit, u - 1)
                act.activation(w_hi[:, u % 2, :], w_raw[:, u % 4, :], ACT.Copy).then_inc(hi_done, 1)

            act.wait_ge(ld_x, 16 * NTT)
            act.wait_ge(small_zero, 1)
            for t, (t0, n) in enumerate(TILES):
                ch(act.activation(junk[0:n, :], xin[0:n, t, :], ACT.Square, accum_out=small[0:n, t:t + 1]))
            act.drain().then_inc(ss_ready, 1)
            act.wait_ge(inv_ready, 1)
            act.activation(rs, rs, ACT.Sqrt).then_inc(rs_ready, 1)
            for g in range(4 * NTT):
                t, k4 = g // 4, g % 4
                t0, n = TILES[t]
                act.wait_ge(xT_ready, g + 1)
                act.activation(hT_hi[:, 4 * k4:4 * k4 + 4, t0:t0 + n],
                               ps[:, g % 8, :].rearrange("p (k c) -> p k c", k=4)[:, :, 0:n], ACT.Copy).then_inc(hT_hi_done, 1)
            join(act, 0)
            for f in range(24):
                hi(4 * f)
                hi(4 * f + 1)
                if f:
                    act_feature(act, ch, f - 1)
                hi(4 * f + 2)
                hi(4 * f + 3)
            for c in range(5):
                for k in range(KT):
                    hi(U_KV + KT * c + k)
                    if k == 1:
                        if c == 0:
                            act_feature(act, ch, 23)
                        else:
                            act_tokens(act, ch, c - 1)
            hi(U_GD)
            hi(U_GD + 1)
            act_tokens(act, ch, 4)
            act.wait_ge(pe_unit, U_GD + 2)
            for t, (t0, n) in enumerate(TILES):
                act.activation(gdt[0:n, t, :], ps[0:n, 5, 64 * t:64 * t + 64], ACT.Copy).then_inc(tok_evac, 1)
            join(act, 1)
            act.activation(gdt[:, :, 0:48], gdt[:, :, 0:48], ACT.Sigmoid)
            act.wait_ge(ld_ssd, 64)
            act.activation(eA, eA, ACT.Exp).then_inc(v_ready, 1)
            act.wait_ge(v_ready, 2)
            ch(act.activation(w5, w5, ACT.Exp))
            act.activation(w5, w5, ACT.Ln, bias=1.0).then_inc(l_ready, 1)
            for G in range(3 * NTT):
                t, b = G // 3, G % 3
                n = TILES[t][1]
                act.wait_ge(tokT_ready, G + 1)
                dst = xsk[0:n, t, 512 * b:512 * b + 512] if b < 2 else Bk[0:n, t, :]
                act.activation(dst, ps[0:n, G % 6, :], ACT.Copy).then_inc(tokT_evac, 1)
            act.wait_ge(sum_ready, 1)
            act.activation(sp_[:, 208:448], sp_[:, 208:448], ACT.Exp).then_inc(exps_ready, 1)
            for p in range(8):
                act.wait_ge(h0T_ready, p + 1)
                if p:
                    act.wait_ge(yo_ready, p)
                act.activation(h0T[:].rearrange("n (a s) p -> n a (s p)", a=2), ps[:, 0:2, :], ACT.Copy).then_inc(h0T_evac, 1)
                act.wait_ge(yo_ready, p + 1)
                if p:
                    act.wait_ge(yoff_ready, p)
                act.activation(yoT[:], ps[:, 2, 0:64], ACT.Copy).then_inc(yoT_evac, 1)
                if p >= 2:
                    act.wait_ge(new_ready, p - 1)
                act.activation(dec[:, p % 2, :], ps[:, 3, 0:8], ACT.Exp).then_inc(dec_ready, 1)
            for w in range(20):
                n = TILES[w // 4][1]
                act.wait_ge(seg_ready, w + 1)
                act.activation(seg[0:n, w % 2, :, 0:n], seg[0:n, w % 2, :, 0:n], ACT.Exp).then_inc(dec_exp, 1)
            act.wait_ge(unit_done, 20)
            for t, (t0, n) in enumerate(TILES):
                for g in range(4):
                    act.activation(xsk[0:n, 0, 0:256], zs[0:n, t, 256 * g:256 * g + 256], ACT.Square,
                                   accum_out=sp_[0:n, 448 + 4 * t + g:449 + 4 * t + g]).then_inc(ss2_ready, 1)
                    act.wait_ge(ss2_ready, 4 * t + g + 1)
            act.wait_ge(inv2, 1)
            act.activation(ss2, ss2, ACT.Sqrt).then_inc(rs2, 1)
            join(act, 2)
            act.wait_ge(rb_mm, 1)
            act.activation(brow[:, 0:512], ps[0:NH, 0, :], ACT.Copy)
            act.activation(brow[:, 512:BL], ps[0:NH, 1, 0:BL - 512], ACT.Copy).then_inc(rb_ready, 1)
            act.wait_ge(pe_T, 1)
            act.activation(peT, ps[:, 2, 0:32], ACT.Copy).then_inc(peT_ready, 1)
            act.wait_ge(hb_ready, 1)
            e = 0
            for c, (s0, ns) in enumerate(CH):
                for s in range(ns):
                    for b in range(4):
                        act.wait_ge(pairT_ready, e + 1)
                        if b == 0 and s == 0 and c:
                            act.wait_ge(hid_ready, 2 * c)
                        act.activation(kvp[:, b % 2, s, :, 128 * (b // 2):128 * (b // 2) + 128],
                                       ps[:, e % 2, :].rearrange("p (g i) -> p g i", g=4), ACT.Copy).then_inc(pairT_evac, 1)
                        e += 1
                n = 124 * ns
                for a in range(2):
                    act.wait_ge(hid_ready, 2 * c + a + 1)
                    if a or c:
                        act.wait_ge(kc_ready if a else vc_ready, c + 1 if a else c)
                    act.activation(gact[:, 0:n], ps[:, 2 + a, 0:n], ACT.Gelu_apprx_tanh, bias=hb[:, a:a + 1]).then_inc(gelu_done, 1)
                act.activation(kcT[:, s0:s0 + ns].rearrange("p s g n -> p (s g n)"), ps[:, 4, 0:62 * ns], ACT.Identity, bias=b2k).then_inc(kc_evac, 1)
            join(act, 3)
            act.wait_ge(kn_mm, 1)
            act.activation(knT[:].rearrange("p b g c -> p (b g c)"), ps[:, 0, 0:256], ACT.Copy).then_inc(kn_ready, 1)
            act.wait_ge(pc_sub, 1)
            act.activation(scc[:], scc[:], ACT.Exp).then_inc(pc_exp, 1)
            act.wait_ge(pcT_mm, 1)
            act.activation(pc0[:].rearrange("n (a s) p -> n a (s p)", a=2), ps[0:NCMP, 0:2, :], ACT.Copy).then_inc(pcT_evac, 1)
            act.wait_ge(pcT_mm, 2)
            act.activation(pcg[:].rearrange("n (a s) p -> n a (s p)", a=2), ps[0:NCMP, 4:6, :], ACT.Copy).then_inc(pcT_evac, 1)

            def kt_evac(y):
                for gp in range(2):
                    act.wait_ge(KT_mm, 2 * y + gp + 1)
                    if y >= 2:
                        act.wait_ge(s_mm, y - 1)
                    act.activation(KTs[:, y % 2, gp, :], ps[:, 4 + gp, :], ACT.Copy).then_inc(KT_evac, 1)

            def pt_evac(y):
                act.wait_ge(pT_mm, y + 1)
                if y >= 2:
                    act.wait_ge(pv_mm, y - 1)
                act.activation(pTs[:, y % 2, 0:4, :].rearrange("p k c -> p (k c)"), ps[:, 6, :], ACT.Copy)
                act.activation(pTs[0:64, y % 2, 4, :], ps[0:64, 7, 0:128], ACT.Copy).then_inc(pT_evac, 1)

            kt_evac(0)
            for y in range(17):
                if y < 16:
                    act.wait_ge(s_max, y + 1)
                    act.activation(scs[:, y % 2, :], scs[:, y % 2, :], ACT.Exp, bias=st_[:, y % 2, 0:1], accum_out=st_[:, y % 2, 1:2]).then_inc(s_exp, 1)
                if y < 15:
                    kt_evac(y + 1)
                if y >= 1:
                    pt_evac(y - 1)
            join(act, 4)
            for k in range(4):
                act.wait_ge(kp_mm, k + 1)
                act.activation(KTp[:, k // 2, k % 2, :], ps[:, k, :], ACT.Copy).then_inc(kp_evac, 1)
            for w in range(NU + 2):
                if w < NU:
                    h, i, br, n = pu(w)
                    act.wait_ge(P_max, w + 1)
                    act.activation(scp[:, w % 3, 0:n], scp[:, w % 3, 0:n], ACT.Exp, bias=ast[:, 4 * (w % 3):4 * (w % 3) + 1],
                                   accum_out=ast[:, 4 * (w % 3) + 1:4 * (w % 3) + 2]).then_inc(P_exp, 1)
                if w >= 2:
                    v = w - 2
                    h, i, br, n = pu(v)
                    act.wait_ge(P_T, v + 1)
                    if h >= 2 and v % 12 == 0:
                        act.wait_ge(P_pv, h - 1)
                    if br < 2:
                        act.activation(pT[:, h % 2, br, 0:i + 1, 128 * i:128 * i + 128],
                                       ps[:, 3 + v % 2, 0:n].rearrange("p (k c) -> p k c", c=128), ACT.Copy).then_inc(P_Te, 1)
                    else:
                        act.activation(pcT[0:n, h % 2, 128 * i:128 * i + 128], ps[0:n, 3 + v % 2, 0:128], ACT.Copy).then_inc(P_Te, 1)
            join(act, 5)
            for k in range(8):
                act.activation(hT_hi[:, k, :], mixA[:, k, :], ACT.Copy).then_inc(ms_hi, 1)
            for e in range(2 * NTT):
                t, k4 = e // 2, e % 2
                t0, n = TILES[t]
                act.wait_ge(xT_ready, 4 * NTT + e + 1)
                act.activation(hT_hi[:, 8 + 4 * k4:12 + 4 * k4, t0:t0 + n],
                               ps[:, e % 8, :].rearrange("p (k c) -> p k c", k=4)[:, :, 0:n], ACT.Copy).then_inc(hT_hi_done, 1)
            for c in range(4):
                for k in range(KT):
                    hi(U_OUT + KT * c + k)
                    if k == 1 and c:
                        out_tokens(act, c - 1)
            out_tokens(act, 3)
            join(act, 6)
            def squares(src, count):
                for t, (t0, n) in enumerate(TILES):
                    ch(act.activation(ps[0:n, 0:4, :].rearrange("p b c -> p (b c)"), src[0:n, t, :], ACT.Square, accum_out=small[0:n, t:t + 1]))
                act.drain().then_inc(ss_ready, 1)
                act.wait_ge(inv_ready, count)
                act.activation(rs, rs, ACT.Sqrt).then_inc(rs_ready, 1)

            squares(mo, 2)
            act.wait_ge(x2_ready, NTT)
            squares(xin, 3)
            join(act, 7)
            for g in range(4 * NTT):
                t, k4 = g // 4, g % 4
                t0, n = TILES[t]
                act.wait_ge(xT_ready, 6 * NTT + g + 1)
                act.activation(hT_hi[:, 4 * k4:4 * k4 + 4, t0:t0 + n],
                               ps[:, g % 8, :].rearrange("p (k c) -> p k c", k=4)[:, :, 0:n], ACT.Copy).then_inc(hT_hi_done, 1)
            join(act, 8)
            act.drain().then_inc(g_ready, 1)
            act.drain().then_inc(g_act, 1)
            with act.Fori(0, FT) as f:
                def hi_loop(j):
                    act.wait_ge(raw_loaded[(U_FFN + j) % 4], f * 32 + raw_count(U_FFN + j))
                    act.wait_ge(pe_unit, f * 8 + (U_FFN + j - 1))
                    act.activation(w_hi[:, j % 2, :], w_raw[:, (U_FFN + j) % 4, :], ACT.Copy).then_inc(hi_done, 1)

                for j in range(6):
                    hi_loop(j)
                act.wait_ge(pe_unit, f * 8 + (U_FFN + 4))
                act.activation(xr2[:, 2:2 + HALF], ps[:, 0, 0:HALF], ACT.Copy)
                act.activation(xr2[:, 2 + HALF:2 + NP], ps[:, 1, 0:NP - HALF], ACT.Copy)
                act.activation(xr2[:, 514:594].rearrange("p (s c) -> p s c", s=8)[:, :, 2:10],
                               ps[:, 1, NP - HALF:HALF].rearrange("p (s c) -> p s c", s=8), ACT.Copy).then_inc(g_ready, 1)
                hi_loop(6)
                hi_loop(7)
                act.wait_ge(g_sum, f + 1)
                act.wait_ge(up_done, f + 1)
                act.activation(gl[:, 0:NP], xc2[:, 0:NP], ACT.Gelu_apprx_tanh)
                act.activation(gl[:, NP:TOK].rearrange("p (s c) -> p s c", s=8),
                               xc2[:, 514:594].rearrange("p (s c) -> p s c", s=8)[:, :, 0:8], ACT.Gelu_apprx_tanh).then_inc(g_act, 1)
            join(act, 9)
            for c in range(4):
                peeled, turns = loop_units(c)
                for k in peeled:
                    down_hi(act, c, k, None)
                with act.Fori(0, turns) as i:
                    for j in range(4):
                        down_hi(act, c, 3 + j, i)
            join(act, 10)
            squares(yb, 4)
            join(act, 11)

        @block.vector
        def _(dve):
            ch = Chain(dve, v_ch)
            dve.memset(small[:], 0.0).then_inc(small_zero, 1)
            dve.wait_ge(ld_const, 16)
            dve.wait_ge(ld_g, 16)
            dve.wait_ge(ss_ready, 1)
            ch(dve.tensor_scalar(rs, ss, 1.0 / D, EPS, ALU.mult, ALU.add))
            dve.reciprocal(rs, rs).then_inc(inv_ready, 1)
            dve.wait_ge(rs_ready, 1)
            for t, (t0, n) in enumerate(TILES):
                dve.scalar_tensor_tensor(xin[0:n, t, :], xin[0:n, t, :], small[0:n, 5 + t:6 + t], gb[0:n, :], ALU.mult, ALU.mult).then_inc(xn_ready, 1)
            for g in range(4 * NTT):
                t, k4 = g // 4, g % 4
                t0, n = TILES[t]
                dve.wait_ge(hT_hi_done, g + 1)
                dve.tensor_tensor(hT_lo[:, 4 * k4:4 * k4 + 4, t0:t0 + n],
                                  ps[:, g % 8, :].rearrange("p (k c) -> p k c", k=4)[:, :, 0:n],
                                  hT_hi[:, 4 * k4:4 * k4 + 4, t0:t0 + n].bitcast(F32), ALU.subtract).then_inc(hT_lo_done, 1)
            dve.wait_ge(cw_ready, 1)
            ch(dve.tensor_copy(cwT[:], ps[:, 0, 0:XT * 29].rearrange("p (k c) -> p k c", k=XT)))
            join(dve, 0)
            ch(dve.memset(xr[:, 0:3], 0.0))
            for x in range(XT):
                if x:
                    dve.wait_ge(conv_done, x)
                xs3 = xr[:, 515:603].rearrange("p (s c) -> p s c", s=8)
                dve.tensor_copy(xs3[:, :, 0:3], cwT[:, x, 0:24].rearrange("p (s c) -> p s c", s=8))
                dve.wait_ge(xr_ready, x + 1)
                dve.tensor_copy(cst[:, x, 0:3], xr[:, 512:515])
                ch(dve.tensor_copy(cst[:, x, 3:27].rearrange("p (s c) -> p s c", s=8), xs3[:, :, 8:11]))
                ch(dve.tensor_scalar(xc[:, 0:600], xr[:, 0:600], cwT[:, x, 24:25], cwT[:, x, 28:29], ALU.mult, ALU.add))
                for k in range(1, 4):
                    i = dve.scalar_tensor_tensor(xc[:, 0:600], xr[:, k:600 + k], cwT[:, x, 24 + k:25 + k], xc[:, 0:600], ALU.mult, ALU.add)
                    if k < 3:
                        ch(i)
                    else:
                        i.then_inc(acc_ready, 1)
            dve.wait_ge(acc_ready, XT)
            dve.memset(gdt[64:128, 4, :], 0.0)
            join(dve, 1)
            dve.wait_ge(ld_ssd, 64)
            ch(dve.memset(ss2, 0.0))
            ch(dve.memset(sp_[:, 48:448], 0.0))
            ch(dve.tensor_tensor(v_, gdt[:, :, 48:64], dtb.unsqueeze(1).broadcast_to([128, NTT, NH]), ALU.add))
            ch(dve.tensor_scalar(w5, v_, -1.0, None, ALU.mult))
            dve.tensor_tensor(w5, v_, w5, ALU.min).then_inc(v_ready, 1)
            dve.wait_ge(v_ready, 2)
            dve.wait_ge(l_ready, 1)
            ch(dve.scalar_tensor_tensor(dt_, v_, 0.0, w5, ALU.max, ALU.add))
            dve.scalar_tensor_tensor(a_, dt_, -1.0, eA.unsqueeze(1).broadcast_to([128, NTT, NH]), ALU.mult, ALU.mult).then_inc(a_ready, 1)
            dve.wait_ge(sums_ready, 1)
            for rows, ts in ((128, slice(0, 4)), (64, slice(4, 5))):
                m = ts.stop - ts.start
                S = ps[0:rows, 7, 32 * ts.start:32 * ts.stop].rearrange("p (t x h) -> p t x h", t=m, x=2)
                dve.tensor_copy(acs[0:rows, ts], S[:, :, 0])
                ch(dve.tensor_copy(eac[0:rows, ts], S[:, :, 0]))
                dve.tensor_copy(eto[0:rows, ts], S[:, :, 1])
                ch(dve.tensor_tensor(ete[0:rows, ts], S[:, :, 1], eac[0:rows, ts], ALU.subtract))
            dve.drain().then_inc(sum_ready, 1)
            for p in range(8):
                dve.wait_ge(exps_ready, 1)
                dve.wait_ge(yoff_ready, p + 1)
                dve.tensor_tensor(yoff[:, 128 * p:128 * p + 128].rearrange("c (h p) -> c h p", h=2),
                                  ps[0:64, 6, 0:128].rearrange("c (h p) -> c h p", h=2),
                                  bc(eac[0:64, 4, 2 * p:2 * p + 2], [64, 2, 64]), ALU.mult).then_inc(yoff_evac, 1)
                dve.wait_ge(dec_ready, p + 1)
                dve.wait_ge(h0_loaded[p % 2], 16 * (p // 2 + 1))
                ch(dve.tensor_tensor(h0r[:, p % 2], h0r[:, p % 2], bc(dec[:, p % 2, :], [128, NB, 128]), ALU.mult))
                dve.wait_ge(newps_ready, p + 1)
                dve.tensor_tensor(h0r[:, p % 2].rearrange("p (a s) n -> p a (s n)", a=2),
                                  h0r[:, p % 2].rearrange("p (a s) n -> p a (s n)", a=2), ps[:, 4:6, :], ALU.add).then_inc(new_ready, 1)

            def seg_unit(w):
                t, g = w // 4, w % 4
                n = TILES[t][1]
                dve.wait_ge(s1_ready, w + 1)
                if w >= 2:
                    dve.wait_ge(y_ready, w - 1)
                mask = con[0:n, C_CB:C_CB + n] if t < 4 else con[0:n, C_CBS:C_CBS + n]
                for h in range(4):
                    i = dve.scalar_tensor_tensor(seg[0:n, w % 2, h, 0:n], ps[0:n, 2 + w % 2, 128 * h:128 * h + n],
                                                 acs[0:n, t, 4 * g + h:4 * g + h + 1], mask, ALU.subtract, ALU.add)
                i.then_inc(seg_ready, 1)

            def mix_unit(w):
                t, g = w // 4, w % 4
                n = TILES[t][1]
                dve.wait_ge(dec_exp, w + 1)
                dve.tensor_tensor(seg[0:n, w % 2, :, 0:n], seg[0:n, w % 2, :, 0:n],
                                  ps[0:n, w % 2, 0:n].unsqueeze(1).broadcast_to([n, 4, n]), ALU.mult).then_inc(M_done, 1)

            def out_unit(w):
                t, g = w // 4, w % 4
                n = TILES[t][1]
                dve.wait_ge(y_ready, w + 1)
                y = xsk[0:n, t, 256 * g:256 * g + 256]
                hv = lambda ap: ap.rearrange("c (h p) -> c h p", h=4)
                if 1 <= t <= 3:
                    dve.tensor_tensor(hv(tmp2[0:n, :]), hv(ps[0:n, 5, 0:256]), bc(eac[0:n, t, 4 * g:4 * g + 4], [n, 4, 64]), ALU.mult)
                ch(dve.tensor_tensor(hv(y), hv(y), bc(dsk[0:n, 4 * g:4 * g + 4], [n, 4, 64]), ALU.mult))
                ch(dve.tensor_tensor(y, y, ps[0:n, 4, 0:256], ALU.add))
                if t >= 1:
                    ch(dve.tensor_tensor(y, y, tmp2[0:n, :] if t < 4 else yoff[:, 256 * g:256 * g + 256], ALU.add))
                H = hst[:, 256 * g:256 * g + 256]
                if t == 0:
                    dve.tensor_copy(H, ps[:, 6, 0:256])
                elif t < 4:
                    ch(dve.tensor_tensor(hv(H), hv(H), bc(eto[:, t, 4 * g:4 * g + 4], [128, 4, 64]), ALU.mult))
                    dve.tensor_tensor(H, H, ps[:, 6, 0:256], ALU.add)
                z = zs[0:n, t, 256 * g:256 * g + 256]
                ch(dve.tensor_tensor(z, y, z, ALU.mult))
                dve.drain().then_inc(unit_done, 1)

            for w in range(21):
                if w < 20:
                    seg_unit(w)
                if w >= 1:
                    out_unit(w - 1)
                if w < 20:
                    mix_unit(w)
            dve.wait_ge(fin_T, 1)
            for b in range(2):
                dve.wait_ge(h0_stored[b], 64)
            dve.tensor_copy(cso[:].rearrange("p (b c) -> p b c", b=4), ps[0:27, 0:4, :]).then_inc(fin_copied, 1)
            dve.tensor_copy(hso[:].rearrange("p (a s) n -> p a (s n)", a=2), ps[:, 4:6, :]).then_inc(fin_copied, 1)
            dve.wait_ge(ss2_ready, 20)
            ch(dve.tensor_scalar(ss2, ss2, 1.0 / 256, EPS, ALU.mult, ALU.add))
            dve.reciprocal(ss2, ss2).then_inc(inv2, 1)
            dve.wait_ge(rs2, 1)
            for t, (t0, n) in enumerate(TILES):
                for g in range(4):
                    z = zs[0:n, t, 256 * g:256 * g + 256]
                    dve.scalar_tensor_tensor(z, z, sp_[0:n, 448 + 4 * t + g:449 + 4 * t + g], ngb[0:n, 256 * g:256 * g + 256], ALU.mult, ALU.mult)
            join(dve, 2)
            dve.memset(cs[32:33, 360:376], 1.0).then_inc(tab_set, 1)
            dve.wait_ge(ld_c, 16 * 10)
            dve.wait_ge(pb_mm, 1)
            dve.tensor_tensor(hb, ps[:, 7, 0:2], b1t, ALU.add).then_inc(hb_ready, 1)
            for c, (s0, ns) in enumerate(CH):
                dve.wait_ge(vc_ready, c + 1)
                dve.tensor_tensor(vc[:, s0:s0 + ns].rearrange("n s (g d) -> n (s g) d", g=4),
                                  ps[0:NCMP, 5:7, :].rearrange("n a (s d) -> n (a s) d", d=64)[:, 0:4 * ns],
                                  b2v.unsqueeze(1).broadcast_to([NCMP, 4 * ns, 64]), ALU.add).then_inc(vc_evac, 1)
            join(dve, 3)
            dve.memset(nb[:], NEG).then_inc(nb_set, 1)
            for gp in range(2):
                for r in range(4):
                    i = dve.tensor_copy(qs[:, gp, :, 8 * r:8 * r + 8], qT[:, 4 * gp + r, NP:TOK].rearrange("p (s t) -> p s t", s=NB))
            i.then_inc(qs_ready, 1)
            dve.wait_ge(ld_b, 16 * 2 * NH)
            ch(dve.tensor_copy(sb_[:, 1, :], sb_[:, 0, :]))
            ch(dve.tensor_tensor(sb_[:, 1, 0:8], sb_[:, 1, 0:8], con[:, C_WM:C_WM + 8], ALU.add))
            dve.wait_ge(sc_mm, 1)
            sx = ps[:, 3, 0:NB * NCMP].rearrange("p (s n) -> p s n", s=NB)
            ch(dve.tensor_tensor(scc[:], sx, sb_[:, 0, 31:512:16].unsqueeze(1).broadcast_to([128, NB, NCMP]), ALU.add))
            ch(dve.tensor_reduce(m8, scc[:], AX.X, ALU.max))
            dve.tensor_tensor(scc[:], scc[:], bc(m8, [128, NB, NCMP]), ALU.subtract).then_inc(pc_sub, 1)
            dve.wait_ge(pc_exp, 1)
            ch(dve.tensor_reduce(r8, scc[:], AX.X, ALU.add))
            ch(dve.tensor_scalar(r8, r8, TINY, None, ALU.max))
            ch(dve.reciprocal(r8, r8))
            dve.tensor_tensor(scc[:], scc[:], bc(r8, [128, NB, NCMP]), ALU.mult).then_inc(pc_ready, 1)
            dve.wait_ge(pc_ready, 1)
            dve.wait_ge(ld_gs, 16)
            dve.tensor_tensor(scg[:], scc[:], gsm[:, :, 0:1].broadcast_to([128, NB, NCMP]), ALU.mult).then_inc(pcg_ready, 1)
            dve.wait_ge(imp_mm, 1)
            dve.tensor_copy(imp.rearrange("p s b -> p (s b)"), ps[:, 2, 0:72]).then_inc(imp_ready, 1)
            dve.wait_ge(imp2_mm, 1)
            ch(dve.tensor_copy(d1, ps[:, 3, 0:72].rearrange("p (s b) -> p s b", s=NB)[:, :, 1:7]))
            ch(dve.tensor_reduce(m8, d1, AX.X, ALU.min))
            ch(dve.tensor_tensor(d1, d1, bc(m8, [128, NB, 6]), ALU.is_equal))
            iota = con[:, C_IOTA:C_IOTA + 6].unsqueeze(1).broadcast_to([128, NB, 6])
            ch(dve.tensor_tensor(d1, d1, iota, ALU.mult))
            ch(dve.tensor_reduce(m8, d1, AX.X, ALU.max))
            ch(dve.tensor_tensor(d1, bc(m8, [128, NB, 6]), iota, ALU.is_equal))
            ch(dve.tensor_scalar(drop, d1, NEG, None, ALU.mult))
            dve.drain().then_inc(drop_ready, 1)

            def s_first(y):
                s, br = y // 2, y % 2
                S = scs[:, y % 2, :]
                dve.wait_ge(s_mm, y + 1)
                if y >= 2:
                    dve.wait_ge(pT_mm, y - 1)
                dve.tensor_tensor(S[:, 0:512], ps[:, 2 * (y % 2), :], sb_[:, br, :], ALU.add)
                ch(dve.tensor_tensor(S[:, 512:576], ps[:, 1, 0:64], nb[:, 56 - 8 * s:120 - 8 * s], ALU.add))
                if br == 0:
                    v = S[:, 64:448].rearrange("p (b k) -> p b k", b=6)
                    ch(dve.tensor_tensor(v, v, bc(drop[:, s, :], [128, 6, 64]), ALU.add))
                ch(dve.tensor_reduce(st_[:, y % 2, 2:3], S, AX.X, ALU.max))
                dve.tensor_scalar(st_[:, y % 2, 0:1], st_[:, y % 2, 2:3], CLAMP, -1.0, ALU.max, ALU.mult).then_inc(s_max, 1)

            def s_second(y):
                s, br = y // 2, y % 2
                dve.wait_ge(s_exp, y + 1)
                ch(dve.tensor_scalar(st_[:, y % 2, 3:4], st_[:, y % 2, 1:2], TINY, None, ALU.max))
                ch(dve.reciprocal(st_[:, y % 2, 3:4], st_[:, y % 2, 3:4]))
                dve.tensor_scalar(scs[:, y % 2, :], scs[:, y % 2, :], st_[:, y % 2, 3:4], gsm[:, s, 1 + br:2 + br], ALU.mult, ALU.mult).then_inc(s_p, 1)

            def s_out(s):
                dve.wait_ge(pv_mm, 2 * s + 2)
                if s >= 2:
                    dve.wait_ge(oT_mm, s - 1)
                for g in range(NG):
                    i = dve.tensor_copy(osb[32 * g:32 * g + 32, s % 2, :], ps[32 * g:32 * g + 32, 3, 64 * g:64 * g + 64])
                i.then_inc(o_ready, 1)
                dve.wait_ge(oT_mm, s + 1)
                for par in range(2):
                    i = dve.tensor_copy(mixA[64 * par:64 * par + 64, :, NP + 8 * s:NP + 8 * s + 8],
                                        ps[0:64, 3, 256:384].rearrange("d (h q t) -> d h q t", q=2, t=8)[:, :, par, :])
                i.then_inc(oT_evac, 1)

            for y in range(18):
                if y < 16:
                    s_first(y)
                if 1 <= y < 17:
                    s_second(y - 1)
                if y >= 3 and y % 2 == 1:
                    s_out((y - 3) // 2)
            join(dve, 4)
            dve.wait_ge(ld_TT, 16)
            for w in range(NU + 2):
                if w < NU:
                    h, i, br, n = pu(w)
                    k = 4 * (w % 3)
                    dve.wait_ge(P_mm, w + 1)
                    if w >= 3:
                        dve.wait_ge(P_T, w - 2)
                    y0 = 384 - 128 * i if br < 2 else 415 - 128 * i
                    bias = TT[:, h, y0:y0 + n] if br < 2 else TT[:, h, y0:y0 + 16 * (n - 1) + 1:16]
                    dve.tensor_tensor(scp[:, w % 3, 0:n], ps[:, w % 3, 0:n], bias, ALU.add).then_inc(P_add, 1)
                if 1 <= w <= NU:
                    v = w - 1
                    k1 = 4 * (v % 3)
                    dve.wait_ge(P_exp, v + 1)
                    ch(dve.tensor_scalar(ast[:, k1 + 3:k1 + 4], ast[:, k1 + 1:k1 + 2], TINY, None, ALU.max))
                if w < NU:
                    dve.wait_ge(P_add, w + 1)
                    ch(dve.tensor_reduce(ast[:, k + 2:k + 3], scp[:, w % 3, 0:n], AX.X, ALU.max))
                    dve.tensor_scalar(ast[:, k:k + 1], ast[:, k + 2:k + 3], CLAMP, -1.0, ALU.max, ALU.mult).then_inc(P_max, 1)
                if 1 <= w <= NU:
                    h1, i1, br1, n1 = pu(v)
                    gb1 = 16 * (br1 + 1 if br1 < 2 else 0) + h1
                    ch(dve.reciprocal(ast[:, k1 + 3:k1 + 4], ast[:, k1 + 3:k1 + 4]))
                    dve.tensor_scalar(scp[:, v % 3, 0:n1], scp[:, v % 3, 0:n1], ast[:, k1 + 3:k1 + 4], gdt[:, i1, gb1:gb1 + 1], ALU.mult, ALU.mult).then_inc(P_p, 1)
                if w >= 6 and (w - 6) % 12 == 11:
                    prompt_out(dve, (w - 6) // 12)
            prompt_out(dve, NH - 1)
            join(dve, 5)
            for k in range(8):
                dve.wait_ge(ms_hi, k + 1)
                dve.tensor_tensor(hT_lo[:, k, :], mixA[:, k, :], hT_hi[:, k, :].bitcast(F32), ALU.subtract).then_inc(ms_lo, 1)
            for e in range(2 * NTT):
                t, k4 = e // 2, e % 2
                t0, n = TILES[t]
                dve.wait_ge(hT_hi_done, 4 * NTT + e + 1)
                dve.tensor_tensor(hT_lo[:, 8 + 4 * k4:12 + 4 * k4, t0:t0 + n], ps[:, e % 8, :].rearrange("p (k c) -> p k c", k=4)[:, :, 0:n],
                                  hT_hi[:, 8 + 4 * k4:12 + 4 * k4, t0:t0 + n].bitcast(F32), ALU.subtract).then_inc(hT_lo_done, 1)
            join(dve, 6)
            def inverse(count):
                dve.wait_ge(ss_ready, count)
                ch(dve.tensor_scalar(rs, ss, 1.0 / D, EPS, ALU.mult, ALU.add))
                dve.reciprocal(rs, rs).then_inc(inv_ready, 1)
                dve.wait_ge(rs_ready, count)

            inverse(2)
            dve.wait_ge(ld_g, 48)
            dve.wait_ge(ld_x, 32 * NTT)
            for t, (t0, n) in enumerate(TILES):
                ch(dve.scalar_tensor_tensor(mo[0:n, t, :], mo[0:n, t, :], small[0:n, 5 + t:6 + t], gb[0:n, :], ALU.mult, ALU.mult))
                dve.tensor_tensor(xin[0:n, t, :], xin[0:n, t, :], mo[0:n, t, :], ALU.add).then_inc(x2_ready, 1)
            inverse(3)
            for t, (t0, n) in enumerate(TILES):
                dve.scalar_tensor_tensor(mo[0:n, t, :], xin[0:n, t, :], small[0:n, 5 + t:6 + t], gb2[0:n, :], ALU.mult, ALU.mult)
            join(dve, 7)
            for g in range(4 * NTT):
                t, k4 = g // 4, g % 4
                t0, n = TILES[t]
                dve.wait_ge(hT_hi_done, 6 * NTT + g + 1)
                dve.tensor_tensor(hT_lo[:, 4 * k4:4 * k4 + 4, t0:t0 + n],
                                  ps[:, g % 8, :].rearrange("p (k c) -> p k c", k=4)[:, :, 0:n],
                                  hT_hi[:, 4 * k4:4 * k4 + 4, t0:t0 + n].bitcast(F32), ALU.subtract).then_inc(hT_lo_done, 1)
            dve.wait_ge(fw_T, 1)
            dve.tensor_copy(fwT[:, 0:25, :], ps[:, 0, 0:500].rearrange("p (k c) -> p k c", k=25))
            dve.tensor_copy(fwT[:, 25:FT, :], ps[:, 1, 0:20 * (FT - 25)].rearrange("p (k c) -> p k c", k=FT - 25))
            dve.memset(xr2[:, 0:2], 0.0)
            join(dve, 8)
            dve.drain().then_inc(up_done, 1)
            with dve.Fori(0, FT) as f:
                P = lambda m: fwT[:, bass.ds(f, 1), m:m + 1].rearrange("p a c -> p (a c)")
                x3 = xr2[:, 514:594].rearrange("p (s c) -> p s c", s=8)
                dve.tensor_copy(x3[:, :, 0:2], fwT[:, bass.ds(f, 1), 0:16].rearrange("p a (s c) -> p (a s) c", s=8))
                dve.wait_ge(g_ready, f + 2)
                dve.wait_ge(g_act, f + 1)
                dve.tensor_copy(fst[:, bass.ds(f, 1), 0:2].rearrange("p a c -> p (a c)"), xr2[:, 512:514])
                dve.tensor_copy(fst[:, bass.ds(f, 1), 2:18].rearrange("p a (s c) -> p (a s) c", s=8), x3[:, :, 8:10]).then_inc(f_ch, 1)
                dve.wait_ge(f_ch, f * 3 + 1)
                dve.tensor_scalar(xc2[:, 0:592], xr2[:, 0:592], P(16), P(19), ALU.mult, ALU.add).then_inc(f_ch, 1)
                dve.wait_ge(f_ch, f * 3 + 2)
                dve.scalar_tensor_tensor(xc2[:, 0:592], xr2[:, 1:593], P(17), xc2[:, 0:592], ALU.mult, ALU.add).then_inc(f_ch, 1)
                dve.wait_ge(f_ch, f * 3 + 3)
                dve.scalar_tensor_tensor(xc2[:, 0:592], xr2[:, 2:594], P(18), xc2[:, 0:592], ALU.mult, ALU.add).then_inc(g_sum, 1)
                dve.wait_ge(g_act, f + 2)
                dve.wait_ge(pe_unit, f * 8 + (U_FFN + 8))
                dve.tensor_tensor(acT[:, bass.ds(f, 1), :].rearrange("p a (h c) -> p (a h) c", h=2), gl[:].rearrange("p (h c) -> p h c", h=2),
                                  ps[:, 2:4, 0:HALF], ALU.mult).then_inc(up_done, 1)
            join(dve, 9)
            for c in range(5):
                if c < 4:
                    peeled, turns = loop_units(c)
                    down_lo(dve, c, 0, None)
                    down_lo(dve, c, 1, None)
                if c:
                    dve.wait_ge(pe_unit, U_DOWN + FT * c)
                    for t, (t0, n) in enumerate(TILES):
                        dve.tensor_copy(yb[0:n, t, 512 * (c - 1):512 * c], ps[0:n, t, :]).then_inc(y_evac, 1)
                if c < 4:
                    down_lo(dve, c, 2, None)
                    with dve.Fori(0, turns) as i:
                        for j in range(4):
                            down_lo(dve, c, 3 + j, i)
            join(dve, 10)
            inverse(4)
            dve.wait_ge(ld_x, 16 * (3 * NTT + 1))
            for t, (t0, n) in enumerate(TILES):
                ch(dve.scalar_tensor_tensor(yb[0:n, t, :], yb[0:n, t, :], small[0:n, 5 + t:6 + t], gb3[0:n, :], ALU.mult, ALU.mult))
                dve.tensor_tensor(yb[0:n, t, :], yb[0:n, t, :], x2r[0:n, t, :], ALU.add).then_inc(fin_y, 1)
            for b in range(3):
                m = min(16, FT - 16 * b) * 128
                dve.wait_ge(fco_T, b + 1)
                dve.tensor_copy(fco[:, 2048 * b:2048 * b + m], ps[0:18, 4:8, :].rearrange("p b c -> p (b c)")[:, 0:m]).then_inc(fco_done, 1)
            join(dve, 11)

        @block.gpsimd
        def _(pool):
            join(pool, 0)
            with pool.Fori(0, U_GD // 4) as i:
                for j in range(4):
                    pool.wait_ge(hi_done, i * 4 + (j + 1))
                    pool.tensor_tensor(w_lo[:, j % 2, :], w_raw[:, j, :], w_hi[:, j % 2, :].bitcast(F32), ALU.subtract).then_inc(lo_done, 1)
            for u in range(U_GD, U_GD + 2):
                pool.wait_ge(hi_done, u + 1)
                pool.tensor_tensor(w_lo[:, u % 2, :], w_raw[:, u % 4, :], w_hi[:, u % 2, :].bitcast(F32), ALU.subtract).then_inc(lo_done, 1)
            join(pool, 1)
            def x_scaled(k, t, n, sl, both):
                if k >= 2:
                    t_old = [4, 0, 1, 2, 3, 4][k - 2]
                    pool.wait_ge(y_ready, 4 * (t_old + 1)) if k > 2 else pool.wait_ge(newps_ready, 8)
                xh = lambda ap: ap.rearrange("c (h p) -> c h p", h=NH)
                pool.tensor_tensor(xh(xdt[0:n, sl, :]), xh(xsk[0:n, t, :]), bc(dt_[0:n, t, :], [n, NH, 64]), ALU.mult).then_inc(pool_ch, 1)
                pool.wait_ge(pool_ch, k + 1)
                pool.tensor_tensor(xh(xte[0:n, sl, :]), xh(xdt[0:n, sl, :]), bc(ete[0:n, t, :], [n, NH, 64]), ALU.mult).then_inc(xt_ready, 1)

            pool.wait_ge(tokT_evac, 15)
            pool.wait_ge(exps_ready, 1)
            x_scaled(0, 4, 64, 0, True)
            x_scaled(1, 0, 128, 1, True)
            for g in range(NG):
                if g:
                    pool.wait_ge(newps_ready, 2 * g)
                pool.tensor_tensor(bex[:], Bk[0:64, 4, 128 * g:128 * g + 128].unsqueeze(1).broadcast_to([64, NB, 128]),
                                   bc(con[0:64, C_SEQ:C_SEQ + 8], [64, NB, 128]), ALU.mult).then_inc(bexp_ready, 1)
            for t in range(1, 5):
                x_scaled(t + 1, t, TILES[t][1], (t + 1) % 2, True)
            join(pool, 2)
            join(pool, 3)
            join(pool, 4)
            join(pool, 5)

            def lo_loop(u0, turns):
                with pool.Fori(0, turns) as i:
                    for j in range(4):
                        u = u0 + j
                        pool.wait_ge(hi_done, i * 4 + (u + 1))
                        pool.tensor_tensor(w_lo[:, u % 2, :], w_raw[:, u % 4, :], w_hi[:, u % 2, :].bitcast(F32), ALU.subtract).then_inc(lo_done, 1)

            lo_loop(U_OUT, KT)
            join(pool, 6)
            join(pool, 7)
            join(pool, 8)
            lo_loop(U_FFN, 2 * FT)
            join(pool, 9)
            lo_loop(U_DOWN, FT)
            join(pool, 10)
            join(pool, 11)

        @block.tensor
        def _(pe):
            pe.wait_ge(ld_const, 16)
            for g in range(4 * NTT):
                t, k4 = g // 4, g % 4
                t0, n = TILES[t]
                if k4 == 0:
                    pe.wait_ge(xn_ready, t + 1)
                if g >= 8:
                    pe.wait_ge(hT_lo_done, g - 7)
                for k in range(4):
                    i = pe.transpose(ps[:, g % 8, 128 * k:128 * k + n], xin[0:n, t, 128 * (4 * k4 + k):128 * (4 * k4 + k) + 128], ident[0:n, 0:n])
                i.then_inc(xT_ready, 1)
            pe.wait_ge(ld_cw, 48)
            pe.wait_ge(hT_lo_done, 4 * NTT)
            for k in range(XT):
                i = pe.transpose(ps[:, 0, 29 * k:29 * k + 29], cwst[0:29, 128 * k:128 * k + 128], ident[0:29, 0:29])
            i.then_inc(cw_ready, 1)
            join(pe, 0)

            def feat_tile(f, bank, u0, base, first_wait):
                for j in range(4):
                    pe.wait_ge(lo_done, u0 + (j + 1))
                    for kk in range(4):
                        k = 4 * j + kk
                        s = (base + j) % 2
                        for h in range(2):
                            o = ps[:, bank + h, 0:HALF]
                            W = [w_hi[:, s, 128 * kk:128 * kk + 128], w_lo[:, s, 128 * kk:128 * kk + 128]]
                            X = [hT_hi[:, k, HALF * h:HALF * h + HALF], hT_lo[:, k, HALF * h:HALF * h + HALF]]
                            pe.matmul(o, W[0], X[0], start=(k == 0), stop=False)
                            pe.matmul(o, W[0], X[1], start=False, stop=False)
                            i = pe.matmul(o, W[1], X[0], start=False, stop=(k == KT - 1))
                    i.then_inc(pe_unit, 1)

            for f in range(2):
                feat_tile(f, 2 * f, 4 * f, 0, None)
            with pe.Fori(1, 12) as i:
                for f in range(2):
                    pe.wait_ge(feat_evac, i * 2 + (f - 1))
                    feat_tile(f, 2 * f, i * 8 + 4 * f, 0, None)
            pe.wait_ge(feat_evac, 24)

            def token_unit(u, k, first, last_):
                pe.wait_ge(lo_done, u + 1)
                for t, (t0, n) in enumerate(TILES):
                    o = ps[0:n, t, :]
                    X = [hT_hi[:, k, t0:t0 + n], hT_lo[:, k, t0:t0 + n]]
                    W = [w_hi[:, u % 2, :], w_lo[:, u % 2, :]]
                    if first is not None and k == 0 and first > 0:
                        pe.wait_ge(tok_evac, 5 * (first - 1) + t + 1)
                    pe.matmul(o, X[0], W[0], start=(k == 0), stop=False)
                    pe.matmul(o, X[1], W[0], start=False, stop=False)
                    i = pe.matmul(o, X[0], W[1], start=False, stop=last_)
                i.then_inc(pe_unit, 1)

            for c in range(5):
                for k in range(KT):
                    token_unit(U_KV + KT * c + k, k, c, k == KT - 1)
            pe.wait_ge(lo_done, U_GD + 2)
            for t, (t0, n) in enumerate(TILES):
                o = ps[0:n, 5, 64 * t:64 * t + 64]
                for k in range(KT):
                    s, kk = (U_GD + k // 8) % 2, k % 8
                    X = [hT_hi[:, k, t0:t0 + n], hT_lo[:, k, t0:t0 + n]]
                    W = [w_hi[:, s, 64 * kk:64 * kk + 64], w_lo[:, s, 64 * kk:64 * kk + 64]]
                    pe.matmul(o, X[0], W[0], start=(k == 0), stop=False)
                    pe.matmul(o, X[1], W[0], start=False, stop=False)
                    i = pe.matmul(o, X[0], W[1], start=False, stop=(k == KT - 1))
            i.then_inc(pe_unit, 2)
            join(pe, 1)
            for G in range(3 * NTT):
                t, b = G // 3, G % 3
                t0, n = TILES[t]
                if G >= 6:
                    pe.wait_ge(tokT_evac, G - 5)
                for k in range(4):
                    i = pe.transpose(ps[0:n, G % 6, 128 * k:128 * k + 128], xbcT[:, 4 * b + k, t0:t0 + n], ident)
                i.then_inc(tokT_ready, 1)
            pe.wait_ge(a_ready, 1)
            for t, (t0, n) in enumerate(TILES):
                tri = con[0:n, C_TRI:C_TRI + n] if t < 4 else con[0:n, C_TRIS:C_TRIS + n]
                one = con[0:n, C_ONE:C_ONE + n] if t < 4 else con[0:n, C_BLK:C_BLK + n]
                pe.matmul(ps[0:n, 7, 32 * t:32 * t + 16], tri, a_[0:n, t, :], start=True, stop=True)
                i = pe.matmul(ps[0:n, 7, 32 * t + 16:32 * t + 32], one, a_[0:n, t, :], start=True, stop=True)
            i.then_inc(sums_ready, 1)
            pe.wait_ge(tokT_evac, 15)
            for p in range(8):
                g = p // 2
                pe.wait_ge(h0_loaded[p % 2], 16 * (p // 2 + 1))
                if p:
                    pe.wait_ge(h0T_evac, p)
                for s in range(NB):
                    i = pe.transpose(ps[:, s // 4, 128 * (s % 4):128 * (s % 4) + 128], h0r[:, p % 2, s, :], ident)
                i.then_inc(h0T_ready, 1)
                pe.wait_ge(h0T_evac, p + 1)
                if p:
                    pe.wait_ge(dec_ready, p)
                for s in range(NB):
                    pe.matmul(ps[:, 2, 8 * s:8 * s + 8], h0T[:, s, :], xbcT[:, 12 + g, NP + 8 * s:NP + 8 * s + 8], start=True, stop=True)
                for h in range(2):
                    i = pe.matmul(ps[64 * h:64 * h + 64, 3, 0:8], a_[0:64, 4, 2 * p + h:2 * p + h + 1].broadcast_to([64, 64]),
                                  con[0:64, C_SEQ:C_SEQ + 8], start=True, stop=True)
                i.then_inc(yo_ready, 1)
                pe.wait_ge(yoT_evac, p + 1)
                if p:
                    pe.wait_ge(yoff_evac, p)
                pe.transpose(ps[0:64, 6, 0:128], yoT[:], ident).then_inc(yoff_ready, 1)
                pe.wait_ge(bexp_ready, g + 1)
                pe.wait_ge(xt_ready, 1)
                if p:
                    pe.wait_ge(new_ready, p)
                for hf in range(2):
                    i = pe.matmul(ps[:, 4 + hf, :], xte[0:64, 0, 128 * p:128 * p + 128],
                                  bex[:, 4 * hf:4 * hf + 4, :].rearrange("j s n -> j (s n)"), start=True, stop=True)
                i.then_inc(newps_ready, 1)
            pe.wait_ge(new_ready, 8)
            pe.wait_ge(yoff_evac, 8)

            def ssd_scores(w):
                t, g = w // 4, w % 4
                t0, n = TILES[t]
                tri = con[0:n, C_TRI:C_TRI + n] if t < 4 else con[0:n, C_TRIS:C_TRIS + n]
                if w >= 2:
                    pe.wait_ge(M_done, w - 1)
                pe.matmul(ps[0:n, w % 2, 0:n], xbcT[:, 8 + g, t0:t0 + n], xbcT[:, 12 + g, t0:t0 + n], start=True, stop=True)
                for h in range(4):
                    i = pe.matmul(ps[0:n, 2 + w % 2, 128 * h:128 * h + n], a_[0:n, t, 4 * g + h:4 * g + h + 1].broadcast_to([n, n]), tri, start=True, stop=True)
                i.then_inc(s1_ready, 1)

            def ssd_out(w):
                t, g = w // 4, w % 4
                t0, n = TILES[t]
                sl = (t + 1) % 2
                pe.wait_ge(M_done, w + 1)
                pe.wait_ge(xt_ready, t + 2)
                if w:
                    pe.wait_ge(unit_done, w)
                for h in range(4):
                    i = pe.matmul(ps[0:n, 4, 64 * h:64 * h + 64], seg[0:n, w % 2, h, 0:n],
                                  xdt[0:n, sl, 256 * g + 64 * h:256 * g + 64 * h + 64], start=True, stop=True)
                if 1 <= t <= 3:
                    i = pe.matmul(ps[0:n, 5, 0:256], xbcT[:, 12 + g, t0:t0 + n], hst[:, 256 * g:256 * g + 256], start=True, stop=True)
                if t <= 3:
                    i = pe.matmul(ps[:, 6, 0:256], Bk[0:n, t, 128 * g:128 * g + 128], xte[0:n, sl, 256 * g:256 * g + 256], start=True, stop=True)
                i.then_inc(y_ready, 1)

            ssd_scores(0)
            for w in range(20):
                if w + 1 < 20:
                    ssd_scores(w + 1)
                ssd_out(w)
            pe.wait_ge(unit_done, 20)
            for k in range(XT):
                pe.transpose(ps[0:27, k // 4, 128 * (k % 4):128 * (k % 4) + 128], cst[:, k, :], ident)
            for k in range(8):
                i = pe.transpose(ps[:, 4 + k // 4, 128 * (k % 4):128 * (k % 4) + 128], hst[:, 128 * k:128 * k + 128], ident)
            i.then_inc(fin_T, 1)
            join(pe, 2)
            pe.wait_ge(ld_c, 16 * 10)
            pe.wait_ge(tab_set, 1)
            pe.matmul(ps[0:NH, 0, :], tab, oh[:, 0:512], start=True, stop=True)
            pe.matmul(ps[0:NH, 1, 0:BL - 512], tab, oh[:, 512:BL], start=True, stop=True).then_inc(rb_mm, 1)
            pe.transpose(ps[:, 2, 0:32], pes, ident[0:32, 0:32]).then_inc(pe_T, 1)
            pe.wait_ge(peT_ready, 1)
            for a in range(2):
                for k in range(16):
                    i = pe.matmul(ps[:, 7, a:a + 1], w1p[:, a, k, :], peT[:, 16 * a + k:16 * a + k + 1], start=(k == 0), stop=(k == 15))
            i.then_inc(pb_mm, 1)
            pe.wait_ge(rb_ready, 1)
            e = 0
            for c, (s0, ns) in enumerate(CH):
                for s in range(ns):
                    pe.wait_ge(craw_loaded[(s0 + s) % 2], 128 * ((s0 + s) // 2 + 1))
                    for b in range(4):
                        if e >= 2:
                            pe.wait_ge(pairT_evac, e - 1)
                        for g in range(4):
                            i = pe.transpose(ps[:, e % 2, 128 * g:128 * g + 128],
                                             craw[:, (s0 + s) % 2, b // 2, b % 2, g].rearrange("i q d -> i (q d)"), ident)
                        i.then_inc(pairT_ready, 1)
                        e += 1
                pe.wait_ge(pairT_evac, e)
                for a in range(2):
                    if c:
                        pe.wait_ge(gelu_done, 2 * c)
                    for k in range(16):
                        i = pe.matmul(ps[:, 2 + a, 0:124 * ns], w1p[:, a, k, :],
                                      kvp[:, a, 0:ns, :, k:k + 241:8].rearrange("p s g n -> p (s g) n"), start=(k == 0), stop=(k == 15))
                    i.then_inc(hid_ready, 1)
                pe.wait_ge(gelu_done, 2 * c + 1)
                if c:
                    pe.wait_ge(kc_evac, c)
                for hf in range(2):
                    i = pe.matmul(ps[64 * hf:64 * hf + 64, 4, 0:62 * ns], w2t[:, 0, :],
                                  gact[:, 0:124 * ns].rearrange("p (s g q n) -> p (s g) q n", s=ns, g=2, q=2)[:, :, hf, :], start=True, stop=True)
                i.then_inc(kc_ready, 1)
                pe.wait_ge(gelu_done, 2 * c + 2)
                if c:
                    pe.wait_ge(vc_evac, c)
                for x in range(4 * ns):
                    i = pe.matmul(ps[0:NCMP, 5 + x // 8, 64 * (x % 8):64 * (x % 8) + 64], gact[:, NCMP * x:NCMP * x + NCMP], w2t[:, 1, :], start=True, stop=True)
                i.then_inc(vc_ready, 1)
            join(pe, 3)
            for br in range(2):
                for gp in range(2):
                    col = 512 * (br + 1) + 128 * gp
                    i = pe.transpose(ps[:, 0, 64 * (2 * br + gp):64 * (2 * br + gp) + 64], kvt[0:64, 4, col:col + 128], ident[0:64, 0:64])
            i.then_inc(kn_mm, 1)
            pe.wait_ge(qs_ready, 1)
            for s in range(NB):
                for g in range(NG):
                    q = 64 * (g % 2)
                    i = pe.matmul(ps[32 * g:32 * g + 32, 3, NCMP * s:NCMP * s + NCMP], qs[q:q + 64, g // 2, s, :], kcT[q:q + 64, s, g // 2, :],
                                  start=True, stop=True)
            i.then_inc(sc_mm, 1)
            pe.wait_ge(kn_ready, 1)
            pe.wait_ge(pc_ready, 1)
            for s in range(NB):
                i = pe.transpose(ps[0:NCMP, s // 4, 128 * (s % 4):128 * (s % 4) + 128], scc[:, s, :], ident)
            i.then_inc(pcT_mm, 1)
            pe.wait_ge(pcg_ready, 1)
            for s in range(NB):
                i = pe.transpose(ps[0:NCMP, 4 + s // 4, 128 * (s % 4):128 * (s % 4) + 128], scg[:, s, :], ident)
            i.then_inc(pcT_mm, 1)
            pe.wait_ge(pcT_evac, 1)
            for s in range(NB):
                i = pe.matmul(ps[:, 2, 9 * s:9 * s + 9], pc0[:, s, :], con[0:NCMP, C_OV:C_OV + 9], start=True, stop=True)
            i.then_inc(imp_mm, 1)
            pe.wait_ge(imp_ready, 1)
            pe.matmul(ps[:, 3, 0:72], con[:, C_SAME:C_SAME + 128], imp.rearrange("p s b -> p (s b)"), start=True, stop=True).then_inc(imp2_mm, 1)
            pe.wait_ge(pcT_evac, 2)

            def s_kt(y):
                pe.wait_ge(a_loaded[y % 3], 64 * (y // 3 + 1))
                for gp in range(2):
                    if y:
                        pe.wait_ge(KT_evac, 2 * y - 1 + gp)
                    for k in range(4):
                        i = pe.transpose(ps[:, 4 + gp, 128 * k:128 * k + 128], araw[:, y % 3, k, 128 * gp:128 * gp + 128], ident)
                    i.then_inc(KT_mm, 1)

            def s_scores(y):
                s, br = y // 2, y % 2
                pe.wait_ge(KT_evac, 2 * y + 2)
                if y >= 2:
                    pe.wait_ge(s_max, y - 1)
                else:
                    pe.wait_ge(drop_ready, 1)
                for g in range(NG):
                    q = 64 * (g % 2)
                    pe.matmul(ps[32 * g:32 * g + 32, 2 * (y % 2), :], qs[q:q + 64, g // 2, s, :], KTs[q:q + 64, y % 2, g // 2, :], start=True, stop=True)
                if y:
                    pe.wait_ge(s_max, y)
                for g in range(NG):
                    q = 64 * (g % 2)
                    i = pe.matmul(ps[32 * g:32 * g + 32, 1, 0:64], qs[q:q + 64, g // 2, s, :], knT[q:q + 64, br, g // 2, :], start=True, stop=True)
                i.then_inc(s_mm, 1)

            def s_pt(y):
                pe.wait_ge(s_p, y + 1)
                if y:
                    pe.wait_ge(pT_evac, y)
                for k in range(4):
                    pe.transpose(ps[:, 6, 128 * k:128 * k + 128], scs[:, y % 2, 128 * k:128 * k + 128], ident)
                pe.transpose(ps[0:64, 7, 0:128], scs[:, y % 2, 512:576], ident).then_inc(pT_mm, 1)

            def s_pv(y):
                s, br = y // 2, y % 2
                pe.wait_ge(pT_evac, y + 1)
                o = ps[:, 3, 0:256]
                if br == 0 and s:
                    pe.wait_ge(oT_evac, s)
                for k in range(4):
                    pe.matmul(o, pTs[:, y % 2, k, :], araw[:, y % 3, k, 256:512], start=(br == 0 and k == 0), stop=False, skip_group_check=True)
                col = 512 * (br + 1) + 256
                i = pe.matmul(o, pTs[0:64, y % 2, 4, :], kvt[0:64, 4, col:col + 256], start=False, stop=False, skip_group_check=True)
                if br:
                    i = pe.matmul(o, pcg[:, s, :], vc[:, s, :], start=False, stop=True, skip_group_check=True)
                i.then_inc(pv_mm, 1)

            s_kt(0)
            for y in range(18):
                if y < 16:
                    s_scores(y)
                if y < 15:
                    s_kt(y + 1)
                if y >= 3 and y % 2 == 1:
                    s = (y - 3) // 2
                    pe.wait_ge(o_ready, s + 1)
                    if s:
                        pe.wait_ge(oT_evac, s)
                    pe.transpose(ps[0:64, 3, 256:384], osb[:, s % 2, :], ident).then_inc(oT_mm, 1)
                if 1 <= y < 17:
                    s_pt(y - 1)
                    s_pv(y - 1)
            join(pe, 4)
            for k in range(4):
                for t in range(4):
                    col = 512 * (k // 2 + 1) + 128 * (k % 2)
                    i = pe.transpose(ps[:, k, 128 * t:128 * t + 128], kvt[:, t, col:col + 128], ident)
                i.then_inc(kp_mm, 1)
            pe.wait_ge(kp_evac, 4)
            for w in range(NU + 5):
                if w < NU:
                    h, i, br, n = pu(w)
                    g, r = h // 4, h % 4
                    q = 64 * (g % 2)
                    if w >= 3:
                        pe.wait_ge(P_add, w - 2)
                    K = KTp[q:q + 64, br, g // 2, 0:n] if br < 2 else kcT[q:q + 64, 8, g // 2, 0:n]
                    pe.matmul(ps[:, w % 3, 0:n], qT[q:q + 64, 4 * (g // 2) + r, 128 * i:128 * i + 128], K, start=True, stop=True).then_inc(P_mm, 1)
                if 2 <= w < NU + 2:
                    v = w - 2
                    h, i, br, n = pu(v)
                    pe.wait_ge(P_p, v + 1)
                    if v >= 2:
                        pe.wait_ge(P_Te, v - 1)
                    if br < 2:
                        for k in range(i + 1):
                            ins = pe.transpose(ps[:, 3 + v % 2, 128 * k:128 * k + 128], scp[:, v % 3, 128 * k:128 * k + 128], ident)
                    else:
                        ins = pe.transpose(ps[0:n, 3 + v % 2, 0:128], scp[:, v % 3, 0:n], ident)
                    ins.then_inc(P_T, 1)
                if w >= 4 and (w - 4) % 12 == 11:
                    h = (w - 4) // 12
                    g = h // 4
                    pe.wait_ge(P_Te, 12 * h + 12)
                    if h >= 4:
                        pe.wait_ge(P_o, h - 3)
                    q, b = 64 * (h % 2), 5 + h // 2 % 2
                    for br in range(2):
                        for k in range(4):
                            col = 512 * (br + 1) + 256 + 64 * g
                            pe.matmul(ps[q:q + 64, b, 128 * k:512], kvt[:, k, col:col + 64], pT[:, h % 2, br, k, 128 * k:512],
                                      start=(br == 0 and k == 0), stop=False, skip_group_check=True)
                    for i in range(4):
                        n = 7 + 8 * i
                        ins = pe.matmul(ps[q:q + 64, b, 128 * i:128 * i + 128], vc[0:n, 8, 64 * g:64 * g + 64], pcT[0:n, h % 2, 128 * i:128 * i + 128],
                                        start=False, stop=(i == 3), skip_group_check=True)
                    ins.then_inc(P_pv, 1)
            join(pe, 5)
            for e in range(2 * NTT):
                t, k4 = e // 2, e % 2
                t0, n = TILES[t]
                if e >= 8:
                    pe.wait_ge(hT_lo_done, 4 * NTT + e - 7)
                for k in range(4):
                    i = pe.transpose(ps[:, e % 8, 128 * k:128 * k + n], zs[0:n, t, 128 * (4 * k4 + k):128 * (4 * k4 + k) + 128], ident[0:n, 0:n])
                i.then_inc(xT_ready, 1)
            pe.wait_ge(hT_lo_done, 6 * NTT)
            pe.wait_ge(ms_lo, 8)
            for c in range(4):
                for k in range(KT):
                    u = U_OUT + KT * c + k
                    pe.wait_ge(lo_done, u + 1)
                    for t, (t0, n) in enumerate(TILES):
                        if k == 0 and c:
                            pe.wait_ge(tok_evac, 6 * NTT + NTT * (c - 1) + t + 1)
                        o = ps[0:n, t, :]
                        X = [hT_hi[:, k, t0:t0 + n], hT_lo[:, k, t0:t0 + n]]
                        W = [w_hi[:, u % 2, :], w_lo[:, u % 2, :]]
                        pe.matmul(o, X[0], W[0], start=(k == 0), stop=False)
                        pe.matmul(o, X[1], W[0], start=False, stop=False)
                        i = pe.matmul(o, X[0], W[1], start=False, stop=(k == KT - 1))
                    i.then_inc(pe_unit, 1)
            join(pe, 6)
            join(pe, 7)
            for g in range(4 * NTT):
                t, k4 = g // 4, g % 4
                t0, n = TILES[t]
                if g >= 8:
                    pe.wait_ge(hT_lo_done, 6 * NTT + g - 7)
                for k in range(4):
                    i = pe.transpose(ps[:, g % 8, 128 * k:128 * k + n], mo[0:n, t, 128 * (4 * k4 + k):128 * (4 * k4 + k) + 128], ident[0:n, 0:n])
                i.then_inc(xT_ready, 1)
            pe.wait_ge(ld_cw, 96)
            pe.wait_ge(hT_lo_done, 10 * NTT)
            for k in range(FT):
                i = pe.transpose(ps[:, k // 25, 20 * (k % 25):20 * (k % 25) + 20], fwst[:, 128 * k:128 * k + 128], ident[0:20, 0:20])
            i.then_inc(fw_T, 1)
            join(pe, 8)
            with pe.Fori(0, FT) as f:
                pe.wait_ge(g_ready, f + 1)
                feat_tile(None, 0, f * 8 + U_FFN, 0, None)
                pe.wait_ge(up_done, f + 1)
                feat_tile(None, 2, f * 8 + (U_FFN + 4), 0, None)
            join(pe, 9)
            def down_unit(c, k, i, last):
                v = FT * c + k
                at_ = (lambda base: base) if i is None else (lambda base: i * 4 + base)
                pe.wait_ge(lo_done, at_(U_DOWN + v + 1))
                pe.wait_ge(alo_done, at_(v + 1))
                for t, (t0, n) in enumerate(TILES):
                    if k == 0 and c:
                        pe.wait_ge(y_evac, 5 * (c - 1) + t + 1)
                    o = ps[0:n, t, :]
                    X = [a_hi[:, v % 2, t0:t0 + n], a_lo[:, v % 2, t0:t0 + n]]
                    W = [w_hi[:, v % 2, :], w_lo[:, v % 2, :]]
                    pe.matmul(o, X[0], W[0], start=(k == 0), stop=False, skip_group_check=True)
                    pe.matmul(o, X[1], W[0], start=False, stop=False, skip_group_check=True)
                    m = pe.matmul(o, X[0], W[1], start=False, stop=last, skip_group_check=True)
                m.then_inc(pe_unit, 1)

            for c in range(4):
                peeled, turns = loop_units(c)
                for k in peeled:
                    down_unit(c, k, None, False)
                with pe.Fori(0, turns) as i:
                    for j in range(4):
                        down_unit(c, 3 + j, i, False)
            join(pe, 10)
            for b in range(3):
                if b:
                    pe.wait_ge(fco_done, b)
                for k in range(16 * b, min(16 * b + 16, FT)):
                    i = pe.transpose(ps[0:18, 4 + k % 16 // 4, 128 * (k % 4):128 * (k % 4) + 128], fst[:, k, :], ident)
                i.then_inc(fco_T, 1)
            join(pe, 11)

_INS = ['x_prompt', 'x_sample', 'cache_kv', 'cache_win_kv', 'state_ssm_conv', 'state_ssm', 'state_ffn_conv',
        'page_table', 'rel_table', 'ln_mix_pre', 'w_in', 'cmp_pe', 'cmp_w1', 'cmp_b1', 'cmp_w2', 'cmp_b2',
        'ssm_conv_w', 'ssm_conv_b', 'ssm_dt_bias', 'ssm_a_log', 'ssm_d', 'ssm_norm_g', 'w_out', 'ln_mix_post',
        'ln_ffn_pre', 'ffn_w_gate', 'ffn_w_up', 'ffn_dw_w', 'ffn_dw_b', 'ffn_w_down', 'ln_ffn_post']
_OUTS = [('y_prompt', (1, NP, D)), ('y_sample', (NB, NT, D)), ('kv_prompt', (1, 1, NP, 4, NG, HD)),
         ('kv_sample', (1, NB, NT, 4, NG, HD)), ('win_prompt', (1, 1, NP, 2, NG, HD)),
         ('win_sample', (1, NB, PAST, 2, NG, HD)), ('ssm_conv_prompt', (1, 1, NHIST, XBC)),
         ('ssm_conv_sample', (1, NB, NHIST, XBC)), ('ssm_prompt', (1, 1, NH, HD, STATE)),
         ('ssm_sample', (1, NB, NH, HD, STATE)), ('ffn_conv_prompt', (1, 1, FHIST, FF)),
         ('ffn_conv_sample', (1, NB, FHIST, FF))]


def kernel(**inputs):
    import concourse.bacc as bacc
    from concourse.bass_utils import run_bass_kernel_spmd as run
    nc = bacc.Bacc("TRN2", target_bir_lowering=False, num_devices=1)
    host = {n: np.ascontiguousarray(inputs[n]) for n in _INS}
    host["con"], host["onehot"] = constants(), onehot()
    A = {n: nc.dram_tensor(f"in_{n}", a.shape, mybir.dt.from_np(a.dtype), kind="ExternalInput").ap()
         for n, a in host.items()}
    O = {n: nc.dram_tensor(f"out_{n}", s, F32, kind="ExternalOutput").ap() for n, s in _OUTS}
    build(nc, A, O)
    r = run(nc, [{f"in_{n}": a for n, a in host.items()}], core_ids=[0])
    return tuple(r.results[0][f"out_{n}"] for n, _ in _OUTS)
```

```python
import concourse.bass as bass
from concourse import mybir
from concourse.alu_op_type import AluOpType as ALU
import numpy as np
from contextlib import ExitStack

F32 = mybir.dt.float32
F32R = mybir.dt.float32r
I32 = mybir.dt.int32
ACT = mybir.ActivationFunctionType
AX = mybir.AxisListType

D = 2048
NP, NB, NT = 512, 8, 8
NS = NB * NT
TOK = NP + NS
HALF = TOK // 2
KT = D // 128
HD, NH, NG, HPG = 64, 16, 4, 4
PAST, PAGE = 512, 128
QW = NH * HD
KVW = 6 * NG * HD
O_KV = QW
O_GATE = O_KV + KVW
O_Z = O_GATE + 3 * NH
O_XBC = O_Z + 1024
XBC = 2048
O_DT = O_XBC + XBC
INW = O_DT + NH
FF = 5504
FT = FF // 128
NCMP = 31
NSEL = 9
STATE = 128
EPS = 1e-6
NEG = -1e30
MASKED = 1e30
CLAMP = 1e29
TINY = 1e-30
BL = 656
BX = 520
XT = XBC // 128
NHIST, FHIST = 3, 2
TILES = [(128 * i, min(128, TOK - 128 * i)) for i in range(-(-TOK // 128))]
NTT = len(TILES)

U_Q, U_XBC, U_KV, U_Z, U_GD = 0, 32, 96, 144, 176
U_OUT = U_GD + 2
U_FFN = U_OUT + 4 * KT
U_DOWN = U_FFN + 8 * FT
U_END = U_DOWN + 4 * FT

C_ID, C_TRI, C_CB, C_TRIS, C_CBS, C_SEQ, C_SAME, C_OV, C_WM, C_IOTA = 0, 128, 256, 384, 448, 512, 520, 648, 657, 665
C_ONE, C_BLK = 672, 800
C_END = 864


def constants():
    c = np.zeros((128, C_END), np.float32)
    k, i = np.arange(128)[:, None], np.arange(128)[None, :]
    c[:, C_ID:C_ID + 128] = k == i
    c[:, C_TRI:C_TRI + 128] = k <= i
    c[:, C_CB:C_CB + 128] = np.where(k <= i, 0.0, NEG)
    ks, js = np.arange(64)[:, None], np.arange(64)[None, :]
    same = ks // NT == js // NT
    c[:64, C_TRIS:C_TRIS + 64] = same & (ks <= js)
    c[:64, C_CBS:C_CBS + 64] = np.where(same & (ks <= js), 0.0, NEG)
    c[:64, C_SEQ:C_SEQ + 8] = ks // NT == np.arange(8)[None, :]
    c[:, C_SAME:C_SAME + 128] = (k // 32 == i // 32) & (k % 8 == i % 8)
    c0, s0 = np.arange(NCMP)[:, None] * 16, np.arange(NSEL)[None, :] * 64
    c[:NCMP, C_OV:C_OV + NSEL] = np.clip(np.minimum(c0 + 32, s0 + 64) - np.maximum(c0, s0), 0, None) / 32
    c[:, C_WM:C_WM + 8] = np.where(np.arange(8)[None, :] < k % 8, MASKED, 0.0)
    c[:, C_IOTA:C_IOTA + 6] = np.arange(1, 7)[None, :]
    c[:, C_ONE:C_ONE + 128] = 1.0
    c[:64, C_BLK:C_BLK + 64] = same
    return c


def onehot():
    dist = BX - np.arange(BL)
    n = np.maximum(dist, 0)
    nf = np.maximum(n, 1).astype(np.float32)
    large = 16 + (np.log(nf / np.float32(16)) / np.float32(np.log(8.0)) * np.float32(16)).astype(np.int32)
    b = np.where(n < 16, n, np.minimum(large, 31))
    o = np.zeros((33, BL), np.float32)
    ok = dist >= 0
    o[b[ok], np.arange(BL)[ok]] = -1.0
    o[32, ~ok] = MASKED
    return o


def build(nc, A, O):
    ctx = ExitStack()
    with ctx:
        def at(name, shape, off, dt=F32):
            return nc.alloc_sbuf_tensor_at(name, shape, dt, offset=BASE + off)

        def sem(name):
            return ctx.enter_context(nc.semaphore(name))

        def dram(ap, off, dims):
            return bass.AP(ap.tensor, off, dims)

        BASE = -(-nc.sbuf_base // 32) * 32
        ps = ctx.enter_context(nc.psum_tensor("ps", [128, 8, 512], F32))
        RA = 0
        RW = 73728
        RC = RW + 16384
        RB = RC + 8192
        hT_hi = at("hT_hi", [128, KT, TOK], RA, F32R)
        hT_lo = at("hT_lo", [128, KT, TOK], RA + 36864, F32R)
        w_raw = at("w_raw", [128, 4, 512], RW)
        w_hi = at("w_hi", [128, 2, 512], RW + 8192, F32R)
        w_lo = at("w_lo", [128, 2, 512], RW + 12288, F32R)
        con = at("con", [128, C_END], RC)
        cwT = at("cwT", [128, XT, 29], RC + 3456)
        cst = at("cst", [128, XT, 27], RC + 3456 + 1856)
        small = at("small", [128, 256], RC + 3456 + 1856 + 1728)
        qT = at("qT", [128, 8, TOK], RB)
        xbcT = at("xbcT", [128, XT, TOK], RB + 18432)
        kvt = at("kvt", [128, NTT, KVW], RB + 55296)
        zs = at("zs", [128, NTT, 1024], RB + 86016)
        RX = RB + 106496
        xr = at("xr", [128, 604], RX)
        xc = at("xc", [128, 604], RX + 2432)
        xin = at("xin", [128, NTT, D], RB + 55296)
        gb = at("gb", [128, D], RB + 55296 + 40960)
        cwst = at("cwst", [29, XBC], RB + 18432)
        junk = at("junk", [128, D], RB)
        gdt = at("gdt", [128, NTT, 64], RX)
        ss = small[:, 0:5]
        rs = small[:, 5:10]
        ident = con[:, C_ID:C_ID + 128]

        ld_const, ld_x, ld_g, ld_cw = sem("ld_const"), sem("ld_x"), sem("ld_g"), sem("ld_cw")
        raw_loaded = [sem(f"raw_loaded{i}") for i in range(4)]
        hi_done, lo_done, pe_unit = sem("hi_done"), sem("lo_done"), sem("pe_unit")
        phase = sem("phase_done")
        a_ch, v_ch = sem("act_chain"), sem("dve_chain")
        ss_ready, xn_ready = sem("ss_ready"), sem("xn_ready")
        xT_ready, hT_hi_done, hT_lo_done = sem("xT_ready"), sem("hT_hi_done"), sem("hT_lo_done")
        cw_ready = sem("cwT_transposed")
        feat_evac, tok_evac, xr_ready, conv_done = sem("feat_evac"), sem("tok_evac"), sem("xr_ready"), sem("conv_done")
        kv_stored, out_stored = sem("kv_stored"), sem("out_stored")

        w_in, w_out = A["w_in"], A["w_out"]

        class Chain:
            def __init__(self, eng, s):
                self.eng, self.s, self.n = eng, s, 0

            def __call__(self, ins):
                self.n += 1
                ins.then_inc(self.s, 1)
                self.eng.wait_ge(self.s, self.n)

        def join(eng, k):
            eng.drain().then_inc(phase, 1)
            eng.wait_ge(phase, 4 * (k + 1))

        block = ctx.enter_context(nc.Block())

        xsk = at("xs_tok", [128, NTT, 1024], RA)
        Bk = at("B_tok", [128, NTT, 512], RA + 20480)
        h0r = at("h0", [128, 2, NB, STATE], RA + 30720)
        h0T = at("h0T", [128, NB, 128], RA + 38912)
        hst = at("h_state", [128, 1024], RA + 38912)
        seg = at("seg", [128, 2, 4, 128], RA + 43008)
        bex = at("B_by_sequence", [64, NB, 128], RA + 47104)
        yoff = at("y_off", [64, 1024], RA + 51200)
        xdt = at("x_dt", [128, 2, 1024], RA + 55296)
        xte = at("x_to_end", [128, 2, 1024], RA + 63488)
        sp_ = at("ssd_small", [128, 512], RA + 71680)
        dtb, eA, dsk = sp_[:, 0:16], sp_[:, 16:32], sp_[:, 32:48]
        r5 = lambda o: sp_[:, o:o + 80].rearrange("p (t h) -> p t h", t=NTT)
        dt_, a_, eac, ete, eto = r5(48), r5(128), r5(208), r5(288), r5(368)
        ss2 = sp_[:, 448:468]
        pool_ch = sem("pool_chain")
        acs = at("a_cumulative", [128, NTT, NH], RX + 6656)
        dec = sp_[:, 468:484].rearrange("p (b s) -> p b s", b=2)
        yoT = at("y_off_T", [128, 64], RX + 6400)
        ngb = at("norm_gain", [128, 1024], RX + 1280)
        tmp2 = at("y_tmp", [128, 256], RX + 5376)
        v_, w5 = xdt[:, 0, 0:80].rearrange("p (t h) -> p t h", t=NTT), xdt[:, 0, 80:160].rearrange("p (t h) -> p t h", t=NTT)
        cso = at("conv_out", [27, XBC], RA + 30720)
        hso = at("state_out", [128, 8, 128], RA + 47104)
        ld_ssd = sem("ld_ssd")
        h0_loaded, h0_stored = [sem("h0_loaded0"), sem("h0_loaded1")], [sem("h0_stored0"), sem("h0_stored1")]
        tokT_ready, tokT_evac, a_ready, sums_ready, exps_ready = sem("tokT_ready"), sem("tokT_evac"), sem("a_ready"), sem("sums_ready"), sem("exps_ready")
        sum_ready = sem("sum_copies_ready")
        v_ready, l_ready = sem("softplus_arg"), sem("softplus_log")
        h0T_ready, h0T_evac, yo_ready, yoT_evac = sem("h0T_ready"), sem("h0T_evac"), sem("yo_ready"), sem("yoT_evac")
        yoff_ready, yoff_evac, dec_ready, newps_ready, new_ready = sem("yoff_ready"), sem("yoff_evac"), sem("dec_ready"), sem("newps_ready"), sem("new_ready")
        bexp_ready, xt_ready = sem("bexp_ready"), sem("xt_ready")
        s1_ready, seg_ready, dec_exp, M_done = sem("s1_ready"), sem("seg_ready"), sem("decay_ready"), sem("M_done")
        y_ready, unit_done = sem("y_ready"), sem("ssd_unit_done")
        ss2_ready, inv2, rs2 = sem("ss2_ready"), sem("inv2"), sem("rs2_ready")
        fin_T, fin_copied, ssd_stored = sem("fin_T"), sem("fin_copied"), sem("ssd_stored")

        XF = RB + 36864
        mixA = at("mix_attn", [128, 8, TOK], RB + 18432)
        vc = at("v_cmp", [NCMP, 9, 256], XF)
        kcT = at("k_cmp_T", [128, 9, 2, NCMP], XF + 9216)
        kvp = at("pairs_T", [128, 2, 4, 4, 256], RA)
        craw = at("cmp_rows", [128, 2, 2, 2, 4, 2, 64], RA + 32768)
        w1p = at("w1_pairs", [128, 2, 16, 128], RA + 49152)
        gact = at("cmp_hidden", [128, 496], RA + 65536)
        cs = at("cmp_small", [128, 480], RA + 67584)
        w2t, b1t, b2k, hb = cs[:, 0:128].rearrange("p (a d) -> p a d", a=2), cs[:, 128:130], cs[:, 130:131], cs[:, 132:134]
        b2v, pes, peT = cs[0:NCMP, 136:200], cs[0:32, 200:328], cs[:, 328:360]
        tab = cs[0:33, 360:376]
        oh = at("onehot_sb", [33, BL], RA + 69504)
        brow = at("bias_rows", [NH, BL], RX + 1280)
        rb = nc.dram_tensor("bias_scratch", (NH, 128, BL), F32).ap()
        gsc = nc.dram_tensor("gate_scratch", (128, 24), F32).ap()
        ld_c, rb_stored, gsc_stored, tab_set, win_copied = sem("ld_cmp_params"), sem("bias_stored"), sem("gates_stored"), sem("tab_set"), sem("win_copied")
        craw_loaded = [sem("craw_loaded0"), sem("craw_loaded1")]
        rb_mm, rb_ready, pe_T, peT_ready, pb_mm, hb_ready = sem("bias_mm"), sem("bias_rows_ready"), sem("pe_T"), sem("peT_ready"), sem("pe_bias_mm"), sem("hid_bias_ready")
        pairT_ready, pairT_evac = sem("pairT_ready"), sem("pairT_evac")
        hid_ready, gelu_done, kc_ready, kc_evac, vc_ready, vc_evac = sem("hid_ready"), sem("gelu_done"), sem("kc_ready"), sem("kc_evac"), sem("vc_ready"), sem("vc_evac")
        CH = [(0, 4), (4, 4), (8, 1)]

        araw = at("kv_rows", [128, 4, 4, 512], RA)
        KTs = at("K_T", [128, 2, 2, 512], RA + 32768)
        pTs = at("p_T", [128, 2, 5, 128], RA + 40960)
        scs = at("scores_s", [128, 2, 576], RA + 46080)
        sbd = at("bias_and_drop", [128, 2, 512], RA + 50688)
        qs = at("q_s", [128, 2, NB, 32], RA + 54784)
        knT = at("k_new_T", [128, 2, 2, 64], RA + 56832)
        pc0 = at("pc_T", [NCMP, NB, 128], RA + 57856)
        pcg = at("pc_gated_T", [NCMP, NB, 128], RA + 61952)
        scc = at("scores_c", [128, NB, NCMP], RA + 66048)
        scg = at("probs_c_gated", [128, NB, NCMP], RA + 67072)
        osb = at("o_s", [128, 2, 64], RA + 68096)
        as_ = at("attn_small", [128, 512], RA + 68608)
        sb_ = at("bias_s", [128, 2, 512], XF + 11520)
        nb = at("bias_new", [128, 120], XF + 15616)
        gsm_ = at("gates_s", [128, 24], XF + 16128)
        imp = as_[:, 0:72].rearrange("p (s b) -> p s b", s=NB)
        drop = as_[:, 72:120].rearrange("p (s b) -> p s b", s=NB)
        d1 = as_[:, 120:168].rearrange("p (s b) -> p s b", s=NB)
        m8, r8 = as_[:, 168:176], as_[:, 176:184]
        gsm = gsm_[:].rearrange("p (s b) -> p s b", s=NB)
        st_ = as_[:, 208:232].rearrange("p (u x) -> p u x", u=2)
        ld_b, ld_gs = sem("ld_bias_s"), sem("ld_gates_s")
        a_loaded = [sem(f"kv_rows_loaded{i}") for i in range(4)]
        sbd_ready = sem("bias_drop_ready")
        nb_set, qs_ready, kn_mm, kn_ready = sem("nb_set"), sem("qs_ready"), sem("kn_mm"), sem("kn_ready")
        sc_mm, pc_sub, pc_exp, pc_ready, pcT_mm, pcT_evac = sem("cmp_scores_mm"), sem("pc_sub"), sem("pc_exp"), sem("pc_ready"), sem("pcT_mm"), sem("pcT_evac")
        imp_mm, imp_ready, imp2_mm, drop_ready, pcg_ready = sem("imp_mm"), sem("imp_ready"), sem("imp2_mm"), sem("drop_ready"), sem("pcg_ready")
        KT_mm, KT_evac, s_mm, s_max, s_exp, s_p, pT_mm, pT_evac, pv_mm = [sem("sa_" + x) for x in ("KT_mm", "KT_evac", "scores", "max", "exp", "probs", "pT_mm", "pT_evac", "pv")]
        o_ready, oT_mm, oT_evac = sem("sa_o_ready"), sem("sa_oT_mm"), sem("sa_oT_evac")

        TT = at("bias_p", [128, NH, 512], RA)
        pT = at("pT_prompt", [128, 2, 2, 4, 512], RA + 32768)
        cmb = at("bias_c", [128, NH, 4, NCMP], RA + 32768)
        pcp = at("probs_c_prompt", [128, NH, 4, NCMP], RA + 65536)
        pcT = at("pcT_prompt", [NCMP, 2, 512], RX + 1280)
        ast = at("softmax_small", [128, 64], RX + 7424)
        cm = at("cmp_softmax_small", [128, NH, 4], RA + 49152)
        KTp = at("K_T_prompt", [128, 2, 2, 512], XF)
        scp = [at(f"scores_p{i}", [128, 512], XF + 11520 + 2048 * i if i < 3 else RX + 5376) for i in range(4)]
        ld_TT, kp_mm, kp_evac = sem("ld_TT"), sem("kp_mm"), sem("kp_evac")
        P_mm, P_min, P_exp, P_p, P_T, P_Te, P_pv, P_o = [sem("pa_" + x) for x in ("scores", "min", "exp", "probs", "pT_mm", "pT_evac", "pv", "o_evac")]
        C_mm, C_sub, C_exp, C_p = [sem("pa_c_" + x) for x in ("scores", "shifted", "exp", "probs")]
        NPAIR = 4 * NH
        def turn(P, br):
            return 2 * P + br + (P + 3) // 4

        mo = at("mix_out", [128, NTT, D], RB)
        gb2 = at("gain2", [128, D], RB + 40960)
        x2d = nc.dram_tensor("x2_scratch", (TOK, D), F32).ap()
        acT = at("ffn_act_T", [128, FT, TOK], RB)
        fwT = at("ffn_params_T", [128, FT, 20], RB + 99072)
        fst = at("ffn_conv_rows", [128, FT, 18], RB + 102528)
        xr2 = at("ffn_xr", [128, 594], RB + 105632)
        xc2 = at("ffn_xc", [128, 594], RB + 108032)
        gl = at("gelu_gate", [128, TOK], RB + 110432)
        FB = 11
        fwst = at("ffn_params", [80, 128 * FB], RB + 49152)
        ssc = small[:, 16:16 + 4 * NTT].rearrange("p (t c) -> p t c", t=NTT)
        sqj2 = at("squares_unused2", [128, D], RB + 104448)
        a_hi = at("act_hi", [128, 2, TOK], RA, F32R)
        a_lo = at("act_lo", [128, 2, TOK], RA + 4608, F32R)
        yT = at("ffn_out_T", [128, KT, TOK], RA + 9216)
        yn = at("ffn_out_normed", [128, 2, D], RB + 71680)
        sqj = at("squares_unused", [128, D], RB + 88064)
        gb3 = at("gain3", [128, D], RA + 50176)
        x2r = at("x2", [128, NTT, D], RB)
        fco = at("ffn_conv_out", [18, FF], RB + 49152)
        ms_hi, ms_lo = sem("mix_hi"), sem("mix_lo")
        x2_ready, x2_stored, x2n_ready, fw_T = sem("x2_ready"), sem("x2_stored"), sem("x2_normed"), sem("fw_T")
        g_ready, g_sum, g_act, up_done, f_ch = sem("gate_out"), sem("gate_sum"), sem("gate_act"), sem("up_done"), sem("ffn_chain")
        y_used = sem("y_tile_used")
        ahi_done, alo_done, y_evac, fin_y, y_stored = sem("act_hi_done"), sem("act_lo_done"), sem("y_evac"), sem("y_ready_out"), sem("y_stored")
        fco_T, fco_done = sem("fco_T"), sem("fco_done")

        def loop_units(c):
            return range(3), 10

        def bc(ap, dims):
            return ap.unsqueeze(len(ap.shape)).broadcast_to(dims)

        @block.sync
        def _(sp):
            sp.dma_start(con[:], A["con"]).then_inc(ld_const, 16)
            for t, (t0, n) in enumerate(TILES):
                src = A["x_prompt"][0, t0:t0 + n, :] if t < 4 else A["x_sample"].rearrange("b t d -> (b t) d")
                sp.dma_start(xin[0:n, t, :], src).then_inc(ld_x, 16)
            sp.dma_start(gb[:], dram(A["ln_mix_pre"], 0, [[0, 128], [1, D]])).then_inc(ld_g, 16)
            sp.dma_start(cwst[0:24, :], A["state_ssm_conv"].rearrange("l b k c -> (l b k) c")).then_inc(ld_cw, 16)
            sp.dma_start(cwst[24:28, :], A["ssm_conv_w"].rearrange("l k c -> (l k) c")).then_inc(ld_cw, 16)
            sp.dma_start(cwst[28:29, :], A["ssm_conv_b"]).then_inc(ld_cw, 16)

            def unit(u, src, shape):
                if u >= 4:
                    sp.wait_ge(lo_done, u - 3)
                dst = w_raw[:, u % 4, :]
                if shape:
                    dst = dst.rearrange("p (k c) -> p k c", k=shape)
                sp.dma_start(dst, src).then_inc(raw_loaded[u % 4], 16)

            def feat_cols(w, wd, col, k0):
                return dram(w, k0 * 128 * wd + col, [[wd, 128], [128 * wd, 4], [1, 128]])

            for f in range(8):
                gp, r = f // 4, f % 4
                for j in range(4):
                    col = (8 * gp + r) * HD
                    u = U_Q + 4 * f + j
                    if u >= 4:
                        sp.wait_ge(lo_done, u - 3)
                    for h in range(2):
                        dst = w_raw[:, u % 4, :].rearrange("p (k c) -> p k c", k=4)[:, :, 64 * h:64 * h + 64]
                        src = dram(w_in, j * 512 * INW + col + 256 * h, [[INW, 128], [128 * INW, 4], [1, 64]])
                        sp.dma_start(dst, src).then_inc(raw_loaded[u % 4], 16)
            for f in range(XT):
                for j in range(4):
                    unit(U_XBC + 4 * f + j, feat_cols(w_in, INW, O_XBC + 128 * f, 4 * j), 4)
            for c in range(5):
                col = O_KV + 512 * c if c < 3 else O_Z + 512 * (c - 3)
                for k in range(KT):
                    unit(U_KV + KT * c + k, dram(w_in, k * 128 * INW + col, [[INW, 128], [1, 512]]), 0)
            for j in range(2):
                u = U_GD + j
                sp.wait_ge(lo_done, u - 3)
                d = w_raw[:, u % 4, :].rearrange("p (k c) -> p k c", k=8)
                sp.dma_start(d[:, :, 0:48], dram(w_in, j * 1024 * INW + O_GATE, [[INW, 128], [128 * INW, 8], [1, 48]])).then_inc(raw_loaded[u % 4], 16)
                sp.dma_start(d[:, :, 48:64], dram(w_in, j * 1024 * INW + O_DT, [[INW, 128], [128 * INW, 8], [1, 16]])).then_inc(raw_loaded[u % 4], 16)

            sp.wait_ge(phase, 8)
            sp.dma_start(dtb, dram(A["ssm_dt_bias"], 0, [[0, 128], [1, NH]])).then_inc(ld_ssd, 16)
            sp.dma_start(eA, dram(A["ssm_a_log"], 0, [[0, 128], [1, NH]])).then_inc(ld_ssd, 16)
            sp.dma_start(dsk, dram(A["ssm_d"], 0, [[0, 128], [1, NH]])).then_inc(ld_ssd, 16)
            sp.dma_start(ngb[:], dram(A["ssm_norm_g"], 0, [[0, 128], [1, 1024]])).then_inc(ld_ssd, 16)
            HS = NH * HD * STATE
            for p in range(10):
                if p >= 2:
                    q = p - 2
                    sp.wait_ge(new_ready, q + 1)
                    sp.dma_start(dram(O["ssm_sample"], q * 16384, [[STATE, 128], [HS, NB], [1, STATE]]), h0r[:, q % 2]).then_inc(h0_stored[q % 2], 16)
                if p < 8:
                    if p >= 2:
                        sp.wait_ge(h0_stored[p % 2], 16 * (p // 2))
                    sp.dma_start(h0r[:, p % 2], dram(A["state_ssm"], p * 16384, [[STATE, 128], [HS, NB], [1, STATE]])).then_inc(h0_loaded[p % 2], 16)
            sp.wait_ge(fin_copied, 2)
            sp.dma_start(O["ssm_conv_prompt"].rearrange("l b k c -> (l b k) c"), cso[0:3, :]).then_inc(ssd_stored, 16)
            sp.dma_start(O["ssm_conv_sample"].rearrange("l b k c -> (l b k) c"), cso[3:27, :]).then_inc(ssd_stored, 16)
            sp.dma_start(dram(O["ssm_prompt"], 0, [[STATE, 128], [16384, 8], [1, STATE]]), hso[:]).then_inc(ssd_stored, 16)
            sp.wait_ge(phase, 12)
            sp.wait_ge(ssd_stored, 48)
            sp.dma_start(oh[:], A["onehot"]).then_inc(ld_c, 16)
            sp.dma_start(tab[0:32, :], A["rel_table"]).then_inc(ld_c, 16)
            sp.dma_start(pes, A["cmp_pe"].rearrange("l a (s q) d -> (l a s) (q d)", q=2)).then_inc(ld_c, 16)
            for a in range(2):
                sp.dma_start(w1p[:, a], dram(A["cmp_w1"], a * 262144, [[128, 128], [16384, 16], [1, 128]])).then_inc(ld_c, 16)
            sp.dma_start(w2t, dram(A["cmp_w2"], 0, [[64, 128], [8192, 2], [1, 64]])).then_inc(ld_c, 16)
            sp.dma_start(b1t, dram(A["cmp_b1"], 0, [[1, 128], [128, 2]]), allow_slow_non_contiguous=True).then_inc(ld_c, 16)
            for a in range(2):
                sp.dma_start(cs[64 * a:64 * a + 64, 130:131], dram(A["cmp_b2"], 0, [[1, 64], [1, 1]])).then_inc(ld_c, 16)
            sp.dma_start(b2v, dram(A["cmp_b2"], 64, [[0, NCMP], [1, 64]])).then_inc(ld_c, 16)
            for s in range(NB):
                for b in range(3):
                    sp.dma_start(dram(gsc, 3 * s + b, [[24, NT], [192, NH]]), gdt[8 * s:8 * s + 8, 4, 16 * b:16 * b + 16],
                                 allow_slow_non_contiguous=True).then_inc(gsc_stored, 16)
            sp.wait_ge(kv_stored, 64)
            PGW = PAGE * 1024
            ckv = A["cache_kv"].rearrange("l n t s g d -> (l n) (t s g d)")
            def page_index(s, p):
                return sp.value_load(A["page_table"][s:s + 1, p:p + 1], min_val=0, max_val=39)
            for s in range(9):
                if s >= 2:
                    sp.wait_ge(pairT_evac, 4 * (s - 1))
                for p in range(4):
                    dst = craw[64 * (p % 2):64 * (p % 2) + 64, s % 2, p // 2]
                    if s < 8:
                        src = ckv[bass.ds(page_index(s, p), 1), :].rearrange("n (i q s g d) -> i (n s g) q d", q=2, s=4, g=NG, d=HD)[:, 0:8]
                    else:
                        src = O["kv_prompt"].rearrange("l b t s g d -> (l b t) s g d")[128 * p:128 * p + 128].rearrange("(i q) s g d -> i (s g) q d", q=2)[:, 0:8]
                    dst = dst.rearrange("i a g q d -> i (a g) q d")
                    for q in range(2):
                        sp.dma_start(dst[:, :, q, :], src[:, :, q, :]).then_inc(craw_loaded[s % 2], 16)
            sp.wait_ge(rb_ready, 1)
            sp.dma_start(rb, brow[:].unsqueeze(1).broadcast_to([NH, 128, BL])).then_inc(rb_stored, 16)
            sp.wait_ge(rb_stored, 16)
            sp.wait_ge(gsc_stored, 16 * 3 * NB)
            sp.wait_ge(nb_set, 1)
            for h in range(NH):
                sp.dma_start(sb_[8 * h:8 * h + 8, 0, :], dram(rb, h * 128 * BL + 8, [[BL - 1, 8], [1, 512]])).then_inc(ld_b, 16)
                sp.dma_start(nb[8 * h:8 * h + 8, 56:64], dram(rb, h * 128 * BL + BX, [[BL - 1, 8], [1, 8]])).then_inc(ld_b, 16)
            sp.dma_start(gsm_[:], gsc).then_inc(ld_gs, 16)
            sp.wait_ge(phase, 16)
            for y in range(16):
                s, br = y // 2, y % 2
                if y >= 4:
                    sp.wait_ge(pv_mm, y - 3)
                if br == 0:
                    for p in range(4):
                        src = ckv[bass.ds(page_index(s, p), 1), :].rearrange("n (t c) -> (n t) c", t=PAGE)[:, 512:1024]
                        sp.dma_start(araw[:, y % 4, p, :], src).then_inc(a_loaded[y % 4], 16)
                else:
                    sp.dma_start(araw[:, y % 4, :, :], dram(A["cache_win_kv"], s * PAST * 512, [[512, 128], [65536, 4], [1, 512]])).then_inc(a_loaded[y % 4], 64)
            for s in range(NB):
                sp.dma_start(O["win_sample"][0, s, 0:PAST - NT].rearrange("t s g d -> t (s g d)"),
                             A["cache_win_kv"][0, s, NT:PAST].rearrange("t s g d -> t (s g d)")).then_inc(win_copied, 16)
            sp.wait_ge(phase, 20)
            sp.dma_start(TT[:], dram(rb, 136, [[BL - 1, 128], [128 * BL, NH], [1, 512]])).then_inc(ld_TT, 16)
            for c in range(4):
                for k in range(KT):
                    unit(U_OUT + KT * c + k, dram(A["w_out"], k * 128 * D + 512 * c, [[D, 128], [1, 512]]), 0)
            sp.wait_ge(out_stored, 208)
            for t, (t0, n) in enumerate(TILES):
                src = A["x_prompt"][0, t0:t0 + n, :] if t < 4 else A["x_sample"].rearrange("b t d -> (b t) d")
                sp.dma_start(xin[0:n, t, :], src).then_inc(ld_x, 16)
            sp.dma_start(gb[:], dram(A["ln_mix_post"], 0, [[0, 128], [1, D]])).then_inc(ld_g, 16)
            sp.dma_start(gb2[:], dram(A["ln_ffn_pre"], 0, [[0, 128], [1, D]])).then_inc(ld_g, 16)
            for b in range(4):
                c0, c1 = 128 * FB * b, min(128 * FB * (b + 1), FF)
                for r, src in ((0, A["state_ffn_conv"].rearrange("l b k c -> (l b k) c")),
                               (16, A["ffn_dw_w"].rearrange("l k c -> (l k) c")), (19, A["ffn_dw_b"])):
                    m = src.shape[0]
                    sp.dma_start(fwst[20 * b + r:20 * b + r + m, 0:c1 - c0], src[:, c0:c1]).then_inc(ld_cw, 16)
            W2 = [A[x][0].rearrange("(k p) c -> p k c", p=128) for x in ("ffn_w_gate", "ffn_w_up")]
            with sp.Fori(0, FT) as f:
                for j in range(8):
                    sp.wait_ge(lo_done, f * 8 + (U_FFN + j - 3))
                    sp.dma_start(w_raw[:, (U_FFN + j) % 4, :].rearrange("p (k c) -> p k c", k=4),
                                 W2[j // 4][:, 4 * (j % 4):4 * (j % 4) + 4, bass.ds(f * 128, 128)]).then_inc(raw_loaded[(U_FFN + j) % 4], 16)
            Wd = A["ffn_w_down"][0]
            for c in range(4):
                u0 = U_DOWN + FT * c
                peeled, turns = loop_units(c)
                for k in peeled:
                    unit(u0 + k, Wd[128 * k:128 * k + 128, 512 * c:512 * c + 512], 0)
                with sp.Fori(0, turns) as i:
                    for j in range(4):
                        sp.wait_ge(lo_done, i * 4 + (u0 + j))
                        sp.dma_start(w_raw[:, (u0 + 3 + j) % 4, :], Wd[bass.ds(i * 512 + 128 * (3 + j), 128), 512 * c:512 * c + 512]).then_inc(raw_loaded[(u0 + 3 + j) % 4], 16)
            sp.wait_ge(phase, 32)
            sp.wait_ge(x2_stored, 16 * NTT)
            for t, (t0, n) in enumerate(TILES):
                sp.dma_start(x2r[0:n, t, :], x2d[t0:t0 + n, :]).then_inc(ld_x, 16)
            sp.dma_start(gb3[:], dram(A["ln_ffn_post"], 0, [[0, 128], [1, D]])).then_inc(ld_x, 16)
            for t, (t0, n) in enumerate(TILES):
                sp.wait_ge(fin_y, t + 1)
                dst = O["y_prompt"][0, t0:t0 + n, :] if t < 4 else O["y_sample"].rearrange("b t d -> (b t) d")
                sp.dma_start(dst, x2r[0:n, t, :]).then_inc(y_stored, 16)
            sp.wait_ge(fco_done, 3)
            sp.dma_start(O["ffn_conv_prompt"].rearrange("l b k c -> (l b k) c"), fco[0:2, :]).then_inc(y_stored, 16)
            sp.dma_start(O["ffn_conv_sample"].rearrange("l b k c -> (l b k) c"), fco[2:18, :]).then_inc(y_stored, 16)
            sp.wait_ge(y_stored, 16 * (2 + NTT))
            sp.wait_ge(win_copied, 128)
            sp.wait_ge(ssd_stored, 48)
            sp.wait_ge(h0_stored[0], 64)
            sp.wait_ge(h0_stored[1], 64)
            sp.wait_ge(kv_stored, 64)
            sp.wait_ge(out_stored, 208)

        def raw_count(u):
            return 16 * sum(2 if v < U_XBC or U_GD <= v < U_OUT else 1 for v in range(u % 4, u + 1, 4))

        def act_feature(act, ch, f):
            act.wait_ge(pe_unit, 4 * (f + 1))
            b = 2 * (f % 2)
            if f < 8:
                act.activation(qT[:, f, :].rearrange("p (h c) -> p h c", h=2), ps[:, b:b + 2, 0:HALF],
                               ACT.Copy, scale=-HD ** -0.5).then_inc(feat_evac, 1)
                return
            x = f - 8
            if x:
                act.wait_ge(conv_done, x)
            act.activation(xr[:, 3:3 + HALF], ps[:, b, 0:HALF], ACT.Copy)
            act.activation(xr[:, 3 + HALF:3 + NP], ps[:, b + 1, 0:NP - HALF], ACT.Copy)
            last = act.activation(xr[:, 515:603].rearrange("p (s c) -> p s c", s=8)[:, :, 3:11],
                                  ps[:, b + 1, NP - HALF:HALF].rearrange("p (s c) -> p s c", s=8), ACT.Copy)
            last.then_inc(xr_ready, 1)
            act.wait_ge(xr_ready, x + 1)
            act.sem_inc(feat_evac, 1)
            act.wait_ge(acc_ready, x + 1)
            act.activation(xbcT[:, x, 0:NP], xc[:, 0:NP], ACT.Silu)
            act.activation(xbcT[:, x, NP:TOK].rearrange("p (s c) -> p s c", s=8),
                           xc[:, 515:603].rearrange("p (s c) -> p s c", s=8)[:, :, 0:8], ACT.Silu).then_inc(conv_done, 1)

        inv_ready = sem("mean_square_inverse")
        rs_ready = sem("rs_ready")
        small_zero = sem("small_zeroed")
        acc_ready = sem("conv_sum_ready")

        def act_tokens(act, ch, c):
            act.wait_ge(pe_unit, U_KV + KT * (c + 1))
            for t, (t0, n) in enumerate(TILES):
                if c < 3:
                    i = act.activation(kvt[0:n, t, 512 * c:512 * c + 512], ps[0:n, t, :], ACT.Copy)
                else:
                    i = act.activation(zs[0:n, t, 512 * (c - 3):512 * (c - 3) + 512], ps[0:n, t, :], ACT.Silu)
                i.then_inc(tok_evac, 1)
            if c == 2:
                act.wait_ge(tok_evac, 5 * (c + 1))
                for t, (t0, n) in enumerate(TILES[:4]):
                    act.dma_start(O["kv_prompt"].rearrange("l b t s g d -> (l b t) (s g d)")[t0:t0 + n, :],
                                  kvt[0:n, t, 0:1024]).then_inc(kv_stored, 16)
                    act.dma_start(O["win_prompt"].rearrange("l b t s g d -> (l b t) (s g d)")[t0:t0 + n, :],
                                  kvt[0:n, t, 1024:1536]).then_inc(out_stored, 16)
                act.dma_start(O["kv_sample"].rearrange("l b t s g d -> (l b t) (s g d)"), kvt[0:NS, 4, 0:1024]).then_inc(out_stored, 16)
                for s in range(NB):
                    act.dma_start(O["win_sample"][0, s, PAST - NT:PAST].rearrange("t s g d -> t (s g d)"),
                                  kvt[8 * s:8 * s + 8, 4, 1024:1536]).then_inc(out_stored, 16)

        def out_tokens(act, ch, c):
            act.wait_ge(pe_unit, U_OUT + KT * (c + 1))
            for t, (t0, n) in enumerate(TILES):
                ch(act.activation(sqj2[0:n, 0:512], ps[0:n, t, :], ACT.Square, accum_out=small[0:n, 16 + 4 * t + c:17 + 4 * t + c]))
                act.activation(mo[0:n, t, 512 * c:512 * c + 512], ps[0:n, t, :], ACT.Copy).then_inc(tok_evac, 1)

        def down_hi(act, c, k, i):
            v = FT * c + k
            u = U_DOWN + v
            at_ = (lambda per, base: base) if i is None else (lambda per, base: i * per + base)
            act.wait_ge(raw_loaded[u % 4], at_(16, raw_count(u)))
            act.wait_ge(pe_unit, at_(4, u - 1))
            act.activation(w_hi[:, u % 2, :], w_raw[:, u % 4, :], ACT.Copy).then_inc(hi_done, 1)
            src = acT[:, k, :] if i is None else acT[:, bass.ds(i * 4 + k, 1), :].rearrange("p a c -> p (a c)")
            act.activation(a_hi[:, v % 2, :], src, ACT.Copy).then_inc(ahi_done, 1)

        def down_lo(dve, c, k, i):
            v = FT * c + k
            at_ = (lambda per, base: base) if i is None else (lambda per, base: i * per + base)
            dve.wait_ge(ahi_done, at_(4, v + 1))
            src = acT[:, k, :] if i is None else acT[:, bass.ds(i * 4 + k, 1), :].rearrange("p a c -> p (a c)")
            dve.tensor_tensor(a_lo[:, v % 2, :], src, a_hi[:, v % 2, :].bitcast(F32), ALU.subtract).then_inc(alo_done, 1)

        def prompt_out(dve, h):
            dve.wait_ge(P_pv, h + 1)
            q = 64 * (h % 2)
            dve.tensor_copy(mixA[q:q + 64, h // 2, 0:NP], ps[q:q + 64, 6 + h // 2 % 2, :]).then_inc(P_o, 1)

        @block.scalar
        def _(act):
            ch = Chain(act, a_ch)

            def hi(u):
                act.wait_ge(raw_loaded[u % 4], raw_count(u))
                if u >= 2:
                    act.wait_ge(pe_unit, u - 1)
                act.activation(w_hi[:, u % 2, :], w_raw[:, u % 4, :], ACT.Copy).then_inc(hi_done, 1)

            act.wait_ge(ld_x, 16 * NTT)
            act.wait_ge(small_zero, 1)
            for t, (t0, n) in enumerate(TILES):
                ch(act.activation(junk[0:n, :], xin[0:n, t, :], ACT.Square, accum_out=small[0:n, t:t + 1]))
            act.drain().then_inc(ss_ready, 1)
            act.wait_ge(inv_ready, 1)
            act.activation(rs, rs, ACT.Sqrt).then_inc(rs_ready, 1)
            for g in range(4 * NTT):
                t, k4 = g // 4, g % 4
                t0, n = TILES[t]
                act.wait_ge(xT_ready, g + 1)
                act.activation(hT_hi[:, 4 * k4:4 * k4 + 4, t0:t0 + n],
                               ps[:, g % 8, :].rearrange("p (k c) -> p k c", k=4)[:, :, 0:n], ACT.Copy).then_inc(hT_hi_done, 1)
            join(act, 0)
            for f in range(24):
                hi(4 * f)
                hi(4 * f + 1)
                if f:
                    act_feature(act, ch, f - 1)
                hi(4 * f + 2)
                hi(4 * f + 3)
            for c in range(5):
                for k in range(KT):
                    hi(U_KV + KT * c + k)
                    if k == 1:
                        if c == 0:
                            act_feature(act, ch, 23)
                        else:
                            act_tokens(act, ch, c - 1)
            hi(U_GD)
            hi(U_GD + 1)
            act_tokens(act, ch, 4)
            act.wait_ge(pe_unit, U_GD + 2)
            for t, (t0, n) in enumerate(TILES):
                act.activation(gdt[0:n, t, :], ps[0:n, 5, 64 * t:64 * t + 64], ACT.Copy).then_inc(tok_evac, 1)
            join(act, 1)
            act.activation(gdt[:, :, 0:48], gdt[:, :, 0:48], ACT.Sigmoid)
            act.wait_ge(ld_ssd, 64)
            act.activation(eA, eA, ACT.Exp).then_inc(v_ready, 1)
            act.wait_ge(v_ready, 2)
            ch(act.activation(w5, w5, ACT.Exp))
            act.activation(w5, w5, ACT.Ln, bias=1.0).then_inc(l_ready, 1)
            for G in range(3 * NTT):
                t, b = G // 3, G % 3
                n = TILES[t][1]
                act.wait_ge(tokT_ready, G + 1)
                dst = xsk[0:n, t, 512 * b:512 * b + 512] if b < 2 else Bk[0:n, t, :]
                act.activation(dst, ps[0:n, G % 6, :], ACT.Copy).then_inc(tokT_evac, 1)
            act.wait_ge(sum_ready, 1)
            act.activation(sp_[:, 208:448], sp_[:, 208:448], ACT.Exp).then_inc(exps_ready, 1)
            for p in range(8):
                act.wait_ge(h0T_ready, p + 1)
                if p:
                    act.wait_ge(yo_ready, p)
                act.activation(h0T[:].rearrange("n (a s) p -> n a (s p)", a=2), ps[:, 0:2, :], ACT.Copy).then_inc(h0T_evac, 1)
                act.wait_ge(yo_ready, p + 1)
                if p:
                    act.wait_ge(yoff_ready, p)
                act.activation(yoT[:], ps[:, 2, 0:64], ACT.Copy).then_inc(yoT_evac, 1)
                if p >= 2:
                    act.wait_ge(new_ready, p - 1)
                act.activation(dec[:, p % 2, :], ps[:, 3, 0:8], ACT.Exp).then_inc(dec_ready, 1)
            for w in range(20):
                n = TILES[w // 4][1]
                act.wait_ge(seg_ready, w + 1)
                act.activation(seg[0:n, w % 2, :, 0:n], seg[0:n, w % 2, :, 0:n], ACT.Exp).then_inc(dec_exp, 1)
            act.wait_ge(unit_done, 20)
            for t, (t0, n) in enumerate(TILES):
                for g in range(4):
                    act.activation(xsk[0:n, 0, 0:256], zs[0:n, t, 256 * g:256 * g + 256], ACT.Square,
                                   accum_out=sp_[0:n, 448 + 4 * t + g:449 + 4 * t + g]).then_inc(ss2_ready, 1)
                    act.wait_ge(ss2_ready, 4 * t + g + 1)
            act.wait_ge(inv2, 1)
            act.activation(ss2, ss2, ACT.Sqrt).then_inc(rs2, 1)
            join(act, 2)
            act.wait_ge(rb_mm, 1)
            act.activation(brow[:, 0:512], ps[0:NH, 0, :], ACT.Copy)
            act.activation(brow[:, 512:BL], ps[0:NH, 1, 0:BL - 512], ACT.Copy).then_inc(rb_ready, 1)
            act.wait_ge(pe_T, 1)
            act.activation(peT, ps[:, 2, 0:32], ACT.Copy).then_inc(peT_ready, 1)
            act.wait_ge(hb_ready, 1)
            e = 0
            for c, (s0, ns) in enumerate(CH):
                for s in range(ns):
                    for b in range(4):
                        act.wait_ge(pairT_ready, e + 1)
                        if b == 0 and s == 0 and c:
                            act.wait_ge(hid_ready, 2 * c)
                        act.activation(kvp[:, b % 2, s, :, 128 * (b // 2):128 * (b // 2) + 128],
                                       ps[:, e % 2, :].rearrange("p (g i) -> p g i", g=4), ACT.Copy).then_inc(pairT_evac, 1)
                        e += 1
                n = 124 * ns
                for a in range(2):
                    act.wait_ge(hid_ready, 2 * c + a + 1)
                    if a or c:
                        act.wait_ge(kc_ready if a else vc_ready, c + 1 if a else c)
                    act.activation(gact[:, 0:n], ps[:, 2 + a, 0:n], ACT.Gelu_apprx_tanh, bias=hb[:, a:a + 1]).then_inc(gelu_done, 1)
                act.activation(kcT[:, s0:s0 + ns].rearrange("p s g n -> p (s g n)"), ps[:, 4, 0:62 * ns], ACT.Identity, bias=b2k).then_inc(kc_evac, 1)
            join(act, 3)
            act.wait_ge(kn_mm, 1)
            act.activation(knT[:].rearrange("p b g c -> p (b g c)"), ps[:, 0, 0:256], ACT.Copy).then_inc(kn_ready, 1)
            act.wait_ge(pc_sub, 1)
            act.activation(scc[:], scc[:], ACT.Exp, scale=-1.0).then_inc(pc_exp, 1)
            act.wait_ge(pcT_mm, 1)
            act.activation(pc0[:].rearrange("n (a s) p -> n a (s p)", a=2), ps[0:NCMP, 0:2, :], ACT.Copy).then_inc(pcT_evac, 1)
            act.wait_ge(pcT_mm, 2)
            act.activation(pcg[:].rearrange("n (a s) p -> n a (s p)", a=2), ps[0:NCMP, 4:6, :], ACT.Copy).then_inc(pcT_evac, 1)

            def kt_evac(y):
                for gp in range(2):
                    act.wait_ge(KT_mm, 2 * y + gp + 1)
                    if y >= 2:
                        act.wait_ge(s_mm, y - 1)
                    act.activation(KTs[:, y % 2, gp, :], ps[:, 4 + gp, :], ACT.Copy).then_inc(KT_evac, 1)

            def pt_evac(y):
                act.wait_ge(pT_mm, y + 1)
                if y >= 2:
                    act.wait_ge(pv_mm, y - 1)
                act.activation(pTs[:, y % 2, 0:4, :].rearrange("p k c -> p (k c)"), ps[:, 6, :], ACT.Copy)
                act.activation(pTs[0:64, y % 2, 4, :], ps[0:64, 7, 0:128], ACT.Copy).then_inc(pT_evac, 1)

            kt_evac(0)
            for y in range(17):
                if y < 16:
                    act.wait_ge(s_max, y + 1)
                    act.activation(scs[:, y % 2, :], scs[:, y % 2, :], ACT.Exp, scale=-1.0, bias=st_[:, y % 2, 0:1], accum_out=st_[:, y % 2, 1:2]).then_inc(s_exp, 1)
                if y < 15:
                    kt_evac(y + 1)
                if y >= 1:
                    pt_evac(y - 1)
            join(act, 4)
            for k in range(4):
                act.wait_ge(kp_mm, k + 1)
                act.activation(KTp[:, k // 2, k % 2, :], ps[:, k, :], ACT.Copy).then_inc(kp_evac, 1)
            for b in range(4):
                act.wait_ge(C_sub, b + 1)
                act.activation(pcp[:, 4 * b:4 * b + 4], pcp[:, 4 * b:4 * b + 4], ACT.Exp, scale=-1.0).then_inc(C_exp, 1)

            def pt_out(P):
                h, i = P // 4, P % 4
                n = 128 * (i + 1)
                if h >= 2 and i == 0:
                    act.wait_ge(P_pv, h - 1)
                for br in range(2):
                    e = turn(P, br)
                    act.wait_ge(P_T, e + 1)
                    act.activation(pT[:, h % 2, br, 0:i + 1, 128 * i:128 * i + 128],
                                   ps[:, 4 + e % 2, 0:n].rearrange("p (k c) -> p k c", c=128), ACT.Copy).then_inc(P_Te, 1)
                if i == 0:
                    e = turn(P, 2)
                    act.wait_ge(P_T, e + 1)
                    act.activation(pcT[:, h % 2, :], ps[0:NCMP, 4 + e % 2, :], ACT.Copy).then_inc(P_Te, 1)

            for P in range(NPAIR + 1):
                if P < NPAIR:
                    n = 128 * (P % 4 + 1)
                    for br in range(2):
                        w, k = 2 * P + br, 8 * (P % 2)
                        act.wait_ge(P_min, w + 1)
                        act.activation(scp[w % 4][:, 0:n], scp[w % 4][:, 0:n], ACT.Exp, scale=-1.0, bias=ast[:, k + br:k + br + 1],
                                       accum_out=ast[:, k + 2 + br:k + 3 + br]).then_inc(P_exp, 1)
                if P:
                    pt_out(P - 1)
            join(act, 5)
            for k in range(8):
                act.activation(hT_hi[:, k, :], mixA[:, k, :], ACT.Copy).then_inc(ms_hi, 1)
            for e in range(2 * NTT):
                t, k4 = e // 2, e % 2
                t0, n = TILES[t]
                act.wait_ge(xT_ready, 4 * NTT + e + 1)
                act.activation(hT_hi[:, 8 + 4 * k4:12 + 4 * k4, t0:t0 + n],
                               ps[:, e % 8, :].rearrange("p (k c) -> p k c", k=4)[:, :, 0:n], ACT.Copy).then_inc(hT_hi_done, 1)
            for c in range(4):
                for k in range(KT):
                    hi(U_OUT + KT * c + k)
                    if k == 1 and c:
                        out_tokens(act, ch, c - 1)
            out_tokens(act, ch, 3)
            act.drain().then_inc(ss_ready, 1)
            act.wait_ge(inv_ready, 2)
            act.activation(rs, rs, ACT.Sqrt).then_inc(rs_ready, 1)
            for i in range(1, NTT + 2):
                if i <= NTT:
                    t0, n = TILES[i - 1]
                    act.wait_ge(x2_ready, i)
                    act.dma_start(x2d[t0:t0 + n, :], xin[0:n, i - 1, :]).then_inc(x2_stored, 16)
                    act.activation(sqj2[0:n, :], xin[0:n, i - 1, :], ACT.Square, accum_out=small[0:n, i - 1:i]).then_inc(ss_ready, 1)
                    act.wait_ge(inv_ready, 2 + i)
                    act.activation(small[0:n, 4 + i:5 + i], small[0:n, 4 + i:5 + i], ACT.Sqrt).then_inc(rs_ready, 1)
                if i >= 2:
                    t0, n = TILES[i - 2]
                    for k4 in range(4):
                        g = 4 * (i - 2) + k4
                        act.wait_ge(xT_ready, 6 * NTT + g + 1)
                        act.activation(hT_hi[:, 4 * k4:4 * k4 + 4, t0:t0 + n],
                                       ps[:, g % 8, :].rearrange("p (k c) -> p k c", k=4)[:, :, 0:n], ACT.Copy).then_inc(hT_hi_done, 1)
            join(act, 6)
            act.drain().then_inc(g_ready, 1)
            act.drain().then_inc(g_act, 1)
            with act.Fori(0, FT) as f:
                def hi_loop(j):
                    act.wait_ge(raw_loaded[(U_FFN + j) % 4], f * 32 + raw_count(U_FFN + j))
                    act.wait_ge(pe_unit, f * 8 + (U_FFN + j - 1))
                    act.activation(w_hi[:, j % 2, :], w_raw[:, (U_FFN + j) % 4, :], ACT.Copy).then_inc(hi_done, 1)

                for j in range(6):
                    hi_loop(j)
                act.wait_ge(pe_unit, f * 8 + (U_FFN + 4))
                act.activation(xr2[:, 2:2 + HALF], ps[:, 0, 0:HALF], ACT.Copy)
                act.activation(xr2[:, 2 + HALF:2 + NP], ps[:, 1, 0:NP - HALF], ACT.Copy)
                act.activation(xr2[:, 514:594].rearrange("p (s c) -> p s c", s=8)[:, :, 2:10],
                               ps[:, 1, NP - HALF:HALF].rearrange("p (s c) -> p s c", s=8), ACT.Copy).then_inc(g_ready, 1)
                hi_loop(6)
                hi_loop(7)
                act.wait_ge(g_sum, f + 1)
                act.wait_ge(up_done, f + 1)
                act.activation(gl[:, 0:NP], xc2[:, 0:NP], ACT.Gelu_apprx_tanh)
                act.activation(gl[:, NP:TOK].rearrange("p (s c) -> p s c", s=8),
                               xc2[:, 514:594].rearrange("p (s c) -> p s c", s=8)[:, :, 0:8], ACT.Gelu_apprx_tanh).then_inc(g_act, 1)
            join(act, 7)
            for c in range(4):
                peeled, turns = loop_units(c)
                for k in peeled:
                    down_hi(act, c, k, None)
                with act.Fori(0, turns) as i:
                    for j in range(4):
                        down_hi(act, c, 3 + j, i)
            join(act, 8)
            def fco_copy(b):
                m = min(16, FT - 16 * b) * 128
                act.wait_ge(fco_T, b + 1)
                s = 4 * (b % 2)
                act.activation(fco[:, 2048 * b:2048 * b + m], ps[0:18, s:s + 4, :].rearrange("p b c -> p (b c)")[:, 0:m], ACT.Copy).then_inc(fco_done, 1)

            for t, (t0, n) in enumerate(TILES):
                if t == 4:
                    fco_copy(0)
                s = 4 * (t % 2 if t < 4 else 1)
                act.wait_ge(xT_ready, 10 * NTT + t + 1)
                act.activation(sqj[0:n, :], ps[0:n, s:s + 4, :].rearrange("p b c -> p (b c)"), ACT.Square,
                               accum_out=small[0:n, t:t + 1]).then_inc(ss_ready, 1)
                act.wait_ge(inv_ready, 8 + t)
                act.activation(small[0:n, 5 + t:6 + t], small[0:n, 5 + t:6 + t], ACT.Sqrt).then_inc(rs_ready, 1)
            fco_copy(1)
            fco_copy(2)
            join(act, 9)

        @block.vector
        def _(dve):
            ch = Chain(dve, v_ch)
            dve.memset(small[:], 0.0).then_inc(small_zero, 1)
            dve.wait_ge(ld_const, 16)
            dve.wait_ge(ld_g, 16)
            dve.wait_ge(ss_ready, 1)
            ch(dve.tensor_scalar(rs, ss, 1.0 / D, EPS, ALU.mult, ALU.add))
            dve.reciprocal(rs, rs).then_inc(inv_ready, 1)
            dve.wait_ge(rs_ready, 1)
            for t, (t0, n) in enumerate(TILES):
                dve.scalar_tensor_tensor(xin[0:n, t, :], xin[0:n, t, :], small[0:n, 5 + t:6 + t], gb[0:n, :], ALU.mult, ALU.mult).then_inc(xn_ready, 1)
            for g in range(4 * NTT):
                t, k4 = g // 4, g % 4
                t0, n = TILES[t]
                dve.wait_ge(hT_hi_done, g + 1)
                dve.tensor_tensor(hT_lo[:, 4 * k4:4 * k4 + 4, t0:t0 + n],
                                  ps[:, g % 8, :].rearrange("p (k c) -> p k c", k=4)[:, :, 0:n],
                                  hT_hi[:, 4 * k4:4 * k4 + 4, t0:t0 + n].bitcast(F32), ALU.subtract).then_inc(hT_lo_done, 1)
            dve.wait_ge(cw_ready, 1)
            ch(dve.tensor_copy(cwT[:], ps[:, 0, 0:XT * 29].rearrange("p (k c) -> p k c", k=XT)))
            join(dve, 0)
            ch(dve.memset(xr[:, 0:3], 0.0))
            for x in range(XT):
                if x:
                    dve.wait_ge(conv_done, x)
                xs3 = xr[:, 515:603].rearrange("p (s c) -> p s c", s=8)
                dve.tensor_copy(xs3[:, :, 0:3], cwT[:, x, 0:24].rearrange("p (s c) -> p s c", s=8))
                dve.wait_ge(xr_ready, x + 1)
                dve.tensor_copy(cst[:, x, 0:3], xr[:, 512:515])
                ch(dve.tensor_copy(cst[:, x, 3:27].rearrange("p (s c) -> p s c", s=8), xs3[:, :, 8:11]))
                ch(dve.tensor_scalar(xc[:, 0:600], xr[:, 0:600], cwT[:, x, 24:25], cwT[:, x, 28:29], ALU.mult, ALU.add))
                for k in range(1, 4):
                    i = dve.scalar_tensor_tensor(xc[:, 0:600], xr[:, k:600 + k], cwT[:, x, 24 + k:25 + k], xc[:, 0:600], ALU.mult, ALU.add)
                    if k < 3:
                        ch(i)
                    else:
                        i.then_inc(acc_ready, 1)
            dve.wait_ge(acc_ready, XT)
            dve.memset(gdt[64:128, 4, :], 0.0)
            join(dve, 1)
            dve.wait_ge(ld_ssd, 64)
            ch(dve.memset(ss2, 0.0))
            ch(dve.memset(sp_[:, 48:448], 0.0))
            ch(dve.tensor_tensor(v_, gdt[:, :, 48:64], dtb.unsqueeze(1).broadcast_to([128, NTT, NH]), ALU.add))
            ch(dve.tensor_scalar(w5, v_, -1.0, None, ALU.mult))
            dve.tensor_tensor(w5, v_, w5, ALU.min).then_inc(v_ready, 1)
            dve.wait_ge(v_ready, 2)
            dve.wait_ge(l_ready, 1)
            ch(dve.scalar_tensor_tensor(dt_, v_, 0.0, w5, ALU.max, ALU.add))
            dve.scalar_tensor_tensor(a_, dt_, -1.0, eA.unsqueeze(1).broadcast_to([128, NTT, NH]), ALU.mult, ALU.mult).then_inc(a_ready, 1)
            dve.wait_ge(sums_ready, 1)
            for rows, ts in ((128, slice(0, 4)), (64, slice(4, 5))):
                m = ts.stop - ts.start
                S = ps[0:rows, 7, 32 * ts.start:32 * ts.stop].rearrange("p (t x h) -> p t x h", t=m, x=2)
                dve.tensor_copy(acs[0:rows, ts], S[:, :, 0])
                ch(dve.tensor_copy(eac[0:rows, ts], S[:, :, 0]))
                dve.tensor_copy(eto[0:rows, ts], S[:, :, 1])
                ch(dve.tensor_tensor(ete[0:rows, ts], S[:, :, 1], eac[0:rows, ts], ALU.subtract))
            dve.drain().then_inc(sum_ready, 1)
            for p in range(8):
                dve.wait_ge(exps_ready, 1)
                dve.wait_ge(yoff_ready, p + 1)
                dve.tensor_tensor(yoff[:, 128 * p:128 * p + 128].rearrange("c (h p) -> c h p", h=2),
                                  ps[0:64, 6, 0:128].rearrange("c (h p) -> c h p", h=2),
                                  bc(eac[0:64, 4, 2 * p:2 * p + 2], [64, 2, 64]), ALU.mult).then_inc(yoff_evac, 1)
                dve.wait_ge(dec_ready, p + 1)
                dve.wait_ge(h0_loaded[p % 2], 16 * (p // 2 + 1))
                ch(dve.tensor_tensor(h0r[:, p % 2], h0r[:, p % 2], bc(dec[:, p % 2, :], [128, NB, 128]), ALU.mult))
                dve.wait_ge(newps_ready, p + 1)
                dve.tensor_tensor(h0r[:, p % 2].rearrange("p (a s) n -> p a (s n)", a=2),
                                  h0r[:, p % 2].rearrange("p (a s) n -> p a (s n)", a=2), ps[:, 4:6, :], ALU.add).then_inc(new_ready, 1)

            def seg_unit(w):
                t, g = w // 4, w % 4
                n = TILES[t][1]
                dve.wait_ge(s1_ready, w + 1)
                if w >= 2:
                    dve.wait_ge(y_ready, w - 1)
                mask = con[0:n, C_CB:C_CB + n] if t < 4 else con[0:n, C_CBS:C_CBS + n]
                for h in range(4):
                    i = dve.scalar_tensor_tensor(seg[0:n, w % 2, h, 0:n], ps[0:n, 2 + w % 2, 128 * h:128 * h + n],
                                                 acs[0:n, t, 4 * g + h:4 * g + h + 1], mask, ALU.subtract, ALU.add)
                i.then_inc(seg_ready, 1)

            def mix_unit(w):
                t, g = w // 4, w % 4
                n = TILES[t][1]
                dve.wait_ge(dec_exp, w + 1)
                dve.tensor_tensor(seg[0:n, w % 2, :, 0:n], seg[0:n, w % 2, :, 0:n],
                                  ps[0:n, w % 2, 0:n].unsqueeze(1).broadcast_to([n, 4, n]), ALU.mult).then_inc(M_done, 1)

            def out_unit(w):
                t, g = w // 4, w % 4
                n = TILES[t][1]
                dve.wait_ge(y_ready, w + 1)
                y = xsk[0:n, t, 256 * g:256 * g + 256]
                hv = lambda ap: ap.rearrange("c (h p) -> c h p", h=4)
                if 1 <= t <= 3:
                    dve.tensor_tensor(hv(tmp2[0:n, :]), hv(ps[0:n, 5, 0:256]), bc(eac[0:n, t, 4 * g:4 * g + 4], [n, 4, 64]), ALU.mult)
                ch(dve.tensor_tensor(hv(y), hv(y), bc(dsk[0:n, 4 * g:4 * g + 4], [n, 4, 64]), ALU.mult))
                ch(dve.tensor_tensor(y, y, ps[0:n, 4, 0:256], ALU.add))
                if t >= 1:
                    ch(dve.tensor_tensor(y, y, tmp2[0:n, :] if t < 4 else yoff[:, 256 * g:256 * g + 256], ALU.add))
                H = hst[:, 256 * g:256 * g + 256]
                if t == 0:
                    dve.tensor_copy(H, ps[:, 6, 0:256])
                elif t < 4:
                    ch(dve.tensor_tensor(hv(H), hv(H), bc(eto[:, t, 4 * g:4 * g + 4], [128, 4, 64]), ALU.mult))
                    dve.tensor_tensor(H, H, ps[:, 6, 0:256], ALU.add)
                z = zs[0:n, t, 256 * g:256 * g + 256]
                ch(dve.tensor_tensor(z, y, z, ALU.mult))
                dve.drain().then_inc(unit_done, 1)

            for w in range(21):
                if w < 20:
                    seg_unit(w)
                if w >= 1:
                    out_unit(w - 1)
                if w < 20:
                    mix_unit(w)
            dve.wait_ge(fin_T, 1)
            for b in range(2):
                dve.wait_ge(h0_stored[b], 64)
            dve.tensor_copy(cso[:].rearrange("p (b c) -> p b c", b=4), ps[0:27, 0:4, :]).then_inc(fin_copied, 1)
            dve.tensor_copy(hso[:].rearrange("p (a s) n -> p a (s n)", a=2), ps[:, 4:6, :]).then_inc(fin_copied, 1)
            dve.wait_ge(ss2_ready, 20)
            ch(dve.tensor_scalar(ss2, ss2, 1.0 / 256, EPS, ALU.mult, ALU.add))
            dve.reciprocal(ss2, ss2).then_inc(inv2, 1)
            dve.wait_ge(rs2, 1)
            for t, (t0, n) in enumerate(TILES):
                for g in range(4):
                    z = zs[0:n, t, 256 * g:256 * g + 256]
                    dve.scalar_tensor_tensor(z, z, sp_[0:n, 448 + 4 * t + g:449 + 4 * t + g], ngb[0:n, 256 * g:256 * g + 256], ALU.mult, ALU.mult)
            join(dve, 2)
            dve.memset(cs[32:33, 360:376], 1.0).then_inc(tab_set, 1)
            dve.memset(nb[:], MASKED).then_inc(nb_set, 1)
            dve.wait_ge(ld_c, 16 * 10)
            dve.wait_ge(pb_mm, 1)
            dve.tensor_tensor(hb, ps[:, 7, 0:2], b1t, ALU.add).then_inc(hb_ready, 1)
            for c, (s0, ns) in enumerate(CH):
                dve.wait_ge(vc_ready, c + 1)
                dve.tensor_tensor(vc[:, s0:s0 + ns].rearrange("n s (g d) -> n (s g) d", g=4),
                                  ps[0:NCMP, 5:7, :].rearrange("n a (s d) -> n (a s) d", d=64)[:, 0:4 * ns],
                                  b2v.unsqueeze(1).broadcast_to([NCMP, 4 * ns, 64]), ALU.add).then_inc(vc_evac, 1)
            join(dve, 3)
            for gp in range(2):
                for r in range(4):
                    i = dve.tensor_copy(qs[:, gp, :, 8 * r:8 * r + 8], qT[:, 4 * gp + r, NP:TOK].rearrange("p (s t) -> p s t", s=NB))
            i.then_inc(qs_ready, 1)
            dve.wait_ge(ld_b, 16 * 2 * NH)
            ch(dve.tensor_copy(sb_[:, 1, :], sb_[:, 0, :]))
            ch(dve.tensor_tensor(sb_[:, 1, 0:8], sb_[:, 1, 0:8], con[:, C_WM:C_WM + 8], ALU.add))
            dve.wait_ge(sc_mm, 1)
            sx = ps[:, 3, 0:NB * NCMP].rearrange("p (s n) -> p s n", s=NB)
            ch(dve.tensor_tensor(scc[:], sx, sb_[:, 0, 31:512:16].unsqueeze(1).broadcast_to([128, NB, NCMP]), ALU.add))
            ch(dve.tensor_reduce(m8, scc[:], AX.X, ALU.min))
            dve.tensor_tensor(scc[:], scc[:], bc(m8, [128, NB, NCMP]), ALU.subtract).then_inc(pc_sub, 1)
            dve.wait_ge(pc_exp, 1)
            ch(dve.tensor_reduce(r8, scc[:], AX.X, ALU.add))
            ch(dve.tensor_scalar(r8, r8, TINY, None, ALU.max))
            ch(dve.reciprocal(r8, r8))
            dve.tensor_tensor(scc[:], scc[:], bc(r8, [128, NB, NCMP]), ALU.mult).then_inc(pc_ready, 1)
            dve.wait_ge(pc_ready, 1)
            dve.wait_ge(ld_gs, 16)
            dve.tensor_tensor(scg[:], scc[:], gsm[:, :, 0:1].broadcast_to([128, NB, NCMP]), ALU.mult).then_inc(pcg_ready, 1)
            dve.wait_ge(imp_mm, 1)
            dve.tensor_copy(imp.rearrange("p s b -> p (s b)"), ps[:, 2, 0:72]).then_inc(imp_ready, 1)
            dve.wait_ge(imp2_mm, 1)
            ch(dve.tensor_copy(d1, ps[:, 3, 0:72].rearrange("p (s b) -> p s b", s=NB)[:, :, 1:7]))
            ch(dve.tensor_reduce(m8, d1, AX.X, ALU.min))
            ch(dve.tensor_tensor(d1, d1, bc(m8, [128, NB, 6]), ALU.is_equal))
            iota = con[:, C_IOTA:C_IOTA + 6].unsqueeze(1).broadcast_to([128, NB, 6])
            ch(dve.tensor_tensor(d1, d1, iota, ALU.mult))
            ch(dve.tensor_reduce(m8, d1, AX.X, ALU.max))
            ch(dve.tensor_tensor(d1, bc(m8, [128, NB, 6]), iota, ALU.is_equal))
            ch(dve.tensor_scalar(drop, d1, MASKED, None, ALU.mult))
            dve.drain().then_inc(drop_ready, 1)

            def s_first(y):
                s, br = y // 2, y % 2
                S = scs[:, y % 2, :]
                dve.wait_ge(s_mm, y + 1)
                if y >= 2:
                    dve.wait_ge(pT_mm, y - 1)
                if br == 0:
                    dve.wait_ge(sbd_ready, s + 1)
                bias = sbd[:, s % 2, :] if br == 0 else sb_[:, 1, :]
                ch(dve.tensor_tensor_reduce(out=S[:, 0:512], in0=ps[:, 2 * (y % 2), :], in1=bias, scale=1.0, scalar=CLAMP,
                                            op0=ALU.add, op1=ALU.min, accum_out=st_[:, y % 2, 2:3]))
                dve.tensor_tensor_reduce(out=S[:, 512:576], in0=ps[:, 1, 0:64], in1=nb[:, 56 - 8 * s:120 - 8 * s], scale=1.0,
                                         scalar=st_[:, y % 2, 2:3], op0=ALU.add, op1=ALU.min, accum_out=st_[:, y % 2, 0:1]).then_inc(s_max, 1)

            def s_second(y):
                s, br = y // 2, y % 2
                dve.wait_ge(s_exp, y + 1)
                ch(dve.tensor_scalar(st_[:, y % 2, 3:4], st_[:, y % 2, 1:2], TINY, None, ALU.max))
                ch(dve.reciprocal(st_[:, y % 2, 3:4], st_[:, y % 2, 3:4]))
                dve.tensor_scalar(scs[:, y % 2, :], scs[:, y % 2, :], st_[:, y % 2, 3:4], gsm[:, s, 1 + br:2 + br], ALU.mult, ALU.mult).then_inc(s_p, 1)

            def s_out(s):
                dve.wait_ge(pv_mm, 2 * s + 2)
                if s >= 2:
                    dve.wait_ge(oT_mm, s - 1)
                for g in range(NG):
                    i = dve.tensor_copy(osb[32 * g:32 * g + 32, s % 2, :], ps[32 * g:32 * g + 32, 3, 64 * g:64 * g + 64])
                i.then_inc(o_ready, 1)
                dve.wait_ge(oT_mm, s + 1)
                for par in range(2):
                    i = dve.tensor_copy(mixA[64 * par:64 * par + 64, :, NP + 8 * s:NP + 8 * s + 8],
                                        ps[0:64, 3, 256:384].rearrange("d (h q t) -> d h q t", q=2, t=8)[:, :, par, :])
                i.then_inc(oT_evac, 1)

            for y in range(19):
                if y < 16:
                    s_first(y)
                    s_second(y)
                if y >= 4 and y % 2 == 0:
                    s_out((y - 4) // 2)
            join(dve, 4)
            dve.wait_ge(ld_TT, 16)
            dve.memset(cmb[:], MASKED).then_inc(v_ready, 1)
            dve.wait_ge(v_ready, 3)
            for i in range(4):
                n = 7 + 8 * i
                last = dve.tensor_copy(cmb[:, :, i, 0:n], TT[:, :, 415 - 128 * i:512:16])
            ch(last)
            for b in range(4):
                B = slice(4 * b, 4 * b + 4)
                dve.wait_ge(C_mm, b + 1)
                ch(dve.tensor_tensor(pcp[:, B], ps[:, b, 0:496].rearrange("p (h i n) -> p h i n", h=4, i=4), cmb[:, B], ALU.add))
                ch(dve.tensor_reduce(cm[:, B], pcp[:, B], AX.X, ALU.min))
                ch(dve.tensor_scalar(cm[:, B], cm[:, B], CLAMP, None, ALU.min))
                dve.tensor_tensor(pcp[:, B], pcp[:, B], bc(cm[:, B], [128, 4, 4, NCMP]), ALU.subtract).then_inc(C_sub, 1)
            for b in range(4):
                B = slice(4 * b, 4 * b + 4)
                dve.wait_ge(C_exp, b + 1)
                ch(dve.tensor_reduce(cm[:, B], pcp[:, B], AX.X, ALU.add))
                ch(dve.tensor_scalar(cm[:, B], cm[:, B], TINY, None, ALU.max))
                ch(dve.reciprocal(cm[:, B], cm[:, B]))
                ch(dve.tensor_tensor(cm[:, B], cm[:, B], gdt[:, 0:4, B].rearrange("p i h -> p h i"), ALU.mult))
                dve.tensor_tensor(pcp[:, B], pcp[:, B], bc(cm[:, B], [128, 4, 4, NCMP]), ALU.mult).then_inc(C_p, 1)
            for P in range(NPAIR + 6):
                if P < NPAIR:
                    h, i = P // 4, P % 4
                    n, k = 128 * (i + 1), 8 * (P % 2)
                    if P >= 2:
                        dve.wait_ge(P_T, turn(P - 2, 1) + 1)
                    for br in range(2):
                        w = 2 * P + br
                        dve.wait_ge(P_mm, w + 1)
                        dve.tensor_tensor_reduce(out=scp[w % 4][:, 0:n], in0=ps[:, w % 4, 0:n], in1=TT[:, h, 384 - 128 * i:512], scale=1.0,
                                                 scalar=CLAMP, op0=ALU.add, op1=ALU.min, accum_out=ast[:, k + br:k + br + 1]).then_inc(P_min, 1)
                    dve.wait_ge(P_exp, 2 * P + 2)
                    r = ast[:, k + 4:k + 6]
                    ch(dve.tensor_scalar(r, ast[:, k + 2:k + 4], TINY, None, ALU.max))
                    ch(dve.reciprocal(r, r))
                    for br in range(2):
                        w, gate = 2 * P + br, 16 * (br + 1) + h
                        dve.tensor_scalar(scp[w % 4][:, 0:n], scp[w % 4][:, 0:n], ast[:, k + 4 + br:k + 5 + br], gdt[:, i, gate:gate + 1],
                                          ALU.mult, ALU.mult).then_inc(P_p, 1)
                if P >= 9 and P % 4 == 1:
                    prompt_out(dve, (P - 9) // 4)
            join(dve, 5)
            for k in range(8):
                dve.wait_ge(ms_hi, k + 1)
                dve.tensor_tensor(hT_lo[:, k, :], mixA[:, k, :], hT_hi[:, k, :].bitcast(F32), ALU.subtract).then_inc(ms_lo, 1)
            for e in range(2 * NTT):
                t, k4 = e // 2, e % 2
                t0, n = TILES[t]
                dve.wait_ge(hT_hi_done, 4 * NTT + e + 1)
                dve.tensor_tensor(hT_lo[:, 8 + 4 * k4:12 + 4 * k4, t0:t0 + n], ps[:, e % 8, :].rearrange("p (k c) -> p k c", k=4)[:, :, 0:n],
                                  hT_hi[:, 8 + 4 * k4:12 + 4 * k4, t0:t0 + n].bitcast(F32), ALU.subtract).then_inc(hT_lo_done, 1)
            dve.wait_ge(ss_ready, 2)
            ch(dve.tensor_reduce(ss, ssc, AX.X, ALU.add))
            ch(dve.tensor_scalar(rs, ss, 1.0 / D, EPS, ALU.mult, ALU.add))
            dve.reciprocal(rs, rs).then_inc(inv_ready, 1)
            dve.wait_ge(rs_ready, 2)
            dve.wait_ge(ld_g, 48)
            for i in range(NTT + 2):
                if i < NTT:
                    n = TILES[i][1]
                    dve.scalar_tensor_tensor(mo[0:n, i, :], mo[0:n, i, :], small[0:n, 5 + i:6 + i], gb[0:n, :], ALU.mult, ALU.mult).then_inc(xn_ready, 1)
                if 1 <= i <= NTT:
                    n = TILES[i - 1][1]
                    r = small[0:n, 4 + i:5 + i]
                    dve.wait_ge(ss_ready, 2 + i)
                    ch(dve.tensor_scalar(r, small[0:n, i - 1:i], 1.0 / D, EPS, ALU.mult, ALU.add))
                    dve.reciprocal(r, r).then_inc(inv_ready, 1)
                    dve.wait_ge(rs_ready, 2 + i)
                    dve.scalar_tensor_tensor(mo[0:n, i - 1, :], xin[0:n, i - 1, :], r, gb2[0:n, :], ALU.mult, ALU.mult).then_inc(x2n_ready, 1)
                if i >= 2:
                    t0, n = TILES[i - 2]
                    for k4 in range(4):
                        g = 4 * (i - 2) + k4
                        dve.wait_ge(hT_hi_done, 6 * NTT + g + 1)
                        dve.tensor_tensor(hT_lo[:, 4 * k4:4 * k4 + 4, t0:t0 + n],
                                          ps[:, g % 8, :].rearrange("p (k c) -> p k c", k=4)[:, :, 0:n],
                                          hT_hi[:, 4 * k4:4 * k4 + 4, t0:t0 + n].bitcast(F32), ALU.subtract).then_inc(hT_lo_done, 1)
            dve.wait_ge(fw_T, 1)
            for b0, b1, j0, j1 in ((0, 4, 0, 6), (0, 4, 6, 10), (0, 3, 10, 11)):
                bank, jj = 4 + j0 // 6, j0 % 6
                src = ps[:, bank, 80 * jj:80 * (jj + j1 - j0)].rearrange("p (j b r) -> p b j r", b=4, r=20)[:, b0:b1]
                for b in range(b0, b1):
                    dve.tensor_copy(fwT[:, FB * b + j0:FB * b + j1, :], src[:, b - b0])
            dve.memset(xr2[:, 0:2], 0.0)
            dve.wait_ge(x2_stored, 16 * NTT)
            join(dve, 6)
            dve.drain().then_inc(up_done, 1)
            with dve.Fori(0, FT) as f:
                P = lambda m: fwT[:, bass.ds(f, 1), m:m + 1].rearrange("p a c -> p (a c)")
                x3 = xr2[:, 514:594].rearrange("p (s c) -> p s c", s=8)
                dve.tensor_copy(x3[:, :, 0:2], fwT[:, bass.ds(f, 1), 0:16].rearrange("p a (s c) -> p (a s) c", s=8))
                dve.wait_ge(g_ready, f + 2)
                dve.wait_ge(g_act, f + 1)
                dve.tensor_copy(fst[:, bass.ds(f, 1), 0:2].rearrange("p a c -> p (a c)"), xr2[:, 512:514])
                dve.tensor_copy(fst[:, bass.ds(f, 1), 2:18].rearrange("p a (s c) -> p (a s) c", s=8), x3[:, :, 8:10]).then_inc(f_ch, 1)
                dve.wait_ge(f_ch, f * 3 + 1)
                dve.tensor_scalar(xc2[:, 0:592], xr2[:, 0:592], P(16), P(19), ALU.mult, ALU.add).then_inc(f_ch, 1)
                dve.wait_ge(f_ch, f * 3 + 2)
                dve.scalar_tensor_tensor(xc2[:, 0:592], xr2[:, 1:593], P(17), xc2[:, 0:592], ALU.mult, ALU.add).then_inc(f_ch, 1)
                dve.wait_ge(f_ch, f * 3 + 3)
                dve.scalar_tensor_tensor(xc2[:, 0:592], xr2[:, 2:594], P(18), xc2[:, 0:592], ALU.mult, ALU.add).then_inc(g_sum, 1)
                dve.wait_ge(g_act, f + 2)
                dve.wait_ge(pe_unit, f * 8 + (U_FFN + 8))
                dve.tensor_tensor(acT[:, bass.ds(f, 1), :].rearrange("p a (h c) -> p (a h) c", h=2), gl[:].rearrange("p (h c) -> p h c", h=2),
                                  ps[:, 2:4, 0:HALF], ALU.mult).then_inc(up_done, 1)
            join(dve, 7)
            for c in range(5):
                if c < 4:
                    peeled, turns = loop_units(c)
                    down_lo(dve, c, 0, None)
                    down_lo(dve, c, 1, None)
                if c:
                    dve.wait_ge(pe_unit, U_DOWN + FT * c)
                    for b in range(8):
                        dve.tensor_copy(yT[:, 4 * (c - 1) + b // 2, HALF * (b % 2):HALF * (b % 2) + HALF], ps[:, b, 0:HALF]).then_inc(y_evac, 1)
                if c < 4:
                    down_lo(dve, c, 2, None)
                    with dve.Fori(0, turns) as i:
                        for j in range(4):
                            down_lo(dve, c, 3 + j, i)
            join(dve, 8)
            dve.wait_ge(ld_x, 16 * (3 * NTT + 1))
            for t, (t0, n) in enumerate(TILES):
                b = 4 * (t % 2 if t < 4 else 1)
                r = small[0:n, 5 + t:6 + t]
                dve.wait_ge(ss_ready, 8 + t)
                ch(dve.tensor_scalar(r, small[0:n, t:t + 1], 1.0 / D, EPS, ALU.mult, ALU.add))
                dve.reciprocal(r, r).then_inc(inv_ready, 1)
                dve.wait_ge(rs_ready, 8 + t)
                dve.scalar_tensor_tensor(yn[0:n, t % 2, :], ps[0:n, b:b + 4, :].rearrange("p b c -> p (b c)"), r, gb3[0:n, :],
                                         ALU.mult, ALU.mult).then_inc(y_used, 1)
                dve.wait_ge(y_used, t + 1)
                dve.tensor_tensor(x2r[0:n, t, :], yn[0:n, t % 2, :], x2r[0:n, t, :], ALU.add).then_inc(fin_y, 1)
            join(dve, 9)

        @block.gpsimd
        def _(pool):
            join(pool, 0)
            with pool.Fori(0, U_GD // 4) as i:
                for j in range(4):
                    pool.wait_ge(hi_done, i * 4 + (j + 1))
                    pool.tensor_tensor(w_lo[:, j % 2, :], w_raw[:, j, :], w_hi[:, j % 2, :].bitcast(F32), ALU.subtract).then_inc(lo_done, 1)
            for u in range(U_GD, U_GD + 2):
                pool.wait_ge(hi_done, u + 1)
                pool.tensor_tensor(w_lo[:, u % 2, :], w_raw[:, u % 4, :], w_hi[:, u % 2, :].bitcast(F32), ALU.subtract).then_inc(lo_done, 1)
            join(pool, 1)
            def x_scaled(k, t, n, sl, both):
                if k >= 2:
                    t_old = [4, 0, 1, 2, 3, 4][k - 2]
                    pool.wait_ge(y_ready, 4 * (t_old + 1)) if k > 2 else pool.wait_ge(newps_ready, 8)
                xh = lambda ap: ap.rearrange("c (h p) -> c h p", h=NH)
                pool.tensor_tensor(xh(xdt[0:n, sl, :]), xh(xsk[0:n, t, :]), bc(dt_[0:n, t, :], [n, NH, 64]), ALU.mult).then_inc(pool_ch, 1)
                pool.wait_ge(pool_ch, k + 1)
                pool.tensor_tensor(xh(xte[0:n, sl, :]), xh(xdt[0:n, sl, :]), bc(ete[0:n, t, :], [n, NH, 64]), ALU.mult).then_inc(xt_ready, 1)

            pool.wait_ge(tokT_evac, 15)
            pool.wait_ge(exps_ready, 1)
            x_scaled(0, 4, 64, 0, True)
            x_scaled(1, 0, 128, 1, True)
            for g in range(NG):
                if g:
                    pool.wait_ge(newps_ready, 2 * g)
                pool.tensor_tensor(bex[:], Bk[0:64, 4, 128 * g:128 * g + 128].unsqueeze(1).broadcast_to([64, NB, 128]),
                                   bc(con[0:64, C_SEQ:C_SEQ + 8], [64, NB, 128]), ALU.mult).then_inc(bexp_ready, 1)
            for t in range(1, 5):
                x_scaled(t + 1, t, TILES[t][1], (t + 1) % 2, True)
            join(pool, 2)
            join(pool, 3)
            pool.wait_ge(ld_b, 16 * 2 * NH)
            pool.wait_ge(drop_ready, 1)
            for s in range(NB):
                if s >= 2:
                    pool.wait_ge(s_max, 2 * s - 3)
                pool.tensor_copy(sbd[:, s % 2, 0:64], sb_[:, 0, 0:64])
                pool.tensor_copy(sbd[:, s % 2, 448:512], sb_[:, 0, 448:512])
                v = lambda ap: ap[:, 64:448].rearrange("p (b k) -> p b k", b=6)
                pool.tensor_tensor(v(sbd[:, s % 2, :]), v(sb_[:, 0, :]), bc(drop[:, s, :], [128, 6, 64]), ALU.add)
                pool.drain().then_inc(sbd_ready, 1)
            join(pool, 4)
            join(pool, 5)

            def lo_loop(u0, turns):
                with pool.Fori(0, turns) as i:
                    for j in range(4):
                        u = u0 + j
                        pool.wait_ge(hi_done, i * 4 + (u + 1))
                        pool.tensor_tensor(w_lo[:, u % 2, :], w_raw[:, u % 4, :], w_hi[:, u % 2, :].bitcast(F32), ALU.subtract).then_inc(lo_done, 1)

            lo_loop(U_OUT, KT)
            pool.wait_ge(ld_x, 32 * NTT)
            for t, (t0, n) in enumerate(TILES):
                pool.wait_ge(xn_ready, NTT + t + 1)
                pool.tensor_tensor(xin[0:n, t, :], xin[0:n, t, :], mo[0:n, t, :], ALU.add).then_inc(x2_ready, 1)
            join(pool, 6)
            lo_loop(U_FFN, 2 * FT)
            join(pool, 7)
            lo_loop(U_DOWN, FT)
            join(pool, 8)
            join(pool, 9)

        @block.tensor
        def _(pe):
            pe.wait_ge(ld_const, 16)
            for g in range(4 * NTT):
                t, k4 = g // 4, g % 4
                t0, n = TILES[t]
                if k4 == 0:
                    pe.wait_ge(xn_ready, t + 1)
                if g >= 8:
                    pe.wait_ge(hT_lo_done, g - 7)
                for k in range(4):
                    i = pe.transpose(ps[:, g % 8, 128 * k:128 * k + n], xin[0:n, t, 128 * (4 * k4 + k):128 * (4 * k4 + k) + 128], ident[0:n, 0:n])
                i.then_inc(xT_ready, 1)
            pe.wait_ge(ld_cw, 48)
            pe.wait_ge(hT_lo_done, 4 * NTT)
            for k in range(XT):
                i = pe.transpose(ps[:, 0, 29 * k:29 * k + 29], cwst[0:29, 128 * k:128 * k + 128], ident[0:29, 0:29])
            i.then_inc(cw_ready, 1)
            join(pe, 0)

            def feat_tile(f, bank, u0, base, first_wait):
                for j in range(4):
                    pe.wait_ge(lo_done, u0 + (j + 1))
                    for kk in range(4):
                        k = 4 * j + kk
                        s = (base + j) % 2
                        for h in range(2):
                            o = ps[:, bank + h, 0:HALF]
                            W = [w_hi[:, s, 128 * kk:128 * kk + 128], w_lo[:, s, 128 * kk:128 * kk + 128]]
                            X = [hT_hi[:, k, HALF * h:HALF * h + HALF], hT_lo[:, k, HALF * h:HALF * h + HALF]]
                            pe.matmul(o, W[0], X[0], start=(k == 0), stop=False)
                            pe.matmul(o, W[0], X[1], start=False, stop=False)
                            i = pe.matmul(o, W[1], X[0], start=False, stop=(k == KT - 1))
                    i.then_inc(pe_unit, 1)

            for f in range(2):
                feat_tile(f, 2 * f, 4 * f, 0, None)
            with pe.Fori(1, 12) as i:
                for f in range(2):
                    pe.wait_ge(feat_evac, i * 2 + (f - 1))
                    feat_tile(f, 2 * f, i * 8 + 4 * f, 0, None)
            pe.wait_ge(feat_evac, 24)

            def token_unit(u, k, first, last_):
                pe.wait_ge(lo_done, u + 1)
                for t, (t0, n) in enumerate(TILES):
                    o = ps[0:n, t, :]
                    X = [hT_hi[:, k, t0:t0 + n], hT_lo[:, k, t0:t0 + n]]
                    W = [w_hi[:, u % 2, :], w_lo[:, u % 2, :]]
                    if first is not None and k == 0 and first > 0:
                        pe.wait_ge(tok_evac, 5 * (first - 1) + t + 1)
                    pe.matmul(o, X[0], W[0], start=(k == 0), stop=False)
                    pe.matmul(o, X[1], W[0], start=False, stop=False)
                    i = pe.matmul(o, X[0], W[1], start=False, stop=last_)
                i.then_inc(pe_unit, 1)

            for c in range(5):
                for k in range(KT):
                    token_unit(U_KV + KT * c + k, k, c, k == KT - 1)
            pe.wait_ge(lo_done, U_GD + 2)
            for t, (t0, n) in enumerate(TILES):
                o = ps[0:n, 5, 64 * t:64 * t + 64]
                for k in range(KT):
                    s, kk = (U_GD + k // 8) % 2, k % 8
                    X = [hT_hi[:, k, t0:t0 + n], hT_lo[:, k, t0:t0 + n]]
                    W = [w_hi[:, s, 64 * kk:64 * kk + 64], w_lo[:, s, 64 * kk:64 * kk + 64]]
                    pe.matmul(o, X[0], W[0], start=(k == 0), stop=False)
                    pe.matmul(o, X[1], W[0], start=False, stop=False)
                    i = pe.matmul(o, X[0], W[1], start=False, stop=(k == KT - 1))
            i.then_inc(pe_unit, 2)
            join(pe, 1)
            for G in range(3 * NTT):
                t, b = G // 3, G % 3
                t0, n = TILES[t]
                if G >= 6:
                    pe.wait_ge(tokT_evac, G - 5)
                for k in range(4):
                    i = pe.transpose(ps[0:n, G % 6, 128 * k:128 * k + 128], xbcT[:, 4 * b + k, t0:t0 + n], ident)
                i.then_inc(tokT_ready, 1)
            pe.wait_ge(a_ready, 1)
            for t, (t0, n) in enumerate(TILES):
                tri = con[0:n, C_TRI:C_TRI + n] if t < 4 else con[0:n, C_TRIS:C_TRIS + n]
                one = con[0:n, C_ONE:C_ONE + n] if t < 4 else con[0:n, C_BLK:C_BLK + n]
                pe.matmul(ps[0:n, 7, 32 * t:32 * t + 16], tri, a_[0:n, t, :], start=True, stop=True)
                i = pe.matmul(ps[0:n, 7, 32 * t + 16:32 * t + 32], one, a_[0:n, t, :], start=True, stop=True)
            i.then_inc(sums_ready, 1)
            pe.wait_ge(tokT_evac, 15)
            for p in range(8):
                g = p // 2
                pe.wait_ge(h0_loaded[p % 2], 16 * (p // 2 + 1))
                if p:
                    pe.wait_ge(h0T_evac, p)
                for s in range(NB):
                    i = pe.transpose(ps[:, s // 4, 128 * (s % 4):128 * (s % 4) + 128], h0r[:, p % 2, s, :], ident)
                i.then_inc(h0T_ready, 1)
                pe.wait_ge(h0T_evac, p + 1)
                if p:
                    pe.wait_ge(dec_ready, p)
                for s in range(NB):
                    pe.matmul(ps[:, 2, 8 * s:8 * s + 8], h0T[:, s, :], xbcT[:, 12 + g, NP + 8 * s:NP + 8 * s + 8], start=True, stop=True)
                for h in range(2):
                    i = pe.matmul(ps[64 * h:64 * h + 64, 3, 0:8], a_[0:64, 4, 2 * p + h:2 * p + h + 1].broadcast_to([64, 64]),
                                  con[0:64, C_SEQ:C_SEQ + 8], start=True, stop=True)
                i.then_inc(yo_ready, 1)
                pe.wait_ge(yoT_evac, p + 1)
                if p:
                    pe.wait_ge(yoff_evac, p)
                pe.transpose(ps[0:64, 6, 0:128], yoT[:], ident).then_inc(yoff_ready, 1)
                pe.wait_ge(bexp_ready, g + 1)
                pe.wait_ge(xt_ready, 1)
                if p:
                    pe.wait_ge(new_ready, p)
                for hf in range(2):
                    i = pe.matmul(ps[:, 4 + hf, :], xte[0:64, 0, 128 * p:128 * p + 128],
                                  bex[:, 4 * hf:4 * hf + 4, :].rearrange("j s n -> j (s n)"), start=True, stop=True)
                i.then_inc(newps_ready, 1)
            pe.wait_ge(new_ready, 8)
            pe.wait_ge(yoff_evac, 8)

            def ssd_scores(w):
                t, g = w // 4, w % 4
                t0, n = TILES[t]
                tri = con[0:n, C_TRI:C_TRI + n] if t < 4 else con[0:n, C_TRIS:C_TRIS + n]
                if w >= 2:
                    pe.wait_ge(M_done, w - 1)
                pe.matmul(ps[0:n, w % 2, 0:n], xbcT[:, 8 + g, t0:t0 + n], xbcT[:, 12 + g, t0:t0 + n], start=True, stop=True)
                for h in range(4):
                    i = pe.matmul(ps[0:n, 2 + w % 2, 128 * h:128 * h + n], a_[0:n, t, 4 * g + h:4 * g + h + 1].broadcast_to([n, n]), tri, start=True, stop=True)
                i.then_inc(s1_ready, 1)

            def ssd_out(w):
                t, g = w // 4, w % 4
                t0, n = TILES[t]
                sl = (t + 1) % 2
                pe.wait_ge(M_done, w + 1)
                pe.wait_ge(xt_ready, t + 2)
                if w:
                    pe.wait_ge(unit_done, w)
                for h in range(4):
                    i = pe.matmul(ps[0:n, 4, 64 * h:64 * h + 64], seg[0:n, w % 2, h, 0:n],
                                  xdt[0:n, sl, 256 * g + 64 * h:256 * g + 64 * h + 64], start=True, stop=True)
                if 1 <= t <= 3:
                    i = pe.matmul(ps[0:n, 5, 0:256], xbcT[:, 12 + g, t0:t0 + n], hst[:, 256 * g:256 * g + 256], start=True, stop=True)
                if t <= 3:
                    i = pe.matmul(ps[:, 6, 0:256], Bk[0:n, t, 128 * g:128 * g + 128], xte[0:n, sl, 256 * g:256 * g + 256], start=True, stop=True)
                i.then_inc(y_ready, 1)

            ssd_scores(0)
            for w in range(20):
                if w + 1 < 20:
                    ssd_scores(w + 1)
                ssd_out(w)
            pe.wait_ge(unit_done, 20)
            for k in range(XT):
                pe.transpose(ps[0:27, k // 4, 128 * (k % 4):128 * (k % 4) + 128], cst[:, k, :], ident)
            for k in range(8):
                i = pe.transpose(ps[:, 4 + k // 4, 128 * (k % 4):128 * (k % 4) + 128], hst[:, 128 * k:128 * k + 128], ident)
            i.then_inc(fin_T, 1)
            join(pe, 2)
            pe.wait_ge(ld_c, 16 * 10)
            pe.wait_ge(tab_set, 1)
            pe.matmul(ps[0:NH, 0, :], tab, oh[:, 0:512], start=True, stop=True)
            pe.matmul(ps[0:NH, 1, 0:BL - 512], tab, oh[:, 512:BL], start=True, stop=True).then_inc(rb_mm, 1)
            pe.transpose(ps[:, 2, 0:32], pes, ident[0:32, 0:32]).then_inc(pe_T, 1)
            pe.wait_ge(peT_ready, 1)
            for a in range(2):
                for k in range(16):
                    i = pe.matmul(ps[:, 7, a:a + 1], w1p[:, a, k, :], peT[:, 16 * a + k:16 * a + k + 1], start=(k == 0), stop=(k == 15))
            i.then_inc(pb_mm, 1)
            pe.wait_ge(rb_ready, 1)
            e = 0
            for c, (s0, ns) in enumerate(CH):
                for s in range(ns):
                    pe.wait_ge(craw_loaded[(s0 + s) % 2], 128 * ((s0 + s) // 2 + 1))
                    for b in range(4):
                        if e >= 2:
                            pe.wait_ge(pairT_evac, e - 1)
                        for g in range(4):
                            i = pe.transpose(ps[:, e % 2, 128 * g:128 * g + 128],
                                             craw[:, (s0 + s) % 2, b // 2, b % 2, g].rearrange("i q d -> i (q d)"), ident)
                        i.then_inc(pairT_ready, 1)
                        e += 1
                pe.wait_ge(pairT_evac, e)
                for a in range(2):
                    if c:
                        pe.wait_ge(gelu_done, 2 * c)
                    for k in range(16):
                        i = pe.matmul(ps[:, 2 + a, 0:124 * ns], w1p[:, a, k, :],
                                      kvp[:, a, 0:ns, :, k:k + 241:8].rearrange("p s g n -> p (s g) n"), start=(k == 0), stop=(k == 15))
                    i.then_inc(hid_ready, 1)
                pe.wait_ge(gelu_done, 2 * c + 1)
                if c:
                    pe.wait_ge(kc_evac, c)
                for hf in range(2):
                    i = pe.matmul(ps[64 * hf:64 * hf + 64, 4, 0:62 * ns], w2t[:, 0, :],
                                  gact[:, 0:124 * ns].rearrange("p (s g q n) -> p (s g) q n", s=ns, g=2, q=2)[:, :, hf, :], start=True, stop=True)
                i.then_inc(kc_ready, 1)
                pe.wait_ge(gelu_done, 2 * c + 2)
                if c:
                    pe.wait_ge(vc_evac, c)
                for x in range(4 * ns):
                    i = pe.matmul(ps[0:NCMP, 5 + x // 8, 64 * (x % 8):64 * (x % 8) + 64], gact[:, NCMP * x:NCMP * x + NCMP], w2t[:, 1, :], start=True, stop=True)
                i.then_inc(vc_ready, 1)
            join(pe, 3)
            for br in range(2):
                for gp in range(2):
                    col = 512 * (br + 1) + 128 * gp
                    i = pe.transpose(ps[:, 0, 64 * (2 * br + gp):64 * (2 * br + gp) + 64], kvt[0:64, 4, col:col + 128], ident[0:64, 0:64])
            i.then_inc(kn_mm, 1)
            pe.wait_ge(qs_ready, 1)
            for s in range(NB):
                for g in range(NG):
                    q = 64 * (g % 2)
                    i = pe.matmul(ps[32 * g:32 * g + 32, 3, NCMP * s:NCMP * s + NCMP], qs[q:q + 64, g // 2, s, :], kcT[q:q + 64, s, g // 2, :],
                                  start=True, stop=True)
            i.then_inc(sc_mm, 1)
            pe.wait_ge(kn_ready, 1)
            pe.wait_ge(pc_ready, 1)
            for s in range(NB):
                i = pe.transpose(ps[0:NCMP, s // 4, 128 * (s % 4):128 * (s % 4) + 128], scc[:, s, :], ident)
            i.then_inc(pcT_mm, 1)
            pe.wait_ge(pcg_ready, 1)
            for s in range(NB):
                i = pe.transpose(ps[0:NCMP, 4 + s // 4, 128 * (s % 4):128 * (s % 4) + 128], scg[:, s, :], ident)
            i.then_inc(pcT_mm, 1)
            pe.wait_ge(pcT_evac, 1)
            for s in range(NB):
                i = pe.matmul(ps[:, 2, 9 * s:9 * s + 9], pc0[:, s, :], con[0:NCMP, C_OV:C_OV + 9], start=True, stop=True)
            i.then_inc(imp_mm, 1)
            pe.wait_ge(imp_ready, 1)
            pe.matmul(ps[:, 3, 0:72], con[:, C_SAME:C_SAME + 128], imp.rearrange("p s b -> p (s b)"), start=True, stop=True).then_inc(imp2_mm, 1)
            pe.wait_ge(pcT_evac, 2)

            def s_kt(y):
                pe.wait_ge(a_loaded[y % 4], 64 * (y // 4 + 1))
                for gp in range(2):
                    if y:
                        pe.wait_ge(KT_evac, 2 * y - 1 + gp)
                    for k in range(4):
                        i = pe.transpose(ps[:, 4 + gp, 128 * k:128 * k + 128], araw[:, y % 4, k, 128 * gp:128 * gp + 128], ident)
                    i.then_inc(KT_mm, 1)

            def s_scores(y):
                s, br = y // 2, y % 2
                pe.wait_ge(KT_evac, 2 * y + 2)
                if y >= 2:
                    pe.wait_ge(s_max, y - 1)
                else:
                    pe.wait_ge(drop_ready, 1)
                for g in range(NG):
                    q = 64 * (g % 2)
                    pe.matmul(ps[32 * g:32 * g + 32, 2 * (y % 2), :], qs[q:q + 64, g // 2, s, :], KTs[q:q + 64, y % 2, g // 2, :], start=True, stop=True)
                if y:
                    pe.wait_ge(s_max, y)
                for g in range(NG):
                    q = 64 * (g % 2)
                    i = pe.matmul(ps[32 * g:32 * g + 32, 1, 0:64], qs[q:q + 64, g // 2, s, :], knT[q:q + 64, br, g // 2, :], start=True, stop=True)
                i.then_inc(s_mm, 1)

            def s_pt(y):
                pe.wait_ge(s_p, y + 1)
                if y:
                    pe.wait_ge(pT_evac, y)
                for k in range(4):
                    pe.transpose(ps[:, 6, 128 * k:128 * k + 128], scs[:, y % 2, 128 * k:128 * k + 128], ident)
                pe.transpose(ps[0:64, 7, 0:128], scs[:, y % 2, 512:576], ident).then_inc(pT_mm, 1)

            def s_pv(y):
                s, br = y // 2, y % 2
                pe.wait_ge(pT_evac, y + 1)
                o = ps[:, 3, 0:256]
                if br == 0 and s:
                    pe.wait_ge(oT_evac, s)
                for k in range(4):
                    pe.matmul(o, pTs[:, y % 2, k, :], araw[:, y % 4, k, 256:512], start=(br == 0 and k == 0), stop=False, skip_group_check=True)
                col = 512 * (br + 1) + 256
                i = pe.matmul(o, pTs[0:64, y % 2, 4, :], kvt[0:64, 4, col:col + 256], start=False, stop=False, skip_group_check=True)
                if br:
                    i = pe.matmul(o, pcg[:, s, :], vc[:, s, :], start=False, stop=True, skip_group_check=True)
                i.then_inc(pv_mm, 1)

            s_kt(0)
            for y in range(19):
                if y < 16:
                    s_scores(y)
                if y < 15:
                    s_kt(y + 1)
                if 1 <= y < 17:
                    s_pt(y - 1)
                if y >= 4 and y % 2 == 0:
                    s = (y - 4) // 2
                    pe.wait_ge(o_ready, s + 1)
                    if s:
                        pe.wait_ge(oT_evac, s)
                    pe.transpose(ps[0:64, 3, 256:384], osb[:, s % 2, :], ident).then_inc(oT_mm, 1)
                if 2 <= y < 18:
                    s_pv(y - 2)
            join(pe, 4)
            for k in range(4):
                for t in range(4):
                    col = 512 * (k // 2 + 1) + 128 * (k % 2)
                    i = pe.transpose(ps[:, k, 128 * t:128 * t + 128], kvt[:, t, col:col + 128], ident)
                i.then_inc(kp_mm, 1)
            pe.wait_ge(kp_evac, 4)
            for h in range(NH):
                g, q = h // 4, 64 * (h // 4 % 2)
                for i in range(4):
                    ins = pe.matmul(ps[:, h // 4, 124 * (h % 4) + NCMP * i:124 * (h % 4) + NCMP * i + NCMP],
                                    qT[q:q + 64, 4 * (g // 2) + h % 4, 128 * i:128 * i + 128], kcT[q:q + 64, 8, g // 2, :], start=True, stop=True)
                if h % 4 == 3:
                    ins.then_inc(C_mm, 1)

            def p_scores(P):
                h, i = P // 4, P % 4
                g, r, n = h // 4, h % 4, 128 * (i + 1)
                q = 64 * (g % 2)
                for br in range(2):
                    w = 2 * P + br
                    if w >= 4:
                        pe.wait_ge(P_min, w - 3)
                    pe.matmul(ps[:, w % 4, 0:n], qT[q:q + 64, 4 * (g // 2) + r, 128 * i:128 * i + 128], KTp[q:q + 64, br, g // 2, 0:n],
                              start=True, stop=True).then_inc(P_mm, 1)

            def p_transposes(P):
                h, i = P // 4, P % 4
                for br in range(2):
                    w, e = 2 * P + br, turn(P, br)
                    pe.wait_ge(P_p, w + 1)
                    if e >= 2:
                        pe.wait_ge(P_Te, e - 1)
                    for k in range(i + 1):
                        ins = pe.transpose(ps[:, 4 + e % 2, 128 * k:128 * k + 128], scp[w % 4][:, 128 * k:128 * k + 128], ident)
                    ins.then_inc(P_T, 1)
                if i == 0:
                    e = turn(P, 2)
                    pe.wait_ge(P_Te, e - 1)
                    for k in range(4):
                        ins = pe.transpose(ps[0:NCMP, 4 + e % 2, 128 * k:128 * k + 128], pcp[:, h, k, :], ident)
                    ins.then_inc(P_T, 1)

            def p_values(h, k):
                g = h // 4
                q, b = 64 * (h % 2), 6 + h // 2 % 2
                if k == 0:
                    pe.wait_ge(P_Te, turn(4 * h + 3, 1) + 1)
                    if h >= 4:
                        pe.wait_ge(P_o, h - 3)
                for br in range(2):
                    col = 512 * (br + 1) + 256 + 64 * g
                    pe.matmul(ps[q:q + 64, b, 128 * k:512], kvt[:, k, col:col + 64], pT[:, h % 2, br, k, 128 * k:512],
                              start=(br == 0 and k == 0), stop=False, skip_group_check=True)
                if k == 3:
                    pe.matmul(ps[q:q + 64, b, :], vc[:, 8, 64 * g:64 * g + 64], pcT[:, h % 2, :],
                              start=False, stop=True, skip_group_check=True).then_inc(P_pv, 1)

            pe.wait_ge(C_p, 4)
            for P in range(NPAIR + 5):
                if P < NPAIR:
                    p_scores(P)
                if P >= 5:
                    p_values((P - 5) // 4, (P - 5) % 4)
                if 1 <= P <= NPAIR:
                    p_transposes(P - 1)
            join(pe, 5)
            for e in range(2 * NTT):
                t, k4 = e // 2, e % 2
                t0, n = TILES[t]
                if e >= 8:
                    pe.wait_ge(hT_lo_done, 4 * NTT + e - 7)
                for k in range(4):
                    i = pe.transpose(ps[:, e % 8, 128 * k:128 * k + n], zs[0:n, t, 128 * (4 * k4 + k):128 * (4 * k4 + k) + 128], ident[0:n, 0:n])
                i.then_inc(xT_ready, 1)
            pe.wait_ge(hT_lo_done, 6 * NTT)
            pe.wait_ge(ms_lo, 8)
            for c in range(4):
                for k in range(KT):
                    u = U_OUT + KT * c + k
                    pe.wait_ge(lo_done, u + 1)
                    for t, (t0, n) in enumerate(TILES):
                        if k == 0 and c:
                            pe.wait_ge(tok_evac, 6 * NTT + NTT * (c - 1) + t + 1)
                        o = ps[0:n, t, :]
                        X = [hT_hi[:, k, t0:t0 + n], hT_lo[:, k, t0:t0 + n]]
                        W = [w_hi[:, u % 2, :], w_lo[:, u % 2, :]]
                        pe.matmul(o, X[0], W[0], start=(k == 0), stop=False)
                        pe.matmul(o, X[1], W[0], start=False, stop=False)
                        i = pe.matmul(o, X[0], W[1], start=False, stop=(k == KT - 1))
                    i.then_inc(pe_unit, 1)
            for g in range(4 * NTT):
                t, k4 = g // 4, g % 4
                t0, n = TILES[t]
                pe.wait_ge(x2n_ready, t + 1)
                if g >= 8:
                    pe.wait_ge(hT_lo_done, 6 * NTT + g - 7)
                for k in range(4):
                    i = pe.transpose(ps[:, g % 8, 128 * k:128 * k + n], mo[0:n, t, 128 * (4 * k4 + k):128 * (4 * k4 + k) + 128], ident[0:n, 0:n])
                i.then_inc(xT_ready, 1)
            pe.wait_ge(ld_cw, 48 + 12 * 16)
            pe.wait_ge(hT_lo_done, 6 * NTT + 16)
            for j in range(FB):
                m = 80 if j < FT - 3 * FB else 60
                i = pe.transpose(ps[:, 4 + j // 6, 80 * (j % 6):80 * (j % 6) + m], fwst[0:m, 128 * j:128 * j + 128], ident[0:m, 0:m])
            i.then_inc(fw_T, 1)
            join(pe, 6)
            with pe.Fori(0, FT) as f:
                pe.wait_ge(g_ready, f + 1)
                feat_tile(None, 0, f * 8 + U_FFN, 0, None)
                pe.wait_ge(up_done, f + 1)
                feat_tile(None, 2, f * 8 + (U_FFN + 4), 0, None)
            join(pe, 7)
            def down_unit(c, k, i):
                v = FT * c + k
                at_ = (lambda base: base) if i is None else (lambda base: i * 4 + base)
                pe.wait_ge(lo_done, at_(U_DOWN + v + 1))
                pe.wait_ge(alo_done, at_(v + 1))
                for f in range(4):
                    if k == 0 and c:
                        pe.wait_ge(y_evac, 8 * (c - 1) + 2 * f + 2)
                    W = [w[:, v % 2, 128 * f:128 * f + 128] for w in (w_hi, w_lo)]
                    for x, (wt, act_) in enumerate(((0, a_hi), (0, a_lo), (1, a_hi))):
                        for h in range(2):
                            m = pe.matmul(ps[:, 2 * f + h, 0:HALF], W[wt], act_[:, v % 2, HALF * h:HALF * h + HALF],
                                          start=(k == 0 and x == 0), stop=False, skip_group_check=True)
                m.then_inc(pe_unit, 1)

            for c in range(4):
                peeled, turns = loop_units(c)
                for k in peeled:
                    down_unit(c, k, None)
                with pe.Fori(0, turns) as i:
                    for j in range(4):
                        down_unit(c, 3 + j, i)
            join(pe, 8)
            def y_tile(t, half):
                t0, n = TILES[t]
                for k in range(KT):
                    i = pe.transpose(ps[0:n, 4 * half + k // 4, 128 * (k % 4):128 * (k % 4) + 128], yT[:, k, t0:t0 + n], ident)
                i.then_inc(xT_ready, 1)

            def fco_rows(b):
                for k in range(16 * b, min(16 * b + 16, FT)):
                    i = pe.transpose(ps[0:18, 4 * (b % 2) + k % 16 // 4, 128 * (k % 4):128 * (k % 4) + 128], fst[:, k, :], ident)
                i.then_inc(fco_T, 1)

            for t in range(4):
                if t >= 2:
                    pe.wait_ge(y_used, t - 1)
                y_tile(t, t % 2)
            pe.wait_ge(y_used, 3)
            fco_rows(0)
            pe.wait_ge(y_used, 4)
            y_tile(4, 1)
            pe.wait_ge(y_used, 5)
            fco_rows(1)
            pe.wait_ge(fco_done, 1)
            fco_rows(2)
            join(pe, 9)

_INS = ['x_prompt', 'x_sample', 'cache_kv', 'cache_win_kv', 'state_ssm_conv', 'state_ssm', 'state_ffn_conv',
        'page_table', 'rel_table', 'ln_mix_pre', 'w_in', 'cmp_pe', 'cmp_w1', 'cmp_b1', 'cmp_w2', 'cmp_b2',
        'ssm_conv_w', 'ssm_conv_b', 'ssm_dt_bias', 'ssm_a_log', 'ssm_d', 'ssm_norm_g', 'w_out', 'ln_mix_post',
        'ln_ffn_pre', 'ffn_w_gate', 'ffn_w_up', 'ffn_dw_w', 'ffn_dw_b', 'ffn_w_down', 'ln_ffn_post']
_OUTS = [('y_prompt', (1, NP, D)), ('y_sample', (NB, NT, D)), ('kv_prompt', (1, 1, NP, 4, NG, HD)),
         ('kv_sample', (1, NB, NT, 4, NG, HD)), ('win_prompt', (1, 1, NP, 2, NG, HD)),
         ('win_sample', (1, NB, PAST, 2, NG, HD)), ('ssm_conv_prompt', (1, 1, NHIST, XBC)),
         ('ssm_conv_sample', (1, NB, NHIST, XBC)), ('ssm_prompt', (1, 1, NH, HD, STATE)),
         ('ssm_sample', (1, NB, NH, HD, STATE)), ('ffn_conv_prompt', (1, 1, FHIST, FF)),
         ('ffn_conv_sample', (1, NB, FHIST, FF))]


def kernel(**inputs):
    import concourse.bacc as bacc
    from concourse.bass_utils import run_bass_kernel_spmd as run
    nc = bacc.Bacc("TRN2", target_bir_lowering=False, num_devices=1)
    host = {n: np.ascontiguousarray(inputs[n]) for n in _INS}
    host["con"], host["onehot"] = constants(), onehot()
    A = {n: nc.dram_tensor(f"in_{n}", a.shape, mybir.dt.from_np(a.dtype), kind="ExternalInput").ap()
         for n, a in host.items()}
    O = {n: nc.dram_tensor(f"out_{n}", s, F32, kind="ExternalOutput").ap() for n, s in _OUTS}
    build(nc, A, O)
    r = run(nc, [{f"in_{n}": a for n, a in host.items()}], core_ids=[0])
    return tuple(r.results[0][f"out_{n}"] for n, _ in _OUTS)
```

```python
import concourse.bass as bass
from concourse import mybir
from concourse.alu_op_type import AluOpType as ALU
import numpy as np
from contextlib import ExitStack

F32 = mybir.dt.float32
F32R = mybir.dt.float32r
I32 = mybir.dt.int32
ACT = mybir.ActivationFunctionType
AX = mybir.AxisListType

D = 2048
NP, NB, NT = 512, 8, 8
NS = NB * NT
TOK = NP + NS
HALF = TOK // 2
KT = D // 128
HD, NH, NG, HPG = 64, 16, 4, 4
PAST, PAGE = 512, 128
QW = NH * HD
KVW = 6 * NG * HD
O_KV = QW
O_GATE = O_KV + KVW
O_Z = O_GATE + 3 * NH
O_XBC = O_Z + 1024
XBC = 2048
O_DT = O_XBC + XBC
INW = O_DT + NH
FF = 5504
FT = FF // 128
NCMP = 31
NSEL = 9
STATE = 128
EPS = 1e-6
NEG = -1e30
MASKED = 1e30
CLAMP = 1e29
TINY = 1e-30
BL = 656
BX = 520
XT = XBC // 128
NHIST, FHIST = 3, 2
TILES = [(128 * i, min(128, TOK - 128 * i)) for i in range(-(-TOK // 128))]
NTT = len(TILES)

U_Q, U_XBC, U_KV, U_Z, U_GD = 0, 32, 96, 144, 176
U_OUT = U_GD + 2
U_FFN = U_OUT + 4 * KT
U_DOWN = U_FFN + 8 * FT
U_END = U_DOWN + 4 * FT

C_ID, C_TRI, C_CB, C_TRIS, C_CBS, C_SEQ, C_SAME, C_OV, C_WM, C_IOTA = 0, 128, 256, 384, 448, 512, 520, 648, 657, 665
C_ONE, C_BLK = 672, 800
C_END = 864


def constants():
    c = np.zeros((128, C_END), np.float32)
    k, i = np.arange(128)[:, None], np.arange(128)[None, :]
    c[:, C_ID:C_ID + 128] = k == i
    c[:, C_TRI:C_TRI + 128] = k <= i
    c[:, C_CB:C_CB + 128] = np.where(k <= i, 0.0, NEG)
    ks, js = np.arange(64)[:, None], np.arange(64)[None, :]
    same = ks // NT == js // NT
    c[:64, C_TRIS:C_TRIS + 64] = same & (ks <= js)
    c[:64, C_CBS:C_CBS + 64] = np.where(same & (ks <= js), 0.0, NEG)
    c[:64, C_SEQ:C_SEQ + 8] = ks // NT == np.arange(8)[None, :]
    c[:, C_SAME:C_SAME + 128] = (k // 32 == i // 32) & (k % 8 == i % 8)
    c0, s0 = np.arange(NCMP)[:, None] * 16, np.arange(NSEL)[None, :] * 64
    c[:NCMP, C_OV:C_OV + NSEL] = np.clip(np.minimum(c0 + 32, s0 + 64) - np.maximum(c0, s0), 0, None) / 32
    c[:, C_WM:C_WM + 8] = np.where(np.arange(8)[None, :] < k % 8, MASKED, 0.0)
    c[:, C_IOTA:C_IOTA + 6] = np.arange(1, 7)[None, :]
    c[:, C_ONE:C_ONE + 128] = 1.0
    c[:64, C_BLK:C_BLK + 64] = same
    return c


def onehot():
    dist = BX - np.arange(BL)
    n = np.maximum(dist, 0)
    nf = np.maximum(n, 1).astype(np.float32)
    large = 16 + (np.log(nf / np.float32(16)) / np.float32(np.log(8.0)) * np.float32(16)).astype(np.int32)
    b = np.where(n < 16, n, np.minimum(large, 31))
    o = np.zeros((33, BL), np.float32)
    ok = dist >= 0
    o[b[ok], np.arange(BL)[ok]] = -1.0
    o[32, ~ok] = MASKED
    return o


def build(nc, A, O):
    ctx = ExitStack()
    with ctx:
        def at(name, shape, off, dt=F32):
            return nc.alloc_sbuf_tensor_at(name, shape, dt, offset=BASE + off)

        def sem(name):
            return ctx.enter_context(nc.semaphore(name))

        def dram(ap, off, dims):
            return bass.AP(ap.tensor, off, dims)

        BASE = -(-nc.sbuf_base // 32) * 32
        ps = ctx.enter_context(nc.psum_tensor("ps", [128, 8, 512], F32))
        RA = 0
        RW = 73728
        RC = RW + 16384
        RB = RC + 8192
        hT_hi = at("hT_hi", [128, KT, TOK], RA, F32R)
        hT_lo = at("hT_lo", [128, KT, TOK], RA + 36864, F32R)
        w_raw = at("w_raw", [128, 4, 512], RW)
        w_hi = at("w_hi", [128, 2, 512], RW + 8192, F32R)
        w_lo = at("w_lo", [128, 2, 512], RW + 12288, F32R)
        con = at("con", [128, C_END], RC)
        cwT = at("cwT", [128, XT, 29], RC + 3456)
        cst = at("cst", [128, XT, 27], RC + 3456 + 1856)
        small = at("small", [128, 256], RC + 3456 + 1856 + 1728)
        qT = at("qT", [128, 8, TOK], RB)
        xbcT = at("xbcT", [128, XT, TOK], RB + 18432)
        kvt = at("kvt", [128, NTT, KVW], RB + 55296)
        zs = at("zs", [128, NTT, 1024], RB + 86016)
        RX = RB + 106496
        xr = at("xr", [128, 604], RX)
        xc = at("xc", [128, 604], RX + 2432)
        xin = at("xin", [128, NTT, D], RB + 55296)
        gb = at("gb", [128, D], RB + 55296 + 40960)
        cwst = at("cwst", [29, XBC], RB + 18432)
        junk = at("junk", [128, D], RB)
        gdt = at("gdt", [128, NTT, 64], RX)
        gT = at("gates_T", [64, TOK], RX + 2432)
        gT_ready, gT_done = sem("gates_T_ready"), sem("gates_transposed")
        ss = small[:, 0:5]
        rs = small[:, 5:10]
        ident = con[:, C_ID:C_ID + 128]

        ld_const, ld_x, ld_g, ld_cw = sem("ld_const"), sem("ld_x"), sem("ld_g"), sem("ld_cw")
        raw_loaded = [sem(f"raw_loaded{i}") for i in range(4)]
        hi_done, lo_done, pe_unit = sem("hi_done"), sem("lo_done"), sem("pe_unit")
        phase = sem("phase_done")
        a_ch, v_ch = sem("act_chain"), sem("dve_chain")
        ss_ready, xn_ready = sem("ss_ready"), sem("xn_ready")
        xT_ready, hT_hi_done, hT_lo_done = sem("xT_ready"), sem("hT_hi_done"), sem("hT_lo_done")
        small_zero = sem("small_zeroed")
        cw_ready = sem("cwT_transposed")
        feat_evac, tok_evac, xr_ready, conv_done = sem("feat_evac"), sem("tok_evac"), sem("xr_ready"), sem("conv_done")
        slot_loaded = [sem(f"slot_loaded{i}") for i in range(4)]
        kv_stored, out_stored = sem("kv_stored"), sem("out_stored")

        w_in, w_out = A["w_in"], A["w_out"]

        class Chain:
            def __init__(self, eng, s):
                self.eng, self.s, self.n = eng, s, 0

            def __call__(self, ins):
                self.n += 1
                ins.then_inc(self.s, 1)
                self.eng.wait_ge(self.s, self.n)

        def join(eng, k):
            eng.drain().then_inc(phase, 1)
            eng.wait_ge(phase, 4 * (k + 1))

        block = ctx.enter_context(nc.Block())

        xsk = at("xs_tok", [128, NTT, 1024], RA)
        Bk = at("B_tok", [128, NTT, 512], RA + 20480)
        h0r = at("h0", [128, 4, NB, STATE], RW)
        h0T = at("h0T", [128, NB, 128], RA + 38912)
        hst = at("h_state", [128, 1024], RA + 38912)
        seg = at("seg", [128, 2, 4, 128], RA + 43008)
        bex = at("B_by_sequence", [64, NB, 128], RA + 47104)
        yoff = at("y_off", [64, 1024], RA + 51200)
        xdt = at("x_dt", [128, 2, 1024], RA + 55296)
        xte = at("x_to_end", [128, 2, 1024], RA + 63488)
        sp_ = at("ssd_small", [128, 512], RA + 71680)
        dtb, eA, dsk = small[:, 64:80], small[:, 80:96], small[:, 96:112]
        r5 = lambda o: sp_[:, o:o + 80].rearrange("p (t h) -> p t h", t=NTT)
        dt_, a_, eac, ete, eto = r5(48), r5(128), r5(208), r5(288), r5(368)
        ss2 = sp_[:, 448:468]
        pool_ch = sem("pool_chain")
        acs = at("a_cumulative", [128, NTT, NH], RX + 6656)
        dec = sp_[:, 468:484].rearrange("p (b s) -> p b s", b=2)
        yoT = at("y_off_T", [128, 64], RX + 6400)
        ngb = at("norm_gain", [128, 1024], RX + 1280)
        tmp2 = at("y_tmp", [128, 256], RX + 5376)
        sqj3 = at("squares_unused3", [128, 256], RA + 30720)
        v_, w5 = xdt[:, 0, 0:80].rearrange("p (t h) -> p t h", t=NTT), xdt[:, 0, 80:160].rearrange("p (t h) -> p t h", t=NTT)
        cso = at("conv_out", [27, XBC], RA + 30720)
        hso = at("state_out", [128, 8, 128], RA + 47104)
        ld_ssd = sem("ld_ssd")
        h0_stored = [sem("h0_stored0"), sem("h0_stored1")]
        X_LOADS = 16
        H0_LOADS = X_LOADS + 16 * 2
        z_done, skip_ready = sem("gated_output_ready"), sem("skip_scaled")
        tokT_ready, tokT_evac, a_ready, sums_ready, exps_ready = sem("tokT_ready"), sem("tokT_evac"), sem("a_ready"), sem("sums_ready"), sem("exps_ready")
        sum_ready = sem("sum_copies_ready")
        v_ready, l_ready = sem("softplus_arg"), sem("softplus_log")
        h0T_ready, h0T_evac, yo_ready, yoT_evac = sem("h0T_ready"), sem("h0T_evac"), sem("yo_ready"), sem("yoT_evac")
        yoff_ready, yoff_evac, dec_ready, newps_ready, new_ready = sem("yoff_ready"), sem("yoff_evac"), sem("dec_ready"), sem("newps_ready"), sem("new_ready")
        bexp_ready, xt_ready = sem("bexp_ready"), sem("xt_ready")
        s1_ready, seg_ready, dec_exp, M_done = sem("s1_ready"), sem("seg_ready"), sem("decay_ready"), sem("M_done")
        y_ready, unit_done = sem("y_ready"), sem("ssd_unit_done")
        ss2_ready, inv2, rs2 = sem("ss2_ready"), sem("inv2"), sem("rs2_ready")
        fin_T, fin_copied, ssd_stored = sem("fin_T"), sem("fin_copied"), sem("ssd_stored")

        XF = RB + 36864
        mixA = at("mix_attn", [128, 8, TOK], RB + 18432)
        vc = at("v_cmp", [NCMP, 9, 256], XF)
        kcT = at("k_cmp_T", [128, 9, 2, NCMP], XF + 9216)
        kvp = at("pairs_T", [128, 2, 4, 4, 256], RA)
        craw = at("cmp_rows", [128, 4, 2, 2, 4, 2, 64], RA + 32768)
        w1p = at("w1_pairs", [128, 2, 16, 128], RW)
        gact = at("cmp_hidden", [128, 496], RA + 65536)
        cs = at("cmp_small", [128, 480], RA + 67584)
        w2t, b1t, b2k, hb = cs[:, 0:128].rearrange("p (a d) -> p a d", a=2), cs[:, 128:130], cs[:, 130:131], cs[:, 132:134]
        b2v, pes, peT = cs[0:NCMP, 136:200], cs[0:32, 200:328], cs[:, 328:360]
        tab = cs[0:33, 360:376]
        oh = at("onehot_sb", [33, BL], RA + 69504)
        brow = at("bias_rows", [NH, BL], RX + 5376)
        rb = nc.dram_tensor("bias_scratch", (NH, 128, BL), F32).ap()
        gsc = nc.dram_tensor("gate_scratch", (128, 24), F32).ap()
        ld_c, rb_stored, gsc_stored, tab_set, win_copied = sem("ld_cmp_params"), sem("bias_stored"), sem("gates_stored"), sem("tab_set"), sem("win_copied")
        prep_mm, rb_ready, peT_ready, hb_ready = sem("preparing_mm"), sem("bias_rows_ready"), sem("peT_ready"), sem("hid_bias_ready")
        pairT_ready, pairT_evac = sem("pairT_ready"), sem("pairT_evac")
        hid_ready, gelu_done, kc_ready, kc_evac, vc_ready, vc_evac = sem("hid_ready"), sem("gelu_done"), sem("kc_ready"), sem("kc_evac"), sem("vc_ready"), sem("vc_evac")
        CH = [(0, 4), (4, 4), (8, 1)]

        araw = at("kv_rows", [128, 5, 4, 512], RA)
        KTs = at("K_T", [128, 2, 2, 512], RA + 40960)
        pTs = at("p_T", [128, 2, 5, 128], RA + 49152)
        scs = at("scores_s", [128, 2, 576], RA + 54272)
        sbd = at("bias_and_drop", [128, 2, 512], RA + 58880)
        qs = at("q_s", [128, 2, NB, 32], RA + 62976)
        knT = at("k_new_T", [128, 2, 2, 64], RA + 65024)
        pc0 = at("pc_T", [NCMP, NB, 128], RA + 66048)
        pcg = at("pc_gated_T", [NCMP, NB, 128], RA + 70144)
        scc = at("scores_c", [128, NB, NCMP], RA + 74240)
        scg = at("probs_c_gated", [128, NB, NCMP], RA + 75264)
        osb = at("o_s", [128, 2, 64], RA + 76288)
        as_ = at("attn_small", [128, 512], RA + 76800)
        sb_ = at("bias_s", [128, 2, 512], XF + 11520)
        nb = at("bias_new", [128, 120], XF + 15616)
        gsm_ = at("gates_s", [128, 24], XF + 16128)
        imp = as_[:, 0:72].rearrange("p (s b) -> p s b", s=NB)
        drop = as_[:, 72:120].rearrange("p (s b) -> p s b", s=NB)
        d1 = as_[:, 120:168].rearrange("p (s b) -> p s b", s=NB)
        m8, r8 = as_[:, 168:176], as_[:, 176:184]
        gsm = gsm_[:].rearrange("p (s b) -> p s b", s=NB)
        st_ = as_[:, 208:232].rearrange("p (u x) -> p u x", u=2)
        ld_b, ld_gs = sem("ld_bias_s"), sem("ld_gates_s")
        a_loaded = [sem(f"kv_rows_loaded{i}") for i in range(5)]
        sbd_ready = sem("bias_drop_ready")
        nb_set, qs_ready, kn_ready = sem("nb_set"), sem("qs_ready"), sem("kn_ready")
        pc_sub, pc_exp, pc_ready, pcT_evac = sem("pc_sub"), sem("pc_exp"), sem("pc_ready"), sem("pcT_evac")
        first_mm = sem("compressed_branch_mm")
        imp_ready, drop_ready, pcg_ready = sem("imp_ready"), sem("drop_ready"), sem("pcg_ready")
        KT_mm, KT_evac, s_mm, s_max, s_exp, s_p, pT_mm, pT_evac, pv_mm = [sem("sa_" + x) for x in ("KT_mm", "KT_evac", "scores", "max", "exp", "probs", "pT_mm", "pT_evac", "pv")]
        o_ready, oT_mm, oT_evac = sem("sa_o_ready"), sem("sa_oT_mm"), sem("sa_oT_evac")

        TT = at("bias_p", [128, NH, 512], RA)
        pT = at("pT_prompt", [128, 2, 2, 4, 512], RA + 32768)
        cmb = at("bias_c", [128, NH, 4, NCMP], RA + 32768)
        pcp = at("probs_c_prompt", [128, NH, 4, NCMP], RA + 65536)
        pcT = at("pcT_prompt", [NCMP, 2, 512], RX + 1280)
        ast = at("softmax_small", [128, 64], RX + 7424)
        cm = at("cmp_softmax_small", [128, NH, 4], RA + 49152)
        KTp = at("K_T_prompt", [128, 2, 2, 512], XF)
        scp = [at(f"scores_p{i}", [128, 512], XF + 11520 + 2048 * i if i < 3 else RX + 5376) for i in range(4)]
        ld_TT, kp_mm, kp_evac = sem("ld_TT"), sem("kp_mm"), sem("kp_evac")
        P_mm, P_min, P_exp, P_p, P_T, P_Te, P_pv, P_o = [sem("pa_" + x) for x in ("scores", "min", "exp", "probs", "pT_mm", "pT_evac", "pv", "o_evac")]
        C_mm, C_sub, C_exp, C_p = [sem("pa_c_" + x) for x in ("scores", "shifted", "exp", "probs")]
        NPAIR = 4 * NH
        def turn(P, br):
            return 2 * P + br + (P + 3) // 4

        mo = at("mix_out", [128, NTT, D], RB)
        gb2 = at("gain2", [128, D], RB + 40960)
        x2d = nc.dram_tensor("x2_scratch", (TOK, D), F32).ap()
        acT = at("ffn_act_T", [128, FT, TOK], RB)
        fwT = at("ffn_params_T", [128, FT, 20], RB + 99072)
        fst = at("ffn_conv_rows", [128, FT, 18], RB + 102528)
        xr2 = at("ffn_xr", [128, 594], RB + 105632)
        xc2 = at("ffn_xc", [128, 594], RB + 108032)
        gl = at("gelu_gate", [128, TOK], RB + 110432)
        FB = 11
        fwst = at("ffn_params", [80, 128 * FB], RB + 49152)
        ssc = small[:, 16:16 + 4 * NTT].rearrange("p (t c) -> p t c", t=NTT)
        sqj2 = at("squares_unused2", [128, D], RB + 104448)
        a_hi = at("act_hi", [128, 2, TOK], RA, F32R)
        a_lo = at("act_lo", [128, 2, TOK], RA + 4608, F32R)
        yT = at("ffn_out_T", [128, KT, TOK], RA + 9216)
        yn = at("ffn_out_normed", [128, 2, D], RB + 71680)
        sqj = at("squares_unused", [128, D], RB + 88064)
        gb3 = at("gain3", [128, D], RA + 50176)
        x2r = at("x2", [128, NTT, D], RB)
        fco = at("ffn_conv_out", [18, FF], RB + 49152)
        ms_hi, ms_lo = sem("mix_hi"), sem("mix_lo")
        x2_ready, x2_stored, x2n_ready, fw_T = sem("x2_ready"), sem("x2_stored"), sem("x2_normed"), sem("fw_T")
        g_ready, g_sum, g_act, up_done, f_ch = sem("gate_out"), sem("gate_sum"), sem("gate_act"), sem("up_done"), sem("ffn_chain")
        y_used = sem("y_tile_used")
        ahi_done, alo_done, y_evac, fin_y, y_stored = sem("act_hi_done"), sem("act_lo_done"), sem("y_evac"), sem("y_ready_out"), sem("y_stored")
        fco_T, fco_done = sem("fco_T"), sem("fco_done")

        def loop_units(c):
            return range(3), 10

        def bc(ap, dims):
            return ap.unsqueeze(len(ap.shape)).broadcast_to(dims)

        @block.sync
        def _(sp):
            sp.dma_start(con[:], A["con"]).then_inc(ld_const, 16)
            for t, (t0, n) in enumerate(TILES):
                src = A["x_prompt"][0, t0:t0 + n, :] if t < 4 else A["x_sample"].rearrange("b t d -> (b t) d")
                sp.dma_start(xin[0:n, t, :], src).then_inc(slot_loaded[t] if t < 4 else ld_x, 16)
                if t == 0:
                    sp.dma_start(gb[:], dram(A["ln_mix_pre"], 0, [[0, 128], [1, D]])).then_inc(ld_g, 16)
            sp.dma_start(cwst[0:24, :], A["state_ssm_conv"].rearrange("l b k c -> (l b k) c")).then_inc(ld_cw, 16)
            sp.dma_start(cwst[24:28, :], A["ssm_conv_w"].rearrange("l k c -> (l k) c")).then_inc(ld_cw, 16)
            sp.dma_start(cwst[28:29, :], A["ssm_conv_b"]).then_inc(ld_cw, 16)

            sp.wait_ge(small_zero, 1)
            sp.dma_start(dtb, dram(A["ssm_dt_bias"], 0, [[0, 128], [1, NH]])).then_inc(ld_ssd, 16)
            sp.dma_start(eA, dram(A["ssm_a_log"], 0, [[0, 128], [1, NH]])).then_inc(ld_ssd, 16)
            sp.dma_start(dsk, dram(A["ssm_d"], 0, [[0, 128], [1, NH]])).then_inc(ld_ssd, 16)

            def unit(u, src, shape):
                if u >= 4:
                    sp.wait_ge(lo_done, u - 3)
                dst = w_raw[:, u % 4, :]
                if shape:
                    dst = dst.rearrange("p (k c) -> p k c", k=shape)
                sp.dma_start(dst, src).then_inc(raw_loaded[u % 4], 16)

            def feat_cols(w, wd, col, k0):
                return dram(w, k0 * 128 * wd + col, [[wd, 128], [128 * wd, 4], [1, 128]])

            for f in range(8):
                gp, r = f // 4, f % 4
                for j in range(4):
                    col = (8 * gp + r) * HD
                    u = U_Q + 4 * f + j
                    if u >= 4:
                        sp.wait_ge(lo_done, u - 3)
                    for h in range(2):
                        dst = w_raw[:, u % 4, :].rearrange("p (k c) -> p k c", k=4)[:, :, 64 * h:64 * h + 64]
                        src = dram(w_in, j * 512 * INW + col + 256 * h, [[INW, 128], [128 * INW, 4], [1, 64]])
                        sp.dma_start(dst, src).then_inc(raw_loaded[u % 4], 16)
            for f in range(XT):
                for j in range(4):
                    unit(U_XBC + 4 * f + j, feat_cols(w_in, INW, O_XBC + 128 * f, 4 * j), 4)
            for c in range(5):
                col = O_KV + 512 * c if c < 3 else O_Z + 512 * (c - 3)
                for k in range(KT):
                    unit(U_KV + KT * c + k, dram(w_in, k * 128 * INW + col, [[INW, 128], [1, 512]]), 0)
            for j in range(2):
                u = U_GD + j
                sp.wait_ge(lo_done, u - 3)
                d = w_raw[:, u % 4, :].rearrange("p (k c) -> p k c", k=8)
                sp.dma_start(d[:, :, 0:48], dram(w_in, j * 1024 * INW + O_GATE, [[INW, 128], [128 * INW, 8], [1, 48]])).then_inc(raw_loaded[u % 4], 16)
                sp.dma_start(d[:, :, 48:64], dram(w_in, j * 1024 * INW + O_DT, [[INW, 128], [128 * INW, 8], [1, 16]])).then_inc(raw_loaded[u % 4], 16)

            pages = [[sp.value_load(A["page_table"][s:s + 1, p:p + 1], min_val=0, max_val=39) for p in range(4)] for s in range(NB)]
            sp.wait_ge(phase, 8)
            sp.wait_ge(ld_ssd, 48)
            sp.dma_start(ngb[:], dram(A["ssm_norm_g"], 0, [[0, 128], [1, 1024]])).then_inc(ld_ssd, 16)
            HS = NH * HD * STATE
            for p in range(10):
                if p < 8:
                    if p >= 4:
                        sp.wait_ge(h0_stored[p % 2], 16 * ((p - 4) // 2 + 1))
                    sp.dma_start(h0r[:, p % 4], dram(A["state_ssm"], p * 16384, [[STATE, 128], [HS, NB], [1, STATE]])).then_inc(slot_loaded[p % 4], 16)
                if p >= 2:
                    q = p - 2
                    sp.wait_ge(new_ready, q + 1)
                    sp.dma_start(dram(O["ssm_sample"], q * 16384, [[STATE, 128], [HS, NB], [1, STATE]]), h0r[:, q % 4]).then_inc(h0_stored[q % 2], 16)
            for b in range(2):
                sp.wait_ge(h0_stored[b], 64)
            for a in range(2):
                sp.dma_start(w1p[:, a], dram(A["cmp_w1"], a * 262144, [[128, 128], [16384, 16], [1, 128]])).then_inc(ld_c, 16)
            sp.wait_ge(fin_copied, 2)
            sp.dma_start(O["ssm_conv_prompt"].rearrange("l b k c -> (l b k) c"), cso[0:3, :]).then_inc(ssd_stored, 16)
            sp.dma_start(O["ssm_conv_sample"].rearrange("l b k c -> (l b k) c"), cso[3:27, :]).then_inc(ssd_stored, 16)
            sp.dma_start(dram(O["ssm_prompt"], 0, [[STATE, 128], [16384, 8], [1, STATE]]), hso[:]).then_inc(ssd_stored, 16)
            sp.wait_ge(phase, 12)
            sp.dma_start(oh[:], A["onehot"]).then_inc(ld_c, 16)
            sp.dma_start(tab[0:32, :], A["rel_table"]).then_inc(ld_c, 16)
            sp.dma_start(pes, A["cmp_pe"].rearrange("l a (s q) d -> (l a s) (q d)", q=2)).then_inc(ld_c, 16)
            sp.dma_start(w2t, dram(A["cmp_w2"], 0, [[64, 128], [8192, 2], [1, 64]])).then_inc(ld_c, 16)
            sp.dma_start(b1t, dram(A["cmp_b1"], 0, [[1, 128], [128, 2]]), allow_slow_non_contiguous=True).then_inc(ld_c, 16)
            for a in range(2):
                sp.dma_start(cs[64 * a:64 * a + 64, 130:131], dram(A["cmp_b2"], 0, [[1, 64], [1, 1]])).then_inc(ld_c, 16)
            sp.dma_start(b2v, dram(A["cmp_b2"], 64, [[0, NCMP], [1, 64]])).then_inc(ld_c, 16)
            sp.wait_ge(kv_stored, 64)
            PGW = PAGE * 1024
            ckv = A["cache_kv"].rearrange("l n t s g d -> (l n) (t s g d)")
            sp.wait_ge(ssd_stored, 48)
            for s in range(9):
                if s >= 4:
                    sp.wait_ge(pairT_evac, 4 * (s - 3))
                for p in range(4):
                    dst = craw[64 * (p % 2):64 * (p % 2) + 64, s % 4, p // 2]
                    if s < 8:
                        src = ckv[bass.ds(pages[s][p], 1), :].rearrange("n (i q s g d) -> i (n s g) q d", q=2, s=4, g=NG, d=HD)[:, 0:8]
                    else:
                        src = O["kv_prompt"].rearrange("l b t s g d -> (l b t) s g d")[128 * p:128 * p + 128].rearrange("(i q) s g d -> i (s g) q d", q=2)[:, 0:8]
                    dst = dst.rearrange("i a g q d -> i (a g) q d")
                    for q in range(2):
                        sp.dma_start(dst[:, :, q, :], src[:, :, q, :]).then_inc(slot_loaded[s % 4], 16)
            for s in range(NB):
                for b in range(3):
                    sp.dma_start(dram(gsc, 3 * s + b, [[24, NT], [192, NH]]), gdt[8 * s:8 * s + 8, 4, 16 * b:16 * b + 16],
                                 allow_slow_non_contiguous=True).then_inc(gsc_stored, 16)
            sp.wait_ge(rb_ready, 1)
            sp.dma_start(rb, brow[:].unsqueeze(1).broadcast_to([NH, 128, BL])).then_inc(rb_stored, 16)
            sp.wait_ge(rb_stored, 16)
            sp.wait_ge(gsc_stored, 16 * 3 * NB)
            sp.wait_ge(nb_set, 1)
            for h in range(NH):
                sp.dma_start(sb_[8 * h:8 * h + 8, 0, :], dram(rb, h * 128 * BL + 8, [[BL - 1, 8], [1, 512]])).then_inc(ld_b, 16)
                sp.dma_start(nb[8 * h:8 * h + 8, 56:64], dram(rb, h * 128 * BL + BX, [[BL - 1, 8], [1, 8]])).then_inc(ld_b, 16)
            sp.dma_start(gsm_[:], gsc).then_inc(ld_gs, 16)
            sp.wait_ge(phase, 16)
            for y in range(16):
                s, br = y // 2, y % 2
                if y >= 5:
                    sp.wait_ge(pv_mm, y - 4)
                if br == 0:
                    for p in range(4):
                        src = ckv[bass.ds(pages[s][p], 1), :].rearrange("n (t c) -> (n t) c", t=PAGE)[:, 512:1024]
                        sp.dma_start(araw[:, y % 5, p, :], src).then_inc(a_loaded[y % 5], 16)
                else:
                    sp.dma_start(araw[:, y % 5, :, :], dram(A["cache_win_kv"], s * PAST * 512, [[512, 128], [65536, 4], [1, 512]])).then_inc(a_loaded[y % 5], 64)
            for j, y in ((1, 11), (2, 12), (3, 13), (0, 15)):
                sp.wait_ge(pv_mm, y + 1)
                sp.dma_start(TT[:, 4 * j:4 * j + 4, :], dram(rb, 136 + 4 * j * 128 * BL, [[BL - 1, 128], [128 * BL, 4], [1, 512]])).then_inc(ld_TT, 16)
            sp.wait_ge(phase, 20)
            for s in range(NB):
                sp.dma_start(O["win_sample"][0, s, 0:PAST - NT].rearrange("t s g d -> t (s g d)"),
                             A["cache_win_kv"][0, s, NT:PAST].rearrange("t s g d -> t (s g d)")).then_inc(win_copied, 16)
            for c in range(4):
                for k in range(KT):
                    unit(U_OUT + KT * c + k, dram(A["w_out"], k * 128 * D + 512 * c, [[D, 128], [1, 512]]), 0)
            sp.wait_ge(out_stored, 208)
            for t, (t0, n) in enumerate(TILES):
                src = A["x_prompt"][0, t0:t0 + n, :] if t < 4 else A["x_sample"].rearrange("b t d -> (b t) d")
                sp.dma_start(xin[0:n, t, :], src).then_inc(ld_x, 16)
            sp.dma_start(gb[:], dram(A["ln_mix_post"], 0, [[0, 128], [1, D]])).then_inc(ld_g, 16)
            sp.dma_start(gb2[:], dram(A["ln_ffn_pre"], 0, [[0, 128], [1, D]])).then_inc(ld_g, 16)
            for b in range(4):
                c0, c1 = 128 * FB * b, min(128 * FB * (b + 1), FF)
                for r, src in ((0, A["state_ffn_conv"].rearrange("l b k c -> (l b k) c")),
                               (16, A["ffn_dw_w"].rearrange("l k c -> (l k) c")), (19, A["ffn_dw_b"])):
                    m = src.shape[0]
                    sp.dma_start(fwst[20 * b + r:20 * b + r + m, 0:c1 - c0], src[:, c0:c1]).then_inc(ld_cw, 16)
            W2 = [A[x][0].rearrange("(k p) c -> p k c", p=128) for x in ("ffn_w_gate", "ffn_w_up")]
            with sp.Fori(0, FT) as f:
                for j in range(8):
                    sp.wait_ge(lo_done, f * 8 + (U_FFN + j - 3))
                    sp.dma_start(w_raw[:, (U_FFN + j) % 4, :].rearrange("p (k c) -> p k c", k=4),
                                 W2[j // 4][:, 4 * (j % 4):4 * (j % 4) + 4, bass.ds(f * 128, 128)]).then_inc(raw_loaded[(U_FFN + j) % 4], 16)
            Wd = A["ffn_w_down"][0]
            for c in range(4):
                u0 = U_DOWN + FT * c
                peeled, turns = loop_units(c)
                for k in peeled:
                    unit(u0 + k, Wd[128 * k:128 * k + 128, 512 * c:512 * c + 512], 0)
                with sp.Fori(0, turns) as i:
                    for j in range(4):
                        sp.wait_ge(lo_done, i * 4 + (u0 + j))
                        sp.dma_start(w_raw[:, (u0 + 3 + j) % 4, :], Wd[bass.ds(i * 512 + 128 * (3 + j), 128), 512 * c:512 * c + 512]).then_inc(raw_loaded[(u0 + 3 + j) % 4], 16)
            sp.wait_ge(phase, 32)
            sp.wait_ge(x2_stored, 16 * NTT)
            for t, (t0, n) in enumerate(TILES):
                sp.dma_start(x2r[0:n, t, :], x2d[t0:t0 + n, :]).then_inc(ld_x, 16)
            sp.dma_start(gb3[:], dram(A["ln_ffn_post"], 0, [[0, 128], [1, D]])).then_inc(ld_x, 16)
            for t, (t0, n) in enumerate(TILES):
                sp.wait_ge(fin_y, t + 1)
                dst = O["y_prompt"][0, t0:t0 + n, :] if t < 4 else O["y_sample"].rearrange("b t d -> (b t) d")
                sp.dma_start(dst, x2r[0:n, t, :]).then_inc(y_stored, 16)
            sp.wait_ge(fco_done, 3)
            sp.dma_start(O["ffn_conv_prompt"].rearrange("l b k c -> (l b k) c"), fco[0:2, :]).then_inc(y_stored, 16)
            sp.dma_start(O["ffn_conv_sample"].rearrange("l b k c -> (l b k) c"), fco[2:18, :]).then_inc(y_stored, 16)
            sp.wait_ge(y_stored, 16 * (2 + NTT))
            sp.wait_ge(win_copied, 128)
            sp.wait_ge(ssd_stored, 48)
            sp.wait_ge(h0_stored[0], 64)
            sp.wait_ge(h0_stored[1], 64)
            sp.wait_ge(kv_stored, 64)
            sp.wait_ge(out_stored, 208)

        def raw_count(u):
            return 16 * sum(2 if v < U_XBC or U_GD <= v < U_OUT else 1 for v in range(u % 4, u + 1, 4))

        def act_feature(act, ch, f):
            act.wait_ge(pe_unit, 4 * (f + 1))
            b = 2 * (f % 2)
            if f < 8:
                act.activation(qT[:, f, :].rearrange("p (h c) -> p h c", h=2), ps[:, b:b + 2, 0:HALF],
                               ACT.Copy, scale=-HD ** -0.5).then_inc(feat_evac, 1)
                return
            x = f - 8
            if x:
                act.wait_ge(acc_ready, x)
            act.activation(xr[:, 3:3 + HALF], ps[:, b, 0:HALF], ACT.Copy)
            act.activation(xr[:, 3 + HALF:3 + NP], ps[:, b + 1, 0:NP - HALF], ACT.Copy)
            last = act.activation(xr[:, 515:603].rearrange("p (s c) -> p s c", s=8)[:, :, 3:11],
                                  ps[:, b + 1, NP - HALF:HALF].rearrange("p (s c) -> p s c", s=8), ACT.Copy)
            last.then_inc(xr_ready, 1)
            act.wait_ge(xr_ready, x + 1)
            act.sem_inc(feat_evac, 1)

        def act_silu(act, x):
            act.wait_ge(acc_ready, x + 1)
            act.activation(xbcT[:, x, 0:NP], xc[:, 0:NP], ACT.Silu)
            act.activation(xbcT[:, x, NP:TOK].rearrange("p (s c) -> p s c", s=8),
                           xc[:, 515:603].rearrange("p (s c) -> p s c", s=8)[:, :, 0:8], ACT.Silu).then_inc(conv_done, 1)

        inv_ready = sem("mean_square_inverse")
        rs_ready = sem("rs_ready")
        acc_ready = sem("conv_sum_ready")

        def act_tokens(act, ch, c):
            act.wait_ge(pe_unit, U_KV + KT * (c + 1))
            for t, (t0, n) in enumerate(TILES):
                if c < 3:
                    i = act.activation(kvt[0:n, t, 512 * c:512 * c + 512], ps[0:n, t, :], ACT.Copy)
                else:
                    i = act.activation(zs[0:n, t, 512 * (c - 3):512 * (c - 3) + 512], ps[0:n, t, :], ACT.Silu)
                i.then_inc(tok_evac, 1)
            if c == 2:
                act.wait_ge(tok_evac, 5 * (c + 1))
                for t, (t0, n) in enumerate(TILES[:4]):
                    act.dma_start(O["kv_prompt"].rearrange("l b t s g d -> (l b t) (s g d)")[t0:t0 + n, :],
                                  kvt[0:n, t, 0:1024]).then_inc(kv_stored, 16)
                    act.dma_start(O["win_prompt"].rearrange("l b t s g d -> (l b t) (s g d)")[t0:t0 + n, :],
                                  kvt[0:n, t, 1024:1536]).then_inc(out_stored, 16)
                act.dma_start(O["kv_sample"].rearrange("l b t s g d -> (l b t) (s g d)"), kvt[0:NS, 4, 0:1024]).then_inc(out_stored, 16)
                for s in range(NB):
                    act.dma_start(O["win_sample"][0, s, PAST - NT:PAST].rearrange("t s g d -> t (s g d)"),
                                  kvt[8 * s:8 * s + 8, 4, 1024:1536]).then_inc(out_stored, 16)

        def out_tokens(act, ch, c):
            act.wait_ge(pe_unit, U_OUT + KT * (c + 1))
            for t, (t0, n) in enumerate(TILES):
                ch(act.activation(sqj2[0:n, 0:512], ps[0:n, t, :], ACT.Square, accum_out=small[0:n, 16 + 4 * t + c:17 + 4 * t + c]))
                act.activation(mo[0:n, t, 512 * c:512 * c + 512], ps[0:n, t, :], ACT.Copy).then_inc(tok_evac, 1)

        def down_hi(act, c, k, i):
            v = FT * c + k
            u = U_DOWN + v
            at_ = (lambda per, base: base) if i is None else (lambda per, base: i * per + base)
            act.wait_ge(raw_loaded[u % 4], at_(16, raw_count(u)))
            act.wait_ge(pe_unit, at_(4, u - 1))
            act.activation(w_hi[:, u % 2, :], w_raw[:, u % 4, :], ACT.Copy).then_inc(hi_done, 1)
            src = acT[:, k, :] if i is None else acT[:, bass.ds(i * 4 + k, 1), :].rearrange("p a c -> p (a c)")
            act.activation(a_hi[:, v % 2, :], src, ACT.Copy).then_inc(ahi_done, 1)

        def down_lo(dve, c, k, i):
            v = FT * c + k
            at_ = (lambda per, base: base) if i is None else (lambda per, base: i * per + base)
            dve.wait_ge(ahi_done, at_(4, v + 1))
            src = acT[:, k, :] if i is None else acT[:, bass.ds(i * 4 + k, 1), :].rearrange("p a c -> p (a c)")
            dve.tensor_tensor(a_lo[:, v % 2, :], src, a_hi[:, v % 2, :].bitcast(F32), ALU.subtract).then_inc(alo_done, 1)

        def prompt_out(dve, h):
            dve.wait_ge(P_pv, h + 1)
            q = 64 * (h % 2)
            dve.tensor_copy(mixA[q:q + 64, h // 2, 0:NP], ps[q:q + 64, 6 + h // 2 % 2, :]).then_inc(P_o, 1)

        @block.scalar
        def _(act):
            ch = Chain(act, a_ch)

            def hi(u):
                act.wait_ge(raw_loaded[u % 4], raw_count(u))
                if u >= 2:
                    act.wait_ge(pe_unit, u - 1)
                act.activation(w_hi[:, u % 2, :], w_raw[:, u % 4, :], ACT.Copy).then_inc(hi_done, 1)

            act.wait_ge(small_zero, 1)
            for i in range(NTT + 1):
                if i < NTT:
                    n = TILES[i][1]
                    act.wait_ge(slot_loaded[i] if i < 4 else ld_x, 16)
                    act.activation(junk[0:n, :], xin[0:n, i, :], ACT.Square, accum_out=small[0:n, i:i + 1]).then_inc(ss_ready, 1)
                    act.wait_ge(inv_ready, i + 1)
                    act.activation(small[0:n, 5 + i:6 + i], small[0:n, 5 + i:6 + i], ACT.Sqrt).then_inc(rs_ready, 1)
                if i:
                    t0, n = TILES[i - 1]
                    for k4 in range(4):
                        g = 4 * (i - 1) + k4
                        act.wait_ge(xT_ready, g + 1)
                        act.activation(hT_hi[:, 4 * k4:4 * k4 + 4, t0:t0 + n],
                                       ps[:, g % 8, :].rearrange("p (k c) -> p k c", k=4)[:, :, 0:n], ACT.Copy).then_inc(hT_hi_done, 1)
            join(act, 0)
            for f in range(24):
                hi(4 * f)
                hi(4 * f + 1)
                if f:
                    act_feature(act, ch, f - 1)
                hi(4 * f + 2)
                hi(4 * f + 3)
                if f > 8:
                    act_silu(act, f - 9)
            for c in range(5):
                for k in range(KT):
                    hi(U_KV + KT * c + k)
                    if k == 1:
                        if c == 0:
                            act_feature(act, ch, 23)
                            act_silu(act, XT - 1)
                        else:
                            act_tokens(act, ch, c - 1)
            hi(U_GD)
            hi(U_GD + 1)
            act_tokens(act, ch, 4)
            act.wait_ge(pe_unit, U_GD + 2)
            act.wait_ge(conv_done, XT)
            act.activation(gT[:].rearrange("r (h c) -> r h c", h=2), ps[0:64, 5:7, 0:HALF], ACT.Copy).then_inc(gT_ready, 1)
            act.wait_ge(gT_done, 1)
            act.activation(gdt[:, 0:4, :].rearrange("p t c -> p (t c)"), ps[:, 7, 0:256], ACT.Copy).then_inc(tok_evac, 4)
            act.activation(gdt[0:64, 4, :], ps[0:64, 7, 256:320], ACT.Copy).then_inc(tok_evac, 1)
            join(act, 1)
            act.activation(gdt[:, :, 0:48], gdt[:, :, 0:48], ACT.Sigmoid)
            act.wait_ge(ld_ssd, 48)
            act.activation(eA, eA, ACT.Exp).then_inc(v_ready, 1)
            act.wait_ge(v_ready, 2)
            ch(act.activation(w5, w5, ACT.Exp))
            act.activation(w5, w5, ACT.Ln, bias=1.0).then_inc(l_ready, 1)
            for G in range(3 * NTT):
                t, b = G // 3, G % 3
                n = TILES[t][1]
                act.wait_ge(tokT_ready, G + 1)
                dst = xsk[0:n, t, 512 * b:512 * b + 512] if b < 2 else Bk[0:n, t, :]
                act.activation(dst, ps[0:n, G % 6, :], ACT.Copy).then_inc(tokT_evac, 1)
            act.wait_ge(sum_ready, 1)
            act.activation(sp_[:, 208:448], sp_[:, 208:448], ACT.Exp).then_inc(exps_ready, 1)
            for p in range(8):
                act.wait_ge(h0T_ready, p + 1)
                if p:
                    act.wait_ge(yo_ready, p)
                act.activation(h0T[:].rearrange("n (a s) p -> n a (s p)", a=2), ps[:, 0:2, :], ACT.Copy).then_inc(h0T_evac, 1)
                act.wait_ge(yo_ready, p + 1)
                if p:
                    act.wait_ge(yoff_ready, p)
                act.activation(yoT[:], ps[:, 2, 0:64], ACT.Copy).then_inc(yoT_evac, 1)
                if p >= 2:
                    act.wait_ge(new_ready, p - 1)
                act.activation(dec[:, p % 2, :], ps[:, 3, 0:8], ACT.Exp).then_inc(dec_ready, 1)

            def unit_squares(w):
                t, g = w // 4, w % 4
                n = TILES[t][1]
                act.wait_ge(z_done, w + 1)
                if w:
                    act.wait_ge(ss2_ready, w)
                act.activation(sqj3[0:n, :], zs[0:n, t, 256 * g:256 * g + 256], ACT.Square,
                               accum_out=sp_[0:n, 448 + 4 * t + g:449 + 4 * t + g]).then_inc(ss2_ready, 1)

            for w in range(20):
                n = TILES[w // 4][1]
                act.wait_ge(seg_ready, w + 1)
                act.activation(seg[0:n, w % 2, :, 0:n], seg[0:n, w % 2, :, 0:n], ACT.Exp).then_inc(dec_exp, 1)
                if w:
                    unit_squares(w - 1)
            unit_squares(19)
            join(act, 2)
            act.wait_ge(inv2, 1)
            act.activation(ss2, ss2, ACT.Sqrt).then_inc(rs2, 1)
            act.wait_ge(prep_mm, 1)
            act.activation(brow[:, 0:512], ps[0:NH, 0, :], ACT.Copy)
            act.activation(brow[:, 512:BL], ps[0:NH, 1, 0:BL - 512], ACT.Copy).then_inc(rb_ready, 1)
            act.wait_ge(prep_mm, 2)
            act.activation(peT, ps[:, 2, 0:32], ACT.Copy).then_inc(peT_ready, 1)
            act.wait_ge(hb_ready, 1)
            e = 0
            for c, (s0, ns) in enumerate(CH):
                for s in range(ns):
                    for b in range(4):
                        act.wait_ge(pairT_ready, e + 1)
                        if b == 0 and s == 0 and c:
                            act.wait_ge(hid_ready, 2 * c)
                        act.activation(kvp[:, b % 2, s, :, 128 * (b // 2):128 * (b // 2) + 128],
                                       ps[:, e % 2, :].rearrange("p (g i) -> p g i", g=4), ACT.Copy).then_inc(pairT_evac, 1)
                        e += 1
                n = 124 * ns
                for a in range(2):
                    act.wait_ge(hid_ready, 2 * c + a + 1)
                    if a or c:
                        act.wait_ge(kc_ready if a else vc_ready, c + 1 if a else c)
                    act.activation(gact[:, 0:n], ps[:, 2 + a, 0:n], ACT.Gelu_apprx_tanh, bias=hb[:, a:a + 1]).then_inc(gelu_done, 1)
                act.activation(kcT[:, s0:s0 + ns].rearrange("p s g n -> p (s g n)"), ps[:, 4, 0:62 * ns], ACT.Identity, bias=b2k).then_inc(kc_evac, 1)
            join(act, 3)
            act.wait_ge(first_mm, 1)
            act.activation(knT[:].rearrange("p b g c -> p (b g c)"), ps[:, 0, 0:256], ACT.Copy).then_inc(kn_ready, 1)
            act.wait_ge(pc_sub, 1)
            act.activation(scc[:], scc[:], ACT.Exp, scale=-1.0).then_inc(pc_exp, 1)
            act.wait_ge(first_mm, 3)
            act.activation(pc0[:].rearrange("n (a s) p -> n a (s p)", a=2), ps[0:NCMP, 0:2, :], ACT.Copy).then_inc(pcT_evac, 1)
            act.wait_ge(first_mm, 4)
            act.activation(pcg[:].rearrange("n (a s) p -> n a (s p)", a=2), ps[0:NCMP, 4:6, :], ACT.Copy).then_inc(pcT_evac, 1)

            def kt_evac(y):
                for gp in range(2):
                    act.wait_ge(KT_mm, 2 * y + gp + 1)
                    if y >= 2:
                        act.wait_ge(s_mm, y - 1)
                    act.activation(KTs[:, y % 2, gp, :], ps[:, 4 + gp, :], ACT.Copy).then_inc(KT_evac, 1)

            def pt_evac(y):
                act.wait_ge(pT_mm, y + 1)
                if y >= 2:
                    act.wait_ge(pv_mm, y - 1)
                act.activation(pTs[:, y % 2, 0:4, :].rearrange("p k c -> p (k c)"), ps[:, 6, :], ACT.Copy)
                act.activation(pTs[0:64, y % 2, 4, :], ps[0:64, 7, 0:128], ACT.Copy).then_inc(pT_evac, 1)

            kt_evac(0)
            for y in range(17):
                if y < 16:
                    act.wait_ge(s_max, y + 1)
                    act.activation(scs[:, y % 2, :], scs[:, y % 2, :], ACT.Exp, scale=-1.0, bias=st_[:, y % 2, 0:1], accum_out=st_[:, y % 2, 1:2]).then_inc(s_exp, 1)
                if y < 15:
                    kt_evac(y + 1)
                if y >= 1:
                    pt_evac(y - 1)
            join(act, 4)
            for k in range(4):
                act.wait_ge(kp_mm, k + 1)
                act.activation(KTp[:, k // 2, k % 2, :], ps[:, k, :], ACT.Copy).then_inc(kp_evac, 1)
            for b in range(4):
                act.wait_ge(C_sub, b + 1)
                act.activation(pcp[:, 4 * b:4 * b + 4], pcp[:, 4 * b:4 * b + 4], ACT.Exp, scale=-1.0).then_inc(C_exp, 1)

            def pt_out(P):
                h, i = P // 4, P % 4
                n = 128 * (i + 1)
                if h >= 2 and i == 0:
                    act.wait_ge(P_pv, h - 1)
                for br in range(2):
                    e = turn(P, br)
                    act.wait_ge(P_T, e + 1)
                    act.activation(pT[:, h % 2, br, 0:i + 1, 128 * i:128 * i + 128],
                                   ps[:, 4 + e % 2, 0:n].rearrange("p (k c) -> p k c", c=128), ACT.Copy).then_inc(P_Te, 1)
                if i == 0:
                    e = turn(P, 2)
                    act.wait_ge(P_T, e + 1)
                    act.activation(pcT[:, h % 2, :], ps[0:NCMP, 4 + e % 2, :], ACT.Copy).then_inc(P_Te, 1)

            for P in range(NPAIR + 1):
                if P < NPAIR:
                    n = 128 * (P % 4 + 1)
                    for br in range(2):
                        w, k = 2 * P + br, 8 * (P % 2)
                        act.wait_ge(P_min, w + 1)
                        act.activation(scp[w % 4][:, 0:n], scp[w % 4][:, 0:n], ACT.Exp, scale=-1.0, bias=ast[:, k + br:k + br + 1],
                                       accum_out=ast[:, k + 2 + br:k + 3 + br]).then_inc(P_exp, 1)
                if P:
                    pt_out(P - 1)
            join(act, 5)
            for k in range(8):
                act.activation(hT_hi[:, k, :], mixA[:, k, :], ACT.Copy).then_inc(ms_hi, 1)
            for e in range(2 * NTT):
                t, k4 = e // 2, e % 2
                t0, n = TILES[t]
                act.wait_ge(xT_ready, 4 * NTT + e + 1)
                act.activation(hT_hi[:, 8 + 4 * k4:12 + 4 * k4, t0:t0 + n],
                               ps[:, e % 8, :].rearrange("p (k c) -> p k c", k=4)[:, :, 0:n], ACT.Copy).then_inc(hT_hi_done, 1)
            for c in range(4):
                for k in range(KT):
                    hi(U_OUT + KT * c + k)
                    if k == 1 and c:
                        out_tokens(act, ch, c - 1)
            out_tokens(act, ch, 3)
            act.drain().then_inc(ss_ready, 1)
            act.wait_ge(inv_ready, NTT + 1)
            act.activation(rs, rs, ACT.Sqrt).then_inc(rs_ready, 1)
            for i in range(1, NTT + 2):
                if i <= NTT:
                    t0, n = TILES[i - 1]
                    act.wait_ge(x2_ready, i)
                    act.dma_start(x2d[t0:t0 + n, :], xin[0:n, i - 1, :]).then_inc(x2_stored, 16)
                    act.activation(sqj2[0:n, :], xin[0:n, i - 1, :], ACT.Square, accum_out=small[0:n, i - 1:i]).then_inc(ss_ready, 1)
                    act.wait_ge(inv_ready, NTT + 1 + i)
                    act.activation(small[0:n, 4 + i:5 + i], small[0:n, 4 + i:5 + i], ACT.Sqrt).then_inc(rs_ready, 1)
                if i >= 2:
                    t0, n = TILES[i - 2]
                    for k4 in range(4):
                        g = 4 * (i - 2) + k4
                        act.wait_ge(xT_ready, 6 * NTT + g + 1)
                        act.activation(hT_hi[:, 4 * k4:4 * k4 + 4, t0:t0 + n],
                                       ps[:, g % 8, :].rearrange("p (k c) -> p k c", k=4)[:, :, 0:n], ACT.Copy).then_inc(hT_hi_done, 1)
            join(act, 6)
            act.drain().then_inc(g_ready, 1)
            act.activation(gl[:, 0:1], small[:, 0:1], ACT.Gelu_apprx_tanh)
            act.drain().then_inc(g_act, 1)
            with act.Fori(0, FT) as f:
                def hi_loop(j):
                    act.wait_ge(raw_loaded[(U_FFN + j) % 4], f * 32 + raw_count(U_FFN + j))
                    act.wait_ge(pe_unit, f * 8 + (U_FFN + j - 1))
                    act.activation(w_hi[:, j % 2, :], w_raw[:, (U_FFN + j) % 4, :], ACT.Copy).then_inc(hi_done, 1)

                for j in range(6):
                    hi_loop(j)
                act.wait_ge(pe_unit, f * 8 + (U_FFN + 4))
                act.activation(xr2[:, 2:2 + HALF], ps[:, 0, 0:HALF], ACT.Copy)
                act.activation(xr2[:, 2 + HALF:2 + NP], ps[:, 1, 0:NP - HALF], ACT.Copy)
                act.activation(xr2[:, 514:594].rearrange("p (s c) -> p s c", s=8)[:, :, 2:10],
                               ps[:, 1, NP - HALF:HALF].rearrange("p (s c) -> p s c", s=8), ACT.Copy).then_inc(g_ready, 1)
                hi_loop(6)
                hi_loop(7)
                act.wait_ge(g_sum, f + 1)
                act.wait_ge(up_done, f + 1)
                act.activation(gl[:, 0:NP], xc2[:, 0:NP], ACT.Gelu_apprx_tanh)
                act.activation(gl[:, NP:TOK].rearrange("p (s c) -> p s c", s=8),
                               xc2[:, 514:594].rearrange("p (s c) -> p s c", s=8)[:, :, 0:8], ACT.Gelu_apprx_tanh).then_inc(g_act, 1)
            join(act, 7)
            for c in range(4):
                peeled, turns = loop_units(c)
                for k in peeled:
                    down_hi(act, c, k, None)
                with act.Fori(0, turns) as i:
                    for j in range(4):
                        down_hi(act, c, 3 + j, i)
            join(act, 8)
            def fco_copy(b):
                m = min(16, FT - 16 * b) * 128
                act.wait_ge(fco_T, b + 1)
                s = 4 * (b % 2)
                act.activation(fco[:, 2048 * b:2048 * b + m], ps[0:18, s:s + 4, :].rearrange("p b c -> p (b c)")[:, 0:m], ACT.Copy).then_inc(fco_done, 1)

            for t, (t0, n) in enumerate(TILES):
                if t == 4:
                    fco_copy(0)
                s = 4 * (t % 2 if t < 4 else 1)
                act.wait_ge(xT_ready, 10 * NTT + t + 1)
                act.activation(sqj[0:n, :], ps[0:n, s:s + 4, :].rearrange("p b c -> p (b c)"), ACT.Square,
                               accum_out=small[0:n, t:t + 1]).then_inc(ss_ready, 1)
                act.wait_ge(inv_ready, 2 * NTT + 2 + t)
                act.activation(small[0:n, 5 + t:6 + t], small[0:n, 5 + t:6 + t], ACT.Sqrt).then_inc(rs_ready, 1)
            fco_copy(1)
            fco_copy(2)
            join(act, 9)

        @block.vector
        def _(dve):
            ch = Chain(dve, v_ch)
            dve.memset(small[:], 0.0).then_inc(small_zero, 1)
            dve.wait_ge(ld_const, 16)
            for i in range(NTT + 1):
                if i < NTT:
                    n = TILES[i][1]
                    r = small[0:n, 5 + i:6 + i]
                    dve.wait_ge(ss_ready, i + 1)
                    ch(dve.tensor_scalar(r, small[0:n, i:i + 1], 1.0 / D, EPS, ALU.mult, ALU.add))
                    dve.reciprocal(r, r).then_inc(inv_ready, 1)
                    dve.wait_ge(rs_ready, i + 1)
                    dve.wait_ge(ld_g, 16)
                    dve.scalar_tensor_tensor(xin[0:n, i, :], xin[0:n, i, :], r, gb[0:n, :], ALU.mult, ALU.mult).then_inc(xn_ready, 1)
                if i:
                    t0, n = TILES[i - 1]
                    for k4 in range(4):
                        g = 4 * (i - 1) + k4
                        dve.wait_ge(hT_hi_done, g + 1)
                        dve.tensor_tensor(hT_lo[:, 4 * k4:4 * k4 + 4, t0:t0 + n],
                                          ps[:, g % 8, :].rearrange("p (k c) -> p k c", k=4)[:, :, 0:n],
                                          hT_hi[:, 4 * k4:4 * k4 + 4, t0:t0 + n].bitcast(F32), ALU.subtract).then_inc(hT_lo_done, 1)
            dve.wait_ge(cw_ready, 1)
            ch(dve.tensor_copy(cwT[:], ps[:, 0, 0:XT * 29].rearrange("p (k c) -> p k c", k=XT)))
            join(dve, 0)
            ch(dve.memset(xr[:, 0:3], 0.0))
            for x in range(XT):
                if x:
                    dve.wait_ge(acc_ready, x)
                xs3 = xr[:, 515:603].rearrange("p (s c) -> p s c", s=8)
                dve.tensor_copy(xs3[:, :, 0:3], cwT[:, x, 0:24].rearrange("p (s c) -> p s c", s=8))
                dve.wait_ge(xr_ready, x + 1)
                dve.tensor_copy(cst[:, x, 0:3], xr[:, 512:515])
                ch(dve.tensor_copy(cst[:, x, 3:27].rearrange("p (s c) -> p s c", s=8), xs3[:, :, 8:11]))
                if x:
                    dve.wait_ge(conv_done, x)
                ch(dve.tensor_scalar(xc[:, 0:600], xr[:, 0:600], cwT[:, x, 24:25], cwT[:, x, 28:29], ALU.mult, ALU.add))
                for k in range(1, 4):
                    i = dve.scalar_tensor_tensor(xc[:, 0:600], xr[:, k:600 + k], cwT[:, x, 24 + k:25 + k], xc[:, 0:600], ALU.mult, ALU.add)
                    if k < 3:
                        ch(i)
                    else:
                        i.then_inc(acc_ready, 1)
            dve.wait_ge(acc_ready, XT)
            dve.memset(gdt[64:128, 4, :], 0.0)
            join(dve, 1)
            dve.wait_ge(ld_ssd, 48)
            ch(dve.memset(ss2, 0.0))
            ch(dve.memset(sp_[:, 48:448], 0.0))
            ch(dve.tensor_tensor(v_, gdt[:, :, 48:64], dtb.unsqueeze(1).broadcast_to([128, NTT, NH]), ALU.add))
            ch(dve.tensor_scalar(w5, v_, -1.0, None, ALU.mult))
            dve.tensor_tensor(w5, v_, w5, ALU.min).then_inc(v_ready, 1)
            dve.wait_ge(v_ready, 2)
            dve.wait_ge(l_ready, 1)
            ch(dve.scalar_tensor_tensor(dt_, v_, 0.0, w5, ALU.max, ALU.add))
            dve.scalar_tensor_tensor(a_, dt_, -1.0, eA.unsqueeze(1).broadcast_to([128, NTT, NH]), ALU.mult, ALU.mult).then_inc(a_ready, 1)
            dve.wait_ge(sums_ready, 1)
            for rows, ts in ((128, slice(0, 4)), (64, slice(4, 5))):
                m = ts.stop - ts.start
                S = ps[0:rows, 7, 32 * ts.start:32 * ts.stop].rearrange("p (t x h) -> p t x h", t=m, x=2)
                dve.tensor_copy(acs[0:rows, ts], S[:, :, 0])
                ch(dve.tensor_copy(eac[0:rows, ts], S[:, :, 0]))
                dve.tensor_copy(eto[0:rows, ts], S[:, :, 1])
                ch(dve.tensor_tensor(ete[0:rows, ts], S[:, :, 1], eac[0:rows, ts], ALU.subtract))
            dve.drain().then_inc(sum_ready, 1)
            for p in range(8):
                dve.wait_ge(exps_ready, 1)
                dve.wait_ge(yoff_ready, p + 1)
                dve.tensor_tensor(yoff[:, 128 * p:128 * p + 128].rearrange("c (h p) -> c h p", h=2),
                                  ps[0:64, 6, 0:128].rearrange("c (h p) -> c h p", h=2),
                                  bc(eac[0:64, 4, 2 * p:2 * p + 2], [64, 2, 64]), ALU.mult).then_inc(yoff_evac, 1)
                dve.wait_ge(dec_ready, p + 1)
                dve.wait_ge(slot_loaded[p % 4], X_LOADS + 16 * (p // 4 + 1))
                ch(dve.tensor_tensor(h0r[:, p % 4], h0r[:, p % 4], bc(dec[:, p % 2, :], [128, NB, 128]), ALU.mult))
                dve.wait_ge(newps_ready, p + 1)
                dve.tensor_tensor(h0r[:, p % 4].rearrange("p (a s) n -> p a (s n)", a=2),
                                  h0r[:, p % 4].rearrange("p (a s) n -> p a (s n)", a=2), ps[:, 4:6, :], ALU.add).then_inc(new_ready, 1)

            def seg_unit(w):
                t, g = w // 4, w % 4
                n = TILES[t][1]
                dve.wait_ge(s1_ready, w + 1)
                if w >= 2:
                    dve.wait_ge(y_ready, w - 1)
                mask = con[0:n, C_CB:C_CB + n] if t < 4 else con[0:n, C_CBS:C_CBS + n]
                for h in range(4):
                    i = dve.scalar_tensor_tensor(seg[0:n, w % 2, h, 0:n], ps[0:n, 2 + w % 2, 128 * h:128 * h + n],
                                                 acs[0:n, t, 4 * g + h:4 * g + h + 1], mask, ALU.subtract, ALU.add)
                i.then_inc(seg_ready, 1)

            def mix_unit(w):
                t, g = w // 4, w % 4
                n = TILES[t][1]
                dve.wait_ge(dec_exp, w + 1)
                dve.tensor_tensor(seg[0:n, w % 2, :, 0:n], seg[0:n, w % 2, :, 0:n],
                                  ps[0:n, w % 2, 0:n].unsqueeze(1).broadcast_to([n, 4, n]), ALU.mult).then_inc(M_done, 1)

            def out_unit(w):
                t, g = w // 4, w % 4
                n = TILES[t][1]
                dve.wait_ge(y_ready, w + 1)
                dve.wait_ge(skip_ready, t + 1)
                if w:
                    dve.wait_ge(unit_done, w)
                y = xsk[0:n, t, 256 * g:256 * g + 256]
                hv = lambda ap: ap.rearrange("c (h p) -> c h p", h=4)
                H = hst[:, 256 * g:256 * g + 256]
                if t == 0:
                    dve.tensor_copy(H, ps[:, 6, 0:256])
                    dve.tensor_tensor(y, y, ps[0:n, 4, 0:256], ALU.add).then_inc(unit_done, 1)
                    return
                if t < 4:
                    dve.tensor_tensor(hv(tmp2[0:n, :]), hv(ps[0:n, 5, 0:256]), bc(eac[0:n, t, 4 * g:4 * g + 4], [n, 4, 64]), ALU.mult)
                    dve.tensor_tensor(hv(H), hv(H), bc(eto[:, t, 4 * g:4 * g + 4], [128, 4, 64]), ALU.mult)
                ch(dve.tensor_tensor(y, y, ps[0:n, 4, 0:256], ALU.add))
                if t < 4:
                    dve.tensor_tensor(H, H, ps[:, 6, 0:256], ALU.add)
                dve.tensor_tensor(y, y, tmp2[0:n, :] if t < 4 else yoff[:, 256 * g:256 * g + 256], ALU.add).then_inc(unit_done, 1)

            for w in range(21):
                if w < 20:
                    seg_unit(w)
                if w >= 1:
                    out_unit(w - 1)
                if w < 20:
                    mix_unit(w)
            dve.wait_ge(fin_T, 1)
            dve.wait_ge(ss2_ready, 20)
            dve.tensor_copy(cso[:].rearrange("p (b c) -> p b c", b=4), ps[0:27, 0:4, :]).then_inc(fin_copied, 1)
            dve.tensor_copy(hso[:].rearrange("p (a s) n -> p a (s n)", a=2), ps[:, 4:6, :]).then_inc(fin_copied, 1)
            join(dve, 2)
            dve.memset(cs[32:33, 360:376], 1.0).then_inc(tab_set, 1)
            dve.memset(nb[:], MASKED).then_inc(nb_set, 1)
            dve.wait_ge(ss2_ready, 20)
            dve.wait_ge(ld_ssd, 64)
            ch(dve.tensor_scalar(ss2, ss2, 1.0 / 256, EPS, ALU.mult, ALU.add))
            dve.reciprocal(ss2, ss2).then_inc(inv2, 1)
            dve.wait_ge(rs2, 1)
            for t, (t0, n) in enumerate(TILES):
                for g in range(4):
                    z = zs[0:n, t, 256 * g:256 * g + 256]
                    dve.scalar_tensor_tensor(z, z, sp_[0:n, 448 + 4 * t + g:449 + 4 * t + g], ngb[0:n, 256 * g:256 * g + 256], ALU.mult, ALU.mult)
            dve.wait_ge(ld_c, 16 * 10)
            dve.wait_ge(prep_mm, 3)
            dve.tensor_tensor(hb, ps[:, 7, 0:2], b1t, ALU.add).then_inc(hb_ready, 1)
            for c, (s0, ns) in enumerate(CH):
                dve.wait_ge(vc_ready, c + 1)
                dve.tensor_tensor(vc[:, s0:s0 + ns].rearrange("n s (g d) -> n (s g) d", g=4),
                                  ps[0:NCMP, 5:7, :].rearrange("n a (s d) -> n (a s) d", d=64)[:, 0:4 * ns],
                                  b2v.unsqueeze(1).broadcast_to([NCMP, 4 * ns, 64]), ALU.add).then_inc(vc_evac, 1)
            join(dve, 3)
            for gp in range(2):
                for r in range(4):
                    i = dve.tensor_copy(qs[:, gp, :, 8 * r:8 * r + 8], qT[:, 4 * gp + r, NP:TOK].rearrange("p (s t) -> p s t", s=NB))
            i.then_inc(qs_ready, 1)
            dve.wait_ge(ld_b, 16 * 2 * NH)
            ch(dve.tensor_copy(sb_[:, 1, :], sb_[:, 0, :]))
            ch(dve.tensor_tensor(sb_[:, 1, 0:8], sb_[:, 1, 0:8], con[:, C_WM:C_WM + 8], ALU.add))
            dve.wait_ge(first_mm, 2)
            sx = ps[:, 3, 0:NB * NCMP].rearrange("p (s n) -> p s n", s=NB)
            ch(dve.tensor_tensor(scc[:], sx, sb_[:, 0, 31:512:16].unsqueeze(1).broadcast_to([128, NB, NCMP]), ALU.add))
            ch(dve.tensor_reduce(m8, scc[:], AX.X, ALU.min))
            dve.tensor_tensor(scc[:], scc[:], bc(m8, [128, NB, NCMP]), ALU.subtract).then_inc(pc_sub, 1)
            dve.wait_ge(pc_exp, 1)
            ch(dve.tensor_reduce(r8, scc[:], AX.X, ALU.add))
            ch(dve.tensor_scalar(r8, r8, TINY, None, ALU.max))
            ch(dve.reciprocal(r8, r8))
            dve.tensor_tensor(scc[:], scc[:], bc(r8, [128, NB, NCMP]), ALU.mult).then_inc(pc_ready, 1)
            dve.wait_ge(pc_ready, 1)
            dve.wait_ge(ld_gs, 16)
            dve.tensor_tensor(scg[:], scc[:], gsm[:, :, 0:1].broadcast_to([128, NB, NCMP]), ALU.mult).then_inc(pcg_ready, 1)
            dve.wait_ge(first_mm, 5)
            dve.tensor_copy(imp.rearrange("p s b -> p (s b)"), ps[:, 2, 0:72]).then_inc(imp_ready, 1)
            dve.wait_ge(first_mm, 6)
            ch(dve.tensor_copy(d1, ps[:, 3, 0:72].rearrange("p (s b) -> p s b", s=NB)[:, :, 1:7]))
            ch(dve.tensor_reduce(m8, d1, AX.X, ALU.min))
            ch(dve.tensor_tensor(d1, d1, bc(m8, [128, NB, 6]), ALU.is_equal))
            iota = con[:, C_IOTA:C_IOTA + 6].unsqueeze(1).broadcast_to([128, NB, 6])
            ch(dve.tensor_tensor(d1, d1, iota, ALU.mult))
            ch(dve.tensor_reduce(m8, d1, AX.X, ALU.max))
            ch(dve.tensor_tensor(d1, bc(m8, [128, NB, 6]), iota, ALU.is_equal))
            ch(dve.tensor_scalar(drop, d1, MASKED, None, ALU.mult))
            dve.drain().then_inc(drop_ready, 1)

            def s_first(y):
                s, br = y // 2, y % 2
                S = scs[:, y % 2, :]
                dve.wait_ge(s_mm, y + 1)
                if y >= 2:
                    dve.wait_ge(pT_mm, y - 1)
                if br == 0:
                    dve.wait_ge(sbd_ready, s + 1)
                bias = sbd[:, s % 2, :] if br == 0 else sb_[:, 1, :]
                ch(dve.tensor_tensor_reduce(out=S[:, 0:512], in0=ps[:, 2 * (y % 2), :], in1=bias, scale=1.0, scalar=CLAMP,
                                            op0=ALU.add, op1=ALU.min, accum_out=st_[:, y % 2, 2:3]))
                dve.tensor_tensor_reduce(out=S[:, 512:576], in0=ps[:, 1, 0:64], in1=nb[:, 56 - 8 * s:120 - 8 * s], scale=1.0,
                                         scalar=st_[:, y % 2, 2:3], op0=ALU.add, op1=ALU.min, accum_out=st_[:, y % 2, 0:1]).then_inc(s_max, 1)

            def s_second(y):
                s, br = y // 2, y % 2
                dve.wait_ge(s_exp, y + 1)
                ch(dve.tensor_scalar(st_[:, y % 2, 3:4], st_[:, y % 2, 1:2], TINY, None, ALU.max))
                ch(dve.reciprocal(st_[:, y % 2, 3:4], st_[:, y % 2, 3:4]))
                dve.tensor_scalar(scs[:, y % 2, :], scs[:, y % 2, :], st_[:, y % 2, 3:4], gsm[:, s, 1 + br:2 + br], ALU.mult, ALU.mult).then_inc(s_p, 1)

            def s_out(s):
                dve.wait_ge(pv_mm, 2 * s + 2)
                if s >= 2:
                    dve.wait_ge(oT_mm, s - 1)
                for g in range(NG):
                    i = dve.tensor_copy(osb[32 * g:32 * g + 32, s % 2, :], ps[32 * g:32 * g + 32, 3, 64 * g:64 * g + 64])
                i.then_inc(o_ready, 1)
                dve.wait_ge(oT_mm, s + 1)
                for par in range(2):
                    i = dve.tensor_copy(mixA[64 * par:64 * par + 64, :, NP + 8 * s:NP + 8 * s + 8],
                                        ps[0:64, 3, 256:384].rearrange("d (h q t) -> d h q t", q=2, t=8)[:, :, par, :])
                i.then_inc(oT_evac, 1)

            for y in range(19):
                if y < 16:
                    s_first(y)
                    s_second(y)
                if y >= 4 and y % 2 == 0:
                    s_out((y - 4) // 2)
            join(dve, 4)
            dve.wait_ge(ld_TT, 64)
            dve.memset(cmb[:], MASKED).then_inc(v_ready, 1)
            dve.wait_ge(v_ready, 3)
            for i in range(4):
                n = 7 + 8 * i
                last = dve.tensor_copy(cmb[:, :, i, 0:n], TT[:, :, 415 - 128 * i:512:16])
            ch(last)
            for b in range(4):
                B = slice(4 * b, 4 * b + 4)
                dve.wait_ge(C_mm, b + 1)
                ch(dve.tensor_tensor(pcp[:, B], ps[:, b, 0:496].rearrange("p (h i n) -> p h i n", h=4, i=4), cmb[:, B], ALU.add))
                ch(dve.tensor_reduce(cm[:, B], pcp[:, B], AX.X, ALU.min))
                ch(dve.tensor_scalar(cm[:, B], cm[:, B], CLAMP, None, ALU.min))
                dve.tensor_tensor(pcp[:, B], pcp[:, B], bc(cm[:, B], [128, 4, 4, NCMP]), ALU.subtract).then_inc(C_sub, 1)
            def compressed_probs():
                for b in range(4):
                    B = slice(4 * b, 4 * b + 4)
                    dve.wait_ge(C_exp, b + 1)
                    ch(dve.tensor_reduce(cm[:, B], pcp[:, B], AX.X, ALU.add))
                    ch(dve.tensor_scalar(cm[:, B], cm[:, B], TINY, None, ALU.max))
                    ch(dve.reciprocal(cm[:, B], cm[:, B]))
                    ch(dve.tensor_tensor(cm[:, B], cm[:, B], gdt[:, 0:4, B].rearrange("p i h -> p h i"), ALU.mult))
                    dve.tensor_tensor(pcp[:, B], pcp[:, B], bc(cm[:, B], [128, 4, 4, NCMP]), ALU.mult).then_inc(C_p, 1)

            for P in range(NPAIR + 6):
                if P < NPAIR:
                    h, i = P // 4, P % 4
                    n, k = 128 * (i + 1), 8 * (P % 2)
                    if P >= 2:
                        dve.wait_ge(P_T, turn(P - 2, 1) + 1)
                    for br in range(2):
                        w = 2 * P + br
                        dve.wait_ge(P_mm, w + 1)
                        dve.tensor_tensor_reduce(out=scp[w % 4][:, 0:n], in0=ps[:, w % 4, 0:n], in1=TT[:, h, 384 - 128 * i:512], scale=1.0,
                                                 scalar=CLAMP, op0=ALU.add, op1=ALU.min, accum_out=ast[:, k + br:k + br + 1]).then_inc(P_min, 1)
                    if P == 0:
                        compressed_probs()
                    dve.wait_ge(P_exp, 2 * P + 2)
                    r = ast[:, k + 4:k + 6]
                    ch(dve.tensor_scalar(r, ast[:, k + 2:k + 4], TINY, None, ALU.max))
                    ch(dve.reciprocal(r, r))
                    for br in range(2):
                        w, gate = 2 * P + br, 16 * (br + 1) + h
                        dve.tensor_scalar(scp[w % 4][:, 0:n], scp[w % 4][:, 0:n], ast[:, k + 4 + br:k + 5 + br], gdt[:, i, gate:gate + 1],
                                          ALU.mult, ALU.mult).then_inc(P_p, 1)
                if P >= 9 and P % 4 == 1:
                    prompt_out(dve, (P - 9) // 4)
            join(dve, 5)
            for k in range(8):
                dve.wait_ge(ms_hi, k + 1)
                dve.tensor_tensor(hT_lo[:, k, :], mixA[:, k, :], hT_hi[:, k, :].bitcast(F32), ALU.subtract).then_inc(ms_lo, 1)
            for e in range(2 * NTT):
                t, k4 = e // 2, e % 2
                t0, n = TILES[t]
                dve.wait_ge(hT_hi_done, 4 * NTT + e + 1)
                dve.tensor_tensor(hT_lo[:, 8 + 4 * k4:12 + 4 * k4, t0:t0 + n], ps[:, e % 8, :].rearrange("p (k c) -> p k c", k=4)[:, :, 0:n],
                                  hT_hi[:, 8 + 4 * k4:12 + 4 * k4, t0:t0 + n].bitcast(F32), ALU.subtract).then_inc(hT_lo_done, 1)
            dve.wait_ge(ss_ready, NTT + 1)
            ch(dve.tensor_reduce(ss, ssc, AX.X, ALU.add))
            ch(dve.tensor_scalar(rs, ss, 1.0 / D, EPS, ALU.mult, ALU.add))
            dve.reciprocal(rs, rs).then_inc(inv_ready, 1)
            dve.wait_ge(rs_ready, NTT + 1)
            dve.wait_ge(ld_g, 48)
            for i in range(NTT + 2):
                if i < NTT:
                    n = TILES[i][1]
                    dve.scalar_tensor_tensor(mo[0:n, i, :], mo[0:n, i, :], small[0:n, 5 + i:6 + i], gb[0:n, :], ALU.mult, ALU.mult).then_inc(xn_ready, 1)
                if 1 <= i <= NTT:
                    n = TILES[i - 1][1]
                    r = small[0:n, 4 + i:5 + i]
                    dve.wait_ge(ss_ready, NTT + 1 + i)
                    ch(dve.tensor_scalar(r, small[0:n, i - 1:i], 1.0 / D, EPS, ALU.mult, ALU.add))
                    dve.reciprocal(r, r).then_inc(inv_ready, 1)
                    dve.wait_ge(rs_ready, NTT + 1 + i)
                    dve.scalar_tensor_tensor(mo[0:n, i - 1, :], xin[0:n, i - 1, :], r, gb2[0:n, :], ALU.mult, ALU.mult).then_inc(x2n_ready, 1)
                if i >= 2:
                    t0, n = TILES[i - 2]
                    for k4 in range(4):
                        g = 4 * (i - 2) + k4
                        dve.wait_ge(hT_hi_done, 6 * NTT + g + 1)
                        dve.tensor_tensor(hT_lo[:, 4 * k4:4 * k4 + 4, t0:t0 + n],
                                          ps[:, g % 8, :].rearrange("p (k c) -> p k c", k=4)[:, :, 0:n],
                                          hT_hi[:, 4 * k4:4 * k4 + 4, t0:t0 + n].bitcast(F32), ALU.subtract).then_inc(hT_lo_done, 1)
            dve.wait_ge(fw_T, 1)
            for bank, blocks, j0, j1 in ((4, 4, 0, 6), (5, 4, 6, FB - 1), (5, 3, FB - 1, FB)):
                jj = j0 % 6
                src = ps[:, bank, 80 * jj:80 * (jj + j1 - j0)].rearrange("p (j b r) -> p b j r", b=4, r=20)
                for b in range(blocks):
                    dve.tensor_copy(fwT[:, FB * b + j0:FB * b + j1, :], src[:, b])
            dve.memset(xr2[:, 0:2], 0.0)
            dve.wait_ge(x2_stored, 16 * NTT)
            join(dve, 6)
            dve.drain().then_inc(up_done, 1)
            with dve.Fori(0, FT) as f:
                P = lambda m: fwT[:, bass.ds(f, 1), m:m + 1].rearrange("p a c -> p (a c)")
                x3 = xr2[:, 514:594].rearrange("p (s c) -> p s c", s=8)
                dve.tensor_copy(x3[:, :, 0:2], fwT[:, bass.ds(f, 1), 0:16].rearrange("p a (s c) -> p (a s) c", s=8))
                dve.wait_ge(g_ready, f + 2)
                dve.wait_ge(g_act, f + 1)
                dve.tensor_copy(fst[:, bass.ds(f, 1), 0:2].rearrange("p a c -> p (a c)"), xr2[:, 512:514])
                dve.tensor_copy(fst[:, bass.ds(f, 1), 2:18].rearrange("p a (s c) -> p (a s) c", s=8), x3[:, :, 8:10]).then_inc(f_ch, 1)
                dve.wait_ge(f_ch, f * 3 + 1)
                dve.tensor_scalar(xc2[:, 0:592], xr2[:, 0:592], P(16), P(19), ALU.mult, ALU.add).then_inc(f_ch, 1)
                dve.wait_ge(f_ch, f * 3 + 2)
                dve.scalar_tensor_tensor(xc2[:, 0:592], xr2[:, 1:593], P(17), xc2[:, 0:592], ALU.mult, ALU.add).then_inc(f_ch, 1)
                dve.wait_ge(f_ch, f * 3 + 3)
                dve.scalar_tensor_tensor(xc2[:, 0:592], xr2[:, 2:594], P(18), xc2[:, 0:592], ALU.mult, ALU.add).then_inc(g_sum, 1)
                dve.wait_ge(g_act, f + 2)
                dve.wait_ge(pe_unit, f * 8 + (U_FFN + 8))
                dve.tensor_tensor(acT[:, bass.ds(f, 1), :].rearrange("p a (h c) -> p (a h) c", h=2), gl[:].rearrange("p (h c) -> p h c", h=2),
                                  ps[:, 2:4, 0:HALF], ALU.mult).then_inc(up_done, 1)
            join(dve, 7)
            for c in range(5):
                if c < 4:
                    peeled, turns = loop_units(c)
                    down_lo(dve, c, 0, None)
                    down_lo(dve, c, 1, None)
                if c:
                    dve.wait_ge(pe_unit, U_DOWN + FT * c)
                    for b in range(8):
                        dve.tensor_copy(yT[:, 4 * (c - 1) + b // 2, HALF * (b % 2):HALF * (b % 2) + HALF], ps[:, b, 0:HALF]).then_inc(y_evac, 1)
                if c < 4:
                    down_lo(dve, c, 2, None)
                    with dve.Fori(0, turns) as i:
                        for j in range(4):
                            down_lo(dve, c, 3 + j, i)
            join(dve, 8)
            dve.wait_ge(ld_x, 16 * (2 * NTT + 2))
            for t, (t0, n) in enumerate(TILES):
                b = 4 * (t % 2 if t < 4 else 1)
                r = small[0:n, 5 + t:6 + t]
                dve.wait_ge(ss_ready, 2 * NTT + 2 + t)
                ch(dve.tensor_scalar(r, small[0:n, t:t + 1], 1.0 / D, EPS, ALU.mult, ALU.add))
                dve.reciprocal(r, r).then_inc(inv_ready, 1)
                dve.wait_ge(rs_ready, 2 * NTT + 2 + t)
                dve.scalar_tensor_tensor(yn[0:n, t % 2, :], ps[0:n, b:b + 4, :].rearrange("p b c -> p (b c)"), r, gb3[0:n, :],
                                         ALU.mult, ALU.mult).then_inc(y_used, 1)
                dve.wait_ge(y_used, t + 1)
                dve.tensor_tensor(x2r[0:n, t, :], yn[0:n, t % 2, :], x2r[0:n, t, :], ALU.add).then_inc(fin_y, 1)
            join(dve, 9)

        @block.gpsimd
        def _(pool):
            join(pool, 0)
            with pool.Fori(0, U_GD // 4) as i:
                for j in range(4):
                    pool.wait_ge(hi_done, i * 4 + (j + 1))
                    pool.tensor_tensor(w_lo[:, j % 2, :], w_raw[:, j, :], w_hi[:, j % 2, :].bitcast(F32), ALU.subtract).then_inc(lo_done, 1)
            for u in range(U_GD, U_GD + 2):
                pool.wait_ge(hi_done, u + 1)
                pool.tensor_tensor(w_lo[:, u % 2, :], w_raw[:, u % 4, :], w_hi[:, u % 2, :].bitcast(F32), ALU.subtract).then_inc(lo_done, 1)
            join(pool, 1)
            def x_scaled(k, t, n, sl):
                if k >= 2:
                    t_old = [4, 0, 1, 2, 3, 4][k - 2]
                    pool.wait_ge(y_ready, 4 * (t_old + 1)) if k > 2 else pool.wait_ge(newps_ready, 8)
                xh = lambda ap: ap.rearrange("c (h p) -> c h p", h=NH)
                pool.tensor_tensor(xh(xdt[0:n, sl, :]), xh(xsk[0:n, t, :]), bc(dt_[0:n, t, :], [n, NH, 64]), ALU.mult).then_inc(pool_ch, 1)
                pool.wait_ge(pool_ch, k + 1)
                pool.tensor_tensor(xh(xte[0:n, sl, :]), xh(xdt[0:n, sl, :]), bc(ete[0:n, t, :], [n, NH, 64]), ALU.mult).then_inc(xt_ready, 1)

            def skip_scaled(t):
                n = TILES[t][1]
                xh = xsk[0:n, t, :].rearrange("c (h p) -> c h p", h=NH)
                pool.tensor_tensor(xh, xh, bc(dsk[0:n, :], [n, NH, 64]), ALU.mult).then_inc(skip_ready, 1)

            pool.wait_ge(tokT_evac, 15)
            pool.wait_ge(exps_ready, 1)
            x_scaled(0, 4, 64, 0)
            x_scaled(1, 0, 128, 1)
            skip_scaled(0)
            for g in range(NG):
                if g:
                    pool.wait_ge(newps_ready, 2 * g)
                pool.tensor_tensor(bex[:], Bk[0:64, 4, 128 * g:128 * g + 128].unsqueeze(1).broadcast_to([64, NB, 128]),
                                   bc(con[0:64, C_SEQ:C_SEQ + 8], [64, NB, 128]), ALU.mult).then_inc(bexp_ready, 1)
            for t, (t0, n) in enumerate(TILES):
                if t < 4:
                    x_scaled(t + 2, t + 1, TILES[t + 1][1], t % 2)
                    skip_scaled(t + 1)
                for g in range(4):
                    z = zs[0:n, t, 256 * g:256 * g + 256]
                    pool.wait_ge(unit_done, 4 * t + g + 1)
                    pool.tensor_tensor(z, xsk[0:n, t, 256 * g:256 * g + 256], z, ALU.mult).then_inc(z_done, 1)
            join(pool, 2)
            join(pool, 3)
            pool.wait_ge(ld_b, 16 * 2 * NH)
            pool.wait_ge(drop_ready, 1)
            for s in range(NB):
                if s >= 2:
                    pool.wait_ge(s_max, 2 * s - 3)
                pool.tensor_copy(sbd[:, s % 2, 0:64], sb_[:, 0, 0:64])
                pool.tensor_copy(sbd[:, s % 2, 448:512], sb_[:, 0, 448:512])
                v = lambda ap: ap[:, 64:448].rearrange("p (b k) -> p b k", b=6)
                pool.tensor_tensor(v(sbd[:, s % 2, :]), v(sb_[:, 0, :]), bc(drop[:, s, :], [128, 6, 64]), ALU.add)
                pool.drain().then_inc(sbd_ready, 1)
            join(pool, 4)
            join(pool, 5)

            def lo_loop(u0, turns):
                with pool.Fori(0, turns) as i:
                    for j in range(4):
                        u = u0 + j
                        pool.wait_ge(hi_done, i * 4 + (u + 1))
                        pool.tensor_tensor(w_lo[:, u % 2, :], w_raw[:, u % 4, :], w_hi[:, u % 2, :].bitcast(F32), ALU.subtract).then_inc(lo_done, 1)

            lo_loop(U_OUT, KT)
            pool.wait_ge(ld_x, 16 * (1 + NTT))
            for t, (t0, n) in enumerate(TILES):
                pool.wait_ge(xn_ready, NTT + t + 1)
                pool.tensor_tensor(xin[0:n, t, :], xin[0:n, t, :], mo[0:n, t, :], ALU.add).then_inc(x2_ready, 1)
            join(pool, 6)
            lo_loop(U_FFN, 2 * FT)
            join(pool, 7)
            lo_loop(U_DOWN, FT)
            join(pool, 8)
            join(pool, 9)

        @block.tensor
        def _(pe):
            pe.wait_ge(ld_const, 16)
            for g in range(4 * NTT):
                t, k4 = g // 4, g % 4
                t0, n = TILES[t]
                if k4 == 0:
                    pe.wait_ge(xn_ready, t + 1)
                if g >= 8:
                    pe.wait_ge(hT_lo_done, g - 7)
                for k in range(4):
                    i = pe.transpose(ps[:, g % 8, 128 * k:128 * k + n], xin[0:n, t, 128 * (4 * k4 + k):128 * (4 * k4 + k) + 128], ident[0:n, 0:n])
                i.then_inc(xT_ready, 1)
            pe.wait_ge(ld_cw, 48)
            pe.wait_ge(hT_lo_done, 4 * NTT)
            for k in range(XT):
                i = pe.transpose(ps[:, 0, 29 * k:29 * k + 29], cwst[0:29, 128 * k:128 * k + 128], ident[0:29, 0:29])
            i.then_inc(cw_ready, 1)
            join(pe, 0)

            def feat_tile(bank, u0):
                for j in range(4):
                    pe.wait_ge(lo_done, u0 + (j + 1))
                    for kk in range(4):
                        k = 4 * j + kk
                        s = j % 2
                        for h in range(2):
                            o = ps[:, bank + h, 0:HALF]
                            W = [w_hi[:, s, 128 * kk:128 * kk + 128], w_lo[:, s, 128 * kk:128 * kk + 128]]
                            X = [hT_hi[:, k, HALF * h:HALF * h + HALF], hT_lo[:, k, HALF * h:HALF * h + HALF]]
                            pe.matmul(o, W[0], X[0], start=(k == 0), stop=False)
                            pe.matmul(o, W[0], X[1], start=False, stop=False)
                            i = pe.matmul(o, W[1], X[0], start=False, stop=(k == KT - 1))
                    i.then_inc(pe_unit, 1)

            for f in range(2):
                feat_tile(2 * f, 4 * f)
            with pe.Fori(1, 12) as i:
                for f in range(2):
                    pe.wait_ge(feat_evac, i * 2 + (f - 1))
                    feat_tile(2 * f, i * 8 + 4 * f)
            pe.wait_ge(feat_evac, 24)

            def token_unit(u, k, first, last_):
                pe.wait_ge(lo_done, u + 1)
                for t, (t0, n) in enumerate(TILES):
                    o = ps[0:n, t, :]
                    X = [hT_hi[:, k, t0:t0 + n], hT_lo[:, k, t0:t0 + n]]
                    W = [w_hi[:, u % 2, :], w_lo[:, u % 2, :]]
                    if first is not None and k == 0 and first > 0:
                        pe.wait_ge(tok_evac, 5 * (first - 1) + t + 1)
                    pe.matmul(o, X[0], W[0], start=(k == 0), stop=False)
                    pe.matmul(o, X[1], W[0], start=False, stop=False)
                    i = pe.matmul(o, X[0], W[1], start=False, stop=last_)
                i.then_inc(pe_unit, 1)

            for c in range(5):
                for k in range(KT):
                    token_unit(U_KV + KT * c + k, k, c, k == KT - 1)
            pe.wait_ge(lo_done, U_GD + 2)
            for k in range(KT):
                s, kk = (U_GD + k // 8) % 2, k % 8
                W = [w_hi[:, s, 64 * kk:64 * kk + 64], w_lo[:, s, 64 * kk:64 * kk + 64]]
                for h in range(2):
                    o, H = ps[0:64, 5 + h, 0:HALF], slice(HALF * h, HALF * h + HALF)
                    pe.matmul(o, W[0], hT_hi[:, k, H], start=(k == 0), stop=False)
                    pe.matmul(o, W[0], hT_lo[:, k, H], start=False, stop=False)
                    i = pe.matmul(o, W[1], hT_hi[:, k, H], start=False, stop=(k == KT - 1))
            i.then_inc(pe_unit, 2)
            pe.wait_ge(gT_ready, 1)
            for t, (t0, n) in enumerate(TILES):
                i = pe.transpose(ps[0:n, 7, 64 * t:64 * t + 64], gT[:, t0:t0 + n], ident[0:64, 0:64])
            i.then_inc(gT_done, 1)
            join(pe, 1)
            for G in range(3 * NTT):
                t, b = G // 3, G % 3
                t0, n = TILES[t]
                if G >= 6:
                    pe.wait_ge(tokT_evac, G - 5)
                for k in range(4):
                    i = pe.transpose(ps[0:n, G % 6, 128 * k:128 * k + 128], xbcT[:, 4 * b + k, t0:t0 + n], ident)
                i.then_inc(tokT_ready, 1)
            pe.wait_ge(a_ready, 1)
            for t, (t0, n) in enumerate(TILES):
                tri = con[0:n, C_TRI:C_TRI + n] if t < 4 else con[0:n, C_TRIS:C_TRIS + n]
                one = con[0:n, C_ONE:C_ONE + n] if t < 4 else con[0:n, C_BLK:C_BLK + n]
                pe.matmul(ps[0:n, 7, 32 * t:32 * t + 16], tri, a_[0:n, t, :], start=True, stop=True)
                i = pe.matmul(ps[0:n, 7, 32 * t + 16:32 * t + 32], one, a_[0:n, t, :], start=True, stop=True)
            i.then_inc(sums_ready, 1)
            pe.wait_ge(tokT_evac, 15)

            def state_transposes(p):
                pe.wait_ge(slot_loaded[p % 4], X_LOADS + 16 * (p // 4 + 1))
                for s in range(NB):
                    i = pe.transpose(ps[:, s // 4, 128 * (s % 4):128 * (s % 4) + 128], h0r[:, p % 4, s, :], ident)
                i.then_inc(h0T_ready, 1)

            state_transposes(0)
            for p in range(8):
                g = p // 2
                pe.wait_ge(h0T_evac, p + 1)
                if p:
                    pe.wait_ge(dec_ready, p)
                for s in range(NB):
                    pe.matmul(ps[:, 2, 8 * s:8 * s + 8], h0T[:, s, :], xbcT[:, 12 + g, NP + 8 * s:NP + 8 * s + 8], start=True, stop=True)
                for h in range(2):
                    i = pe.matmul(ps[64 * h:64 * h + 64, 3, 0:8], a_[0:64, 4, 2 * p + h:2 * p + h + 1].broadcast_to([64, 64]),
                                  con[0:64, C_SEQ:C_SEQ + 8], start=True, stop=True)
                i.then_inc(yo_ready, 1)
                if p < 7:
                    state_transposes(p + 1)
                pe.wait_ge(yoT_evac, p + 1)
                if p:
                    pe.wait_ge(yoff_evac, p)
                pe.transpose(ps[0:64, 6, 0:128], yoT[:], ident).then_inc(yoff_ready, 1)
                pe.wait_ge(bexp_ready, g + 1)
                pe.wait_ge(xt_ready, 1)
                if p:
                    pe.wait_ge(new_ready, p)
                for hf in range(2):
                    i = pe.matmul(ps[:, 4 + hf, :], xte[0:64, 0, 128 * p:128 * p + 128],
                                  bex[:, 4 * hf:4 * hf + 4, :].rearrange("j s n -> j (s n)"), start=True, stop=True)
                i.then_inc(newps_ready, 1)
            pe.wait_ge(new_ready, 8)
            pe.wait_ge(yoff_evac, 8)

            def ssd_scores(w):
                t, g = w // 4, w % 4
                t0, n = TILES[t]
                tri = con[0:n, C_TRI:C_TRI + n] if t < 4 else con[0:n, C_TRIS:C_TRIS + n]
                if w >= 2:
                    pe.wait_ge(M_done, w - 1)
                pe.matmul(ps[0:n, w % 2, 0:n], xbcT[:, 8 + g, t0:t0 + n], xbcT[:, 12 + g, t0:t0 + n], start=True, stop=True)
                for h in range(4):
                    i = pe.matmul(ps[0:n, 2 + w % 2, 128 * h:128 * h + n], a_[0:n, t, 4 * g + h:4 * g + h + 1].broadcast_to([n, n]), tri, start=True, stop=True)
                i.then_inc(s1_ready, 1)

            def ssd_out(w):
                t, g = w // 4, w % 4
                t0, n = TILES[t]
                sl = (t + 1) % 2
                pe.wait_ge(M_done, w + 1)
                pe.wait_ge(xt_ready, t + 2)
                if w:
                    pe.wait_ge(unit_done, w)
                for h in range(4):
                    i = pe.matmul(ps[0:n, 4, 64 * h:64 * h + 64], seg[0:n, w % 2, h, 0:n],
                                  xdt[0:n, sl, 256 * g + 64 * h:256 * g + 64 * h + 64], start=True, stop=True)
                if 1 <= t <= 3:
                    i = pe.matmul(ps[0:n, 5, 0:256], xbcT[:, 12 + g, t0:t0 + n], hst[:, 256 * g:256 * g + 256], start=True, stop=True)
                if t <= 3:
                    i = pe.matmul(ps[:, 6, 0:256], Bk[0:n, t, 128 * g:128 * g + 128], xte[0:n, sl, 256 * g:256 * g + 256], start=True, stop=True)
                i.then_inc(y_ready, 1)

            ssd_scores(0)
            for w in range(20):
                if w + 1 < 20:
                    ssd_scores(w + 1)
                ssd_out(w)
            pe.wait_ge(unit_done, 20)
            for k in range(XT):
                pe.transpose(ps[0:27, k // 4, 128 * (k % 4):128 * (k % 4) + 128], cst[:, k, :], ident)
            for k in range(8):
                i = pe.transpose(ps[:, 4 + k // 4, 128 * (k % 4):128 * (k % 4) + 128], hst[:, 128 * k:128 * k + 128], ident)
            i.then_inc(fin_T, 1)
            join(pe, 2)
            pe.wait_ge(ld_c, 16 * 10)
            pe.wait_ge(tab_set, 1)
            pe.matmul(ps[0:NH, 0, :], tab, oh[:, 0:512], start=True, stop=True)
            pe.matmul(ps[0:NH, 1, 0:BL - 512], tab, oh[:, 512:BL], start=True, stop=True).then_inc(prep_mm, 1)
            pe.transpose(ps[:, 2, 0:32], pes, ident[0:32, 0:32]).then_inc(prep_mm, 1)
            pe.wait_ge(peT_ready, 1)
            for a in range(2):
                for k in range(16):
                    i = pe.matmul(ps[:, 7, a:a + 1], w1p[:, a, k, :], peT[:, 16 * a + k:16 * a + k + 1], start=(k == 0), stop=(k == 15))
            i.then_inc(prep_mm, 1)
            pe.wait_ge(rb_ready, 1)
            e = 0
            for c, (s0, ns) in enumerate(CH):
                for s in range(ns):
                    pe.wait_ge(slot_loaded[(s0 + s) % 4], H0_LOADS + 128 * ((s0 + s) // 4 + 1))
                    for b in range(4):
                        if e >= 2:
                            pe.wait_ge(pairT_evac, e - 1)
                        for g in range(4):
                            i = pe.transpose(ps[:, e % 2, 128 * g:128 * g + 128],
                                             craw[:, (s0 + s) % 4, b // 2, b % 2, g].rearrange("i q d -> i (q d)"), ident)
                        i.then_inc(pairT_ready, 1)
                        e += 1
                pe.wait_ge(pairT_evac, e)
                for a in range(2):
                    if c:
                        pe.wait_ge(gelu_done, 2 * c)
                    for k in range(16):
                        i = pe.matmul(ps[:, 2 + a, 0:124 * ns], w1p[:, a, k, :],
                                      kvp[:, a, 0:ns, :, k:k + 241:8].rearrange("p s g n -> p (s g) n"), start=(k == 0), stop=(k == 15))
                    i.then_inc(hid_ready, 1)
                pe.wait_ge(gelu_done, 2 * c + 1)
                if c:
                    pe.wait_ge(kc_evac, c)
                for hf in range(2):
                    i = pe.matmul(ps[64 * hf:64 * hf + 64, 4, 0:62 * ns], w2t[:, 0, :],
                                  gact[:, 0:124 * ns].rearrange("p (s g q n) -> p (s g) q n", s=ns, g=2, q=2)[:, :, hf, :], start=True, stop=True)
                i.then_inc(kc_ready, 1)
                pe.wait_ge(gelu_done, 2 * c + 2)
                if c:
                    pe.wait_ge(vc_evac, c)
                for x in range(4 * ns):
                    i = pe.matmul(ps[0:NCMP, 5 + x // 8, 64 * (x % 8):64 * (x % 8) + 64], gact[:, NCMP * x:NCMP * x + NCMP], w2t[:, 1, :], start=True, stop=True)
                i.then_inc(vc_ready, 1)
            join(pe, 3)
            for br in range(2):
                for gp in range(2):
                    col = 512 * (br + 1) + 128 * gp
                    i = pe.transpose(ps[:, 0, 64 * (2 * br + gp):64 * (2 * br + gp) + 64], kvt[0:64, 4, col:col + 128], ident[0:64, 0:64])
            i.then_inc(first_mm, 1)
            pe.wait_ge(qs_ready, 1)
            for s in range(NB):
                for g in range(NG):
                    q = 64 * (g % 2)
                    i = pe.matmul(ps[32 * g:32 * g + 32, 3, NCMP * s:NCMP * s + NCMP], qs[q:q + 64, g // 2, s, :], kcT[q:q + 64, s, g // 2, :],
                                  start=True, stop=True)
            i.then_inc(first_mm, 1)
            pe.wait_ge(kn_ready, 1)
            pe.wait_ge(pc_ready, 1)
            for s in range(NB):
                i = pe.transpose(ps[0:NCMP, s // 4, 128 * (s % 4):128 * (s % 4) + 128], scc[:, s, :], ident)
            i.then_inc(first_mm, 1)
            pe.wait_ge(pcg_ready, 1)
            for s in range(NB):
                i = pe.transpose(ps[0:NCMP, 4 + s // 4, 128 * (s % 4):128 * (s % 4) + 128], scg[:, s, :], ident)
            i.then_inc(first_mm, 1)
            pe.wait_ge(pcT_evac, 1)
            for s in range(NB):
                i = pe.matmul(ps[:, 2, 9 * s:9 * s + 9], pc0[:, s, :], con[0:NCMP, C_OV:C_OV + 9], start=True, stop=True)
            i.then_inc(first_mm, 1)
            pe.wait_ge(imp_ready, 1)
            pe.matmul(ps[:, 3, 0:72], con[:, C_SAME:C_SAME + 128], imp.rearrange("p s b -> p (s b)"), start=True, stop=True).then_inc(first_mm, 1)
            pe.wait_ge(pcT_evac, 2)

            def s_kt(y):
                pe.wait_ge(a_loaded[y % 5], 64 * (y // 5 + 1))
                for gp in range(2):
                    if y:
                        pe.wait_ge(KT_evac, 2 * y - 1 + gp)
                    for k in range(4):
                        i = pe.transpose(ps[:, 4 + gp, 128 * k:128 * k + 128], araw[:, y % 5, k, 128 * gp:128 * gp + 128], ident)
                    i.then_inc(KT_mm, 1)

            def s_scores(y):
                s, br = y // 2, y % 2
                pe.wait_ge(KT_evac, 2 * y + 2)
                if y >= 2:
                    pe.wait_ge(s_max, y - 1)
                else:
                    pe.wait_ge(drop_ready, 1)
                for g in range(NG):
                    q = 64 * (g % 2)
                    pe.matmul(ps[32 * g:32 * g + 32, 2 * (y % 2), :], qs[q:q + 64, g // 2, s, :], KTs[q:q + 64, y % 2, g // 2, :], start=True, stop=True)
                if y:
                    pe.wait_ge(s_max, y)
                for g in range(NG):
                    q = 64 * (g % 2)
                    i = pe.matmul(ps[32 * g:32 * g + 32, 1, 0:64], qs[q:q + 64, g // 2, s, :], knT[q:q + 64, br, g // 2, :], start=True, stop=True)
                i.then_inc(s_mm, 1)

            def s_pt(y):
                pe.wait_ge(s_p, y + 1)
                if y:
                    pe.wait_ge(pT_evac, y)
                for k in range(4):
                    pe.transpose(ps[:, 6, 128 * k:128 * k + 128], scs[:, y % 2, 128 * k:128 * k + 128], ident)
                pe.transpose(ps[0:64, 7, 0:128], scs[:, y % 2, 512:576], ident).then_inc(pT_mm, 1)

            def s_pv(y):
                s, br = y // 2, y % 2
                pe.wait_ge(pT_evac, y + 1)
                o = ps[:, 3, 0:256]
                if br == 0 and s:
                    pe.wait_ge(oT_evac, s)
                for k in range(4):
                    pe.matmul(o, pTs[:, y % 2, k, :], araw[:, y % 5, k, 256:512], start=(br == 0 and k == 0), stop=False, skip_group_check=True)
                col = 512 * (br + 1) + 256
                i = pe.matmul(o, pTs[0:64, y % 2, 4, :], kvt[0:64, 4, col:col + 256], start=False, stop=False, skip_group_check=True)
                if br:
                    i = pe.matmul(o, pcg[:, s, :], vc[:, s, :], start=False, stop=True, skip_group_check=True)
                i.then_inc(pv_mm, 1)

            s_kt(0)
            for y in range(19):
                if y < 16:
                    s_scores(y)
                if y < 15:
                    s_kt(y + 1)
                if 1 <= y < 17:
                    s_pt(y - 1)
                if y >= 4 and y % 2 == 0:
                    s = (y - 4) // 2
                    pe.wait_ge(o_ready, s + 1)
                    if s:
                        pe.wait_ge(oT_evac, s)
                    pe.transpose(ps[0:64, 3, 256:384], osb[:, s % 2, :], ident).then_inc(oT_mm, 1)
                if 2 <= y < 18:
                    s_pv(y - 2)
            join(pe, 4)
            for k in range(4):
                for t in range(4):
                    col = 512 * (k // 2 + 1) + 128 * (k % 2)
                    i = pe.transpose(ps[:, k, 128 * t:128 * t + 128], kvt[:, t, col:col + 128], ident)
                i.then_inc(kp_mm, 1)
            pe.wait_ge(kp_evac, 4)
            for h in range(NH):
                g, q = h // 4, 64 * (h // 4 % 2)
                for i in range(4):
                    ins = pe.matmul(ps[:, h // 4, 124 * (h % 4) + NCMP * i:124 * (h % 4) + NCMP * i + NCMP],
                                    qT[q:q + 64, 4 * (g // 2) + h % 4, 128 * i:128 * i + 128], kcT[q:q + 64, 8, g // 2, :], start=True, stop=True)
                if h % 4 == 3:
                    ins.then_inc(C_mm, 1)

            def p_scores(P):
                h, i = P // 4, P % 4
                g, r, n = h // 4, h % 4, 128 * (i + 1)
                q = 64 * (g % 2)
                for br in range(2):
                    w = 2 * P + br
                    if w >= 4:
                        pe.wait_ge(P_min, w - 3)
                    pe.matmul(ps[:, w % 4, 0:n], qT[q:q + 64, 4 * (g // 2) + r, 128 * i:128 * i + 128], KTp[q:q + 64, br, g // 2, 0:n],
                              start=True, stop=True).then_inc(P_mm, 1)

            def p_transposes(P):
                h, i = P // 4, P % 4
                for br in range(2):
                    w, e = 2 * P + br, turn(P, br)
                    pe.wait_ge(P_p, w + 1)
                    if e >= 2:
                        pe.wait_ge(P_Te, e - 1)
                    for k in range(i + 1):
                        ins = pe.transpose(ps[:, 4 + e % 2, 128 * k:128 * k + 128], scp[w % 4][:, 128 * k:128 * k + 128], ident)
                    ins.then_inc(P_T, 1)
                if i == 0:
                    e = turn(P, 2)
                    pe.wait_ge(P_Te, e - 1)
                    if h == 0:
                        pe.wait_ge(C_p, 4)
                    for k in range(4):
                        ins = pe.transpose(ps[0:NCMP, 4 + e % 2, 128 * k:128 * k + 128], pcp[:, h, k, :], ident)
                    ins.then_inc(P_T, 1)

            def p_values(h, k):
                g = h // 4
                q, b = 64 * (h % 2), 6 + h // 2 % 2
                if k == 0:
                    pe.wait_ge(P_Te, turn(4 * h + 3, 1) + 1)
                    if h >= 4:
                        pe.wait_ge(P_o, h - 3)
                for br in range(2):
                    col = 512 * (br + 1) + 256 + 64 * g
                    pe.matmul(ps[q:q + 64, b, 128 * k:512], kvt[:, k, col:col + 64], pT[:, h % 2, br, k, 128 * k:512],
                              start=(br == 0 and k == 0), stop=False, skip_group_check=True)
                if k == 3:
                    pe.matmul(ps[q:q + 64, b, :], vc[:, 8, 64 * g:64 * g + 64], pcT[:, h % 2, :],
                              start=False, stop=True, skip_group_check=True).then_inc(P_pv, 1)

            pe.wait_ge(C_sub, 4)
            for P in range(NPAIR + 5):
                if P < NPAIR:
                    p_scores(P)
                if P >= 5:
                    p_values((P - 5) // 4, (P - 5) % 4)
                if 1 <= P <= NPAIR:
                    p_transposes(P - 1)
            join(pe, 5)
            for e in range(2 * NTT):
                t, k4 = e // 2, e % 2
                t0, n = TILES[t]
                if e >= 8:
                    pe.wait_ge(hT_lo_done, 4 * NTT + e - 7)
                for k in range(4):
                    i = pe.transpose(ps[:, e % 8, 128 * k:128 * k + n], zs[0:n, t, 128 * (4 * k4 + k):128 * (4 * k4 + k) + 128], ident[0:n, 0:n])
                i.then_inc(xT_ready, 1)
            pe.wait_ge(hT_lo_done, 6 * NTT)
            pe.wait_ge(ms_lo, 8)
            for c in range(4):
                for k in range(KT):
                    u = U_OUT + KT * c + k
                    pe.wait_ge(lo_done, u + 1)
                    for t, (t0, n) in enumerate(TILES):
                        if k == 0 and c:
                            pe.wait_ge(tok_evac, 6 * NTT + NTT * (c - 1) + t + 1)
                        o = ps[0:n, t, :]
                        X = [hT_hi[:, k, t0:t0 + n], hT_lo[:, k, t0:t0 + n]]
                        W = [w_hi[:, u % 2, :], w_lo[:, u % 2, :]]
                        pe.matmul(o, X[0], W[0], start=(k == 0), stop=False)
                        pe.matmul(o, X[1], W[0], start=False, stop=False)
                        i = pe.matmul(o, X[0], W[1], start=False, stop=(k == KT - 1))
                    i.then_inc(pe_unit, 1)
            for g in range(4 * NTT):
                t, k4 = g // 4, g % 4
                t0, n = TILES[t]
                pe.wait_ge(x2n_ready, t + 1)
                if g >= 8:
                    pe.wait_ge(hT_lo_done, 6 * NTT + g - 7)
                for k in range(4):
                    i = pe.transpose(ps[:, g % 8, 128 * k:128 * k + n], mo[0:n, t, 128 * (4 * k4 + k):128 * (4 * k4 + k) + 128], ident[0:n, 0:n])
                i.then_inc(xT_ready, 1)
            pe.wait_ge(ld_cw, 48 + 12 * 16)
            pe.wait_ge(hT_lo_done, 6 * NTT + 16)
            for j in range(FB):
                m = 80 if j < FT - 3 * FB else 60
                i = pe.transpose(ps[:, 4 + j // 6, 80 * (j % 6):80 * (j % 6) + m], fwst[0:m, 128 * j:128 * j + 128], ident[0:m, 0:m])
            i.then_inc(fw_T, 1)
            join(pe, 6)
            with pe.Fori(0, FT) as f:
                pe.wait_ge(g_ready, f + 1)
                feat_tile(0, f * 8 + U_FFN)
                pe.wait_ge(up_done, f + 1)
                feat_tile(2, f * 8 + (U_FFN + 4))
            join(pe, 7)
            def down_unit(c, k, i):
                v = FT * c + k
                at_ = (lambda base: base) if i is None else (lambda base: i * 4 + base)
                pe.wait_ge(lo_done, at_(U_DOWN + v + 1))
                pe.wait_ge(alo_done, at_(v + 1))
                for f in range(4):
                    if k == 0 and c:
                        pe.wait_ge(y_evac, 8 * (c - 1) + 2 * f + 2)
                    W = [w[:, v % 2, 128 * f:128 * f + 128] for w in (w_hi, w_lo)]
                    for x, (wt, act_) in enumerate(((0, a_hi), (0, a_lo), (1, a_hi))):
                        for h in range(2):
                            m = pe.matmul(ps[:, 2 * f + h, 0:HALF], W[wt], act_[:, v % 2, HALF * h:HALF * h + HALF],
                                          start=(k == 0 and x == 0), stop=False, skip_group_check=True)
                m.then_inc(pe_unit, 1)

            for c in range(4):
                peeled, turns = loop_units(c)
                for k in peeled:
                    down_unit(c, k, None)
                with pe.Fori(0, turns) as i:
                    for j in range(4):
                        down_unit(c, 3 + j, i)
            join(pe, 8)
            def y_tile(t, half):
                t0, n = TILES[t]
                for k in range(KT):
                    i = pe.transpose(ps[0:n, 4 * half + k // 4, 128 * (k % 4):128 * (k % 4) + 128], yT[:, k, t0:t0 + n], ident)
                i.then_inc(xT_ready, 1)

            def fco_rows(b):
                for k in range(16 * b, min(16 * b + 16, FT)):
                    i = pe.transpose(ps[0:18, 4 * (b % 2) + k % 16 // 4, 128 * (k % 4):128 * (k % 4) + 128], fst[:, k, :], ident)
                i.then_inc(fco_T, 1)

            for t in range(4):
                if t >= 2:
                    pe.wait_ge(y_used, t - 1)
                y_tile(t, t % 2)
            pe.wait_ge(y_used, 3)
            fco_rows(0)
            pe.wait_ge(y_used, 4)
            y_tile(4, 1)
            pe.wait_ge(y_used, 5)
            fco_rows(1)
            pe.wait_ge(fco_done, 1)
            fco_rows(2)
            join(pe, 9)

_INS = ['x_prompt', 'x_sample', 'cache_kv', 'cache_win_kv', 'state_ssm_conv', 'state_ssm', 'state_ffn_conv',
        'page_table', 'rel_table', 'ln_mix_pre', 'w_in', 'cmp_pe', 'cmp_w1', 'cmp_b1', 'cmp_w2', 'cmp_b2',
        'ssm_conv_w', 'ssm_conv_b', 'ssm_dt_bias', 'ssm_a_log', 'ssm_d', 'ssm_norm_g', 'w_out', 'ln_mix_post',
        'ln_ffn_pre', 'ffn_w_gate', 'ffn_w_up', 'ffn_dw_w', 'ffn_dw_b', 'ffn_w_down', 'ln_ffn_post']
_OUTS = [('y_prompt', (1, NP, D)), ('y_sample', (NB, NT, D)), ('kv_prompt', (1, 1, NP, 4, NG, HD)),
         ('kv_sample', (1, NB, NT, 4, NG, HD)), ('win_prompt', (1, 1, NP, 2, NG, HD)),
         ('win_sample', (1, NB, PAST, 2, NG, HD)), ('ssm_conv_prompt', (1, 1, NHIST, XBC)),
         ('ssm_conv_sample', (1, NB, NHIST, XBC)), ('ssm_prompt', (1, 1, NH, HD, STATE)),
         ('ssm_sample', (1, NB, NH, HD, STATE)), ('ffn_conv_prompt', (1, 1, FHIST, FF)),
         ('ffn_conv_sample', (1, NB, FHIST, FF))]


def kernel(**inputs):
    import concourse.bacc as bacc
    from concourse.bass_utils import run_bass_kernel_spmd as run
    nc = bacc.Bacc("TRN2", target_bir_lowering=False, num_devices=1)
    host = {n: np.ascontiguousarray(inputs[n]) for n in _INS}
    host["con"], host["onehot"] = constants(), onehot()
    A = {n: nc.dram_tensor(f"in_{n}", a.shape, mybir.dt.from_np(a.dtype), kind="ExternalInput").ap()
         for n, a in host.items()}
    O = {n: nc.dram_tensor(f"out_{n}", s, F32, kind="ExternalOutput").ap() for n, s in _OUTS}
    build(nc, A, O)
    r = run(nc, [{f"in_{n}": a for n, a in host.items()}], core_ids=[0])
    return tuple(r.results[0][f"out_{n}"] for n, _ in _OUTS)
```
